# Optimizing a Trainium2 kernel written in Bass

```python
import math
import jax, jax.numpy as jnp
from jax import lax
import numpy as np

D_MODEL = 1024
BATCH = 1
SEQ = 256
DEPTH = 1

HEAD_DIM = 64
N_DIFF_HEADS = D_MODEL // 256
DIFF_WIDTH = N_DIFF_HEADS * 2 * HEAD_DIM
N_NAT_HEADS = D_MODEL // 128
NAT_WIDTH = N_NAT_HEADS * HEAD_DIM
MIX_WIDTH = DIFF_WIDTH + NAT_WIDTH
GRID_W = 64
NAT_KH_MAX = 8
NAT_KW = 16
Q_BLOCK = 128
N_EXPERTS = 32
TOP_K = 4
D_FF_EXPERT = D_MODEL
SWIGLU_LIMIT = 7.0
SWIGLU_ALPHA = 1.702
MOE_BLOCK = 128
RMS_EPS = 1e-6


def rms_norm(x, g):
    xf = x.astype(jnp.float32)
    y = xf * lax.rsqrt(jnp.mean(xf * xf, axis=-1, keepdims=True) + RMS_EPS)
    return (y * g.astype(jnp.float32)).astype(x.dtype)

def alibi_slopes(n_heads):
    i = jnp.arange(1, n_heads + 1, dtype=jnp.float32)
    return jnp.exp2(-8.0 * i / n_heads)

def diff_attention(q, k, v, lam, lam_init, g_sub):
    B, L, H, _, Dh = q.shape
    nb = L // Q_BLOCK
    slopes = alibi_slopes(H)
    kpos = jnp.arange(L, dtype=jnp.float32)
    scale = Dh ** -0.5
    qb = q.reshape(B, nb, Q_BLOCK, H, 2, Dh).transpose(1, 0, 2, 3, 4, 5)

    def block(args):
        q_blk, i = args
        s = jnp.einsum('bqhmd,bkhmd->bhmqk', q_blk, k).astype(jnp.float32) * scale
        qpos = (i * Q_BLOCK + jnp.arange(Q_BLOCK)).astype(jnp.float32)
        dist = jnp.abs(qpos[:, None] - kpos[None, :])
        s = s - slopes[None, :, None, None, None] * dist[None, None, None]
        p = jax.nn.softmax(s, axis=-1)
        a = p[:, :, 0] - lam * p[:, :, 1]
        return jnp.einsum('bhqk,bkhe->bqhe', a.astype(v.dtype), v)

    o = lax.map(block, (qb, jnp.arange(nb)))
    o = o.transpose(1, 0, 2, 3, 4).reshape(B, L, H, 2 * Dh)
    o = rms_norm(o, g_sub) * (1.0 - lam_init)
    return o.reshape(B, L, H * 2 * Dh)

def neighbourhood_attention(q, k, v, rpb):
    B, L, H, Dh = q.shape
    rows = L // GRID_W
    kh = min(NAT_KH_MAX, rows)
    scale = Dh ** -0.5
    qg = q.reshape(B, rows, GRID_W, H, Dh)
    kg = k.reshape(B, rows, GRID_W, H, Dh)
    vg = v.reshape(B, rows, GRID_W, H, Dh)
    r = jnp.arange(rows)
    row_start = jnp.clip(r - kh // 2, 0, rows - kh)
    row_idx = row_start[:, None] + jnp.arange(kh)[None, :]
    k_rows = kg[:, row_idx]
    v_rows = vg[:, row_idx]
    c = jnp.arange(GRID_W)
    col_start = jnp.clip(c - NAT_KW // 2, 0, GRID_W - NAT_KW)
    col_in = (c[None, :] >= col_start[:, None]) & (c[None, :] < col_start[:, None] + NAT_KW)
    dr = row_idx - r[:, None] + (NAT_KH_MAX - 1)
    dc = jnp.clip(c[None, :] - c[:, None], -(NAT_KW - 1), NAT_KW - 1) + (NAT_KW - 1)
    bias = rpb.astype(jnp.float32)[:, dr[:, None, :, None], dc[None, :, None, :]]
    s = jnp.einsum('brqhd,brkwhd->bhrqkw', qg, k_rows).astype(jnp.float32) * scale + bias[None]
    s = jnp.where(col_in[:, None, :], s, -jnp.inf)
    p = jax.nn.softmax(s.reshape(B, H, rows, GRID_W, kh * GRID_W), axis=-1)
    p = p.reshape(B, H, rows, GRID_W, kh, GRID_W).astype(v.dtype)
    o = jnp.einsum('bhrqkw,brkwhd->brqhd', p, v_rows)
    return o.reshape(B, L, H * Dh)

def swiglu_clamped(hh):
    x_glu = jnp.minimum(hh[..., ::2], SWIGLU_LIMIT)
    x_lin = jnp.clip(hh[..., 1::2], -SWIGLU_LIMIT, SWIGLU_LIMIT)
    return x_glu * jax.nn.sigmoid(SWIGLU_ALPHA * x_glu) * (x_lin + 1.0)

def moe_ffn(h, w_router, b_router, w1, b1, w2, b2):
    B, L, D = h.shape
    T = B * L
    hf = h.reshape(T, D)
    logits = (hf @ w_router + b_router).astype(jnp.float32)
    top_val, top_idx = lax.top_k(logits, TOP_K)
    gates = jax.nn.softmax(top_val, axis=-1)
    n_assign = T * TOP_K
    flat_e = top_idx.reshape(-1).astype(jnp.int32)
    flat_tok = jnp.arange(n_assign, dtype=jnp.int32) // TOP_K
    order = jnp.argsort(flat_e, stable=True)
    sorted_e = flat_e[order]
    counts = jnp.bincount(flat_e, length=N_EXPERTS).astype(jnp.int32)
    padded = (counts + MOE_BLOCK - 1) // MOE_BLOCK * MOE_BLOCK
    pad_end = jnp.cumsum(padded)
    pad_start = pad_end - padded
    grp_start = jnp.cumsum(counts) - counts
    rank = jnp.arange(n_assign, dtype=jnp.int32) - grp_start[sorted_e]
    dest_sorted = (pad_start[sorted_e] + rank).astype(jnp.int32)
    cap = (n_assign + N_EXPERTS * (MOE_BLOCK - 1) + MOE_BLOCK - 1) // MOE_BLOCK * MOE_BLOCK
    n_blocks = cap // MOE_BLOCK
    tok_buf = jnp.zeros((cap,), jnp.int32).at[dest_sorted].set(flat_tok[order])
    blk_start = jnp.arange(n_blocks, dtype=jnp.int32) * MOE_BLOCK
    blk_expert = jnp.minimum(jnp.searchsorted(pad_end, blk_start, side='right'), N_EXPERTS - 1)
    x_buf = hf[tok_buf].reshape(n_blocks, MOE_BLOCK, D)

    def expert_block(args):
        xb, e = args
        hh = xb @ w1[e] + b1[e]
        return swiglu_clamped(hh) @ w2[e] + b2[e]

    y_buf = lax.map(expert_block, (x_buf, blk_expert)).reshape(cap, D)
    dest = jnp.zeros((n_assign,), jnp.int32).at[order].set(dest_sorted)
    y = y_buf[dest].reshape(T, TOP_K, D)
    out = jnp.einsum('tk,tkd->td', gates.astype(y.dtype), y)
    return out.reshape(B, L, D)

def first_inputs(seed: int = 0) -> dict:
    key = jax.random.key(seed)
    ks = jax.random.split(key, 24)
    f32 = jnp.float32
    D, F = D_MODEL, D_FF_EXPERT
    n = lambda k, shape, s: jax.random.normal(k, shape, f32) * s
    return {
        "x": n(ks[0], (BATCH, SEQ, D), 1.0),
        "c": n(ks[1], (BATCH, D), 1.0),
        "w_ada": n(ks[2], (DEPTH, D, 6 * D), 0.5 * D ** -0.5),
        "b_ada": n(ks[3], (DEPTH, 6 * D), 0.02),
        "g_pre_mix": 1.0 + n(ks[4], (DEPTH, D), 0.02),
        "g_post_mix": 1.0 + n(ks[5], (DEPTH, D), 0.02),
        "w_in": n(ks[6], (DEPTH, D, 3 * MIX_WIDTH), D ** -0.5),
        "w_out": n(ks[7], (DEPTH, MIX_WIDTH, D), MIX_WIDTH ** -0.5),
        "lam_q1": n(ks[8], (DEPTH, HEAD_DIM), 0.1),
        "lam_k1": n(ks[9], (DEPTH, HEAD_DIM), 0.1),
        "lam_q2": n(ks[10], (DEPTH, HEAD_DIM), 0.1),
        "lam_k2": n(ks[11], (DEPTH, HEAD_DIM), 0.1),
        "g_subln": 1.0 + n(ks[12], (DEPTH, 2 * HEAD_DIM), 0.02),
        "nat_rpb": n(ks[13], (DEPTH, N_NAT_HEADS, 2 * NAT_KH_MAX - 1, 2 * NAT_KW - 1), 0.02),
        "g_pre_ffn": 1.0 + n(ks[14], (DEPTH, D), 0.02),
        "g_post_ffn": 1.0 + n(ks[15], (DEPTH, D), 0.02),
        "w_router": n(ks[16], (DEPTH, D, N_EXPERTS), D ** -0.5),
        "b_router": n(ks[17], (DEPTH, N_EXPERTS), 0.01),
        "w1": n(ks[18], (DEPTH, N_EXPERTS, D, 2 * F), D ** -0.5),
        "b1": n(ks[19], (DEPTH, N_EXPERTS, 2 * F), 0.01),
        "w2": n(ks[20], (DEPTH, N_EXPERTS, F, D), F ** -0.5),
        "b2": n(ks[21], (DEPTH, N_EXPERTS, D), 0.01),
    }

def first_block(x, c, w_ada, b_ada, g_pre_mix, g_post_mix, w_in, w_out,
              lam_q1, lam_k1, lam_q2, lam_k2, g_subln, nat_rpb,
              g_pre_ffn, g_post_ffn, w_router, b_router, w1, b1, w2, b2):
    B, L, D = x.shape
    splits = [DIFF_WIDTH, 2 * DIFF_WIDTH, 3 * DIFF_WIDTH,
              3 * DIFF_WIDTH + NAT_WIDTH, 3 * DIFF_WIDTH + 2 * NAT_WIDTH]
    for l in range(DEPTH):
        lam_init = 0.8 - 0.6 * math.exp(-0.3 * l)
        mod = jax.nn.silu(c) @ w_ada[l] + b_ada[l]
        sh1, sc1, gt1, sh2, sc2, gt2 = jnp.split(mod[:, None, :], 6, axis=-1)

        h = rms_norm(x, g_pre_mix[l]) * (1.0 + sc1) + sh1
        proj = h @ w_in[l]
        dq, dk, dv, nq, nk, nv = jnp.split(proj, splits, axis=-1)
        dq = dq.reshape(B, L, N_DIFF_HEADS, 2, HEAD_DIM)
        dk = dk.reshape(B, L, N_DIFF_HEADS, 2, HEAD_DIM)
        dv = dv.reshape(B, L, N_DIFF_HEADS, 2 * HEAD_DIM)
        lam = (jnp.exp(jnp.sum(lam_q1[l].astype(jnp.float32) * lam_k1[l].astype(jnp.float32)))
               - jnp.exp(jnp.sum(lam_q2[l].astype(jnp.float32) * lam_k2[l].astype(jnp.float32)))
               + lam_init)
        o_diff = diff_attention(dq, dk, dv, lam, lam_init, g_subln[l])
        o_nat = neighbourhood_attention(nq.reshape(B, L, N_NAT_HEADS, HEAD_DIM),
                                        nk.reshape(B, L, N_NAT_HEADS, HEAD_DIM),
                                        nv.reshape(B, L, N_NAT_HEADS, HEAD_DIM),
                                        nat_rpb[l])
        mix = jnp.concatenate([o_diff, o_nat], axis=-1) @ w_out[l]
        x = x + gt1 * rms_norm(mix, g_post_mix[l])

        h2 = rms_norm(x, g_pre_ffn[l]) * (1.0 + sc2) + sh2
        f = moe_ffn(h2, w_router[l], b_router[l], w1[l], b1[l], w2[l], b2[l])
        x = x + gt2 * rms_norm(f, g_post_ffn[l])
    return x


DEPTH_2 = 2

RET_HEADS = 4
RET_DK = 128
RET_DV = 128
RET_CHUNK = 128
ROPE_BASE = 10000.0
NSA_HEADS = 8
NSA_KV_GROUPS = 2
NSA_HPG = NSA_HEADS // NSA_KV_GROUPS
NSA_HD = 64
CMP_BLOCK = 32
CMP_STRIDE = 16
SLC_BLOCK = 64
N_SELECT = 8
FORCED_LOCAL = 2
FORCE_BONUS = 1.0e4
WINDOW = 512
HGRN_HEADS = 8
HGRN_DK = D_MODEL // HGRN_HEADS
HGRN_DV = D_MODEL // HGRN_HEADS
HGRN_CHUNK = 64
D_FF = -(-8 * D_MODEL // (3 * 256)) * 256
EPS = 1e-6

EVEN_SIZES = ([RET_HEADS * RET_DK] * 2 + [RET_HEADS * RET_DV] * 2 + [NSA_HEADS * NSA_HD]
              + [NSA_KV_GROUPS * NSA_HD] * 6 + [3 * NSA_HEADS])
EVEN_IN = sum(EVEN_SIZES)
EVEN_MIX = RET_HEADS * RET_DV + NSA_HEADS * NSA_HD
ODD_SIZES = [HGRN_HEADS * HGRN_DK] * 2 + [HGRN_HEADS * HGRN_DV] * 2
ODD_IN = sum(ODD_SIZES)
ODD_MIX = HGRN_HEADS * HGRN_DV
N_EVEN = (DEPTH_2 + 1) // 2
N_ODD = DEPTH_2 // 2


def _split(a, sizes):
    return jnp.split(a, list(np.cumsum(sizes)[:-1]), axis=-1)

def rmsnorm(x, g):
    xf = x.astype(jnp.float32)
    y = xf * lax.rsqrt(jnp.mean(xf * xf, axis=-1, keepdims=True) + EPS)
    return (y * g.astype(jnp.float32)).astype(x.dtype)

def rotary(x):
    S, d = x.shape[-2], x.shape[-1]
    half = d // 2
    inv = ROPE_BASE ** (-jnp.arange(half, dtype=jnp.float32) / half)
    ang = jnp.arange(S, dtype=jnp.float32)[:, None] * inv[None, :]
    cos, sin = jnp.cos(ang), jnp.sin(ang)
    x1, x2 = x[..., :half], x[..., half:]
    return jnp.concatenate([x1 * cos - x2 * sin, x1 * sin + x2 * cos], axis=-1)

def masked_softmax(s, mask):
    s = jnp.where(mask, s, -jnp.inf)
    m = jnp.max(s, axis=-1, keepdims=True)
    m = jnp.where(jnp.isfinite(m), m, 0.0)
    p = jnp.exp(s - m)
    return p / jnp.maximum(jnp.sum(p, axis=-1, keepdims=True), 1e-30)

def retention_chunkwise(q, k, v):
    B, H, S, dk = q.shape
    dv = v.shape[-1]
    C = min(RET_CHUNK, S)
    NC = S // C
    log_gamma = jnp.log(1.0 - 2.0 ** (-5.0 - jnp.arange(H, dtype=jnp.float32)))
    q = q.reshape(B, H, NC, C, dk)
    k = k.reshape(B, H, NC, C, dk)
    v = v.reshape(B, H, NC, C, dv)
    idx = jnp.arange(C, dtype=jnp.float32)
    diff = idx[:, None] - idx[None, :]
    causal = diff >= 0
    dmat = jnp.where(causal, jnp.exp(log_gamma[:, None, None] * jnp.where(causal, diff, 0.0)), 0.0)
    scores = jnp.einsum('bhncd,bhnsd->bhncs', q, k) * dmat[None, :, None]
    o_inner = jnp.einsum('bhncs,bhnse->bhnce', scores, v)
    k_dec = k * jnp.exp(log_gamma[:, None] * (C - 1 - idx)[None, :])[None, :, None, :, None]
    chunk_kv = jnp.einsum('bhncd,bhnce->nbhde', k_dec, v)
    gamma_c = jnp.exp(log_gamma * C)[None, :, None, None]

    def step(state, kv):
        return gamma_c * state + kv, state

    _, r_prev = lax.scan(step, jnp.zeros((B, H, dk, dv), jnp.float32), chunk_kv)
    q_dec = q * jnp.exp(log_gamma[:, None] * (idx + 1.0)[None, :])[None, :, None, :, None]
    o_cross = jnp.einsum('bhncd,nbhde->bhnce', q_dec, r_prev)
    return (o_inner + o_cross).reshape(B, H, S, dv)

def nsa_compress(kv, pos_emb, w1, w2):
    B, G, S, d = kv.shape
    r = CMP_BLOCK // CMP_STRIDE
    parts = kv.reshape(B, G, S // CMP_STRIDE, CMP_STRIDE, d)
    n = S // CMP_STRIDE - r + 1
    blocks = jnp.concatenate([parts[:, :, j:j + n] for j in range(r)], axis=3)
    flat = (blocks + pos_emb.astype(jnp.float32)).reshape(B, G, n, CMP_BLOCK * d)
    return jax.nn.gelu(flat @ w1.astype(jnp.float32)) @ w2.astype(jnp.float32)

def nsa_attention(q, k_cmp, v_cmp, k_slc, v_slc, k_win, v_win, gates):
    B, G, HPG, S, d = q.shape
    scale = d ** -0.5
    n_cmp = k_cmp.shape[2]
    n_slc = S // SLC_BLOCK
    n_sel = min(N_SELECT, n_slc)
    cs = np.arange(n_cmp) * CMP_STRIDE
    ce = cs + CMP_BLOCK - 1
    ss = np.arange(n_slc) * SLC_BLOCK
    se = ss + SLC_BLOCK - 1
    overlap = jnp.asarray(((cs[:, None] <= se[None, :]) & (ce[:, None] >= ss[None, :])).astype(np.float32))
    cmp_end = jnp.asarray(ce.astype(np.int32))
    ks_blocks = k_slc.reshape(B, G, n_slc, SLC_BLOCK, d)
    vs_blocks = v_slc.reshape(B, G, n_slc, SLC_BLOCK, d)
    kw_pad = jnp.pad(k_win, ((0, 0), (0, 0), (WINDOW, 0), (0, 0)))
    vw_pad = jnp.pad(v_win, ((0, 0), (0, 0), (WINDOW, 0), (0, 0)))
    bi = jnp.arange(B)[:, None, None, None]
    gi = jnp.arange(G)[None, :, None, None]
    jblk = jnp.arange(n_slc)
    offs = jnp.arange(SLC_BLOCK)

    def block(i):
        q0 = i * Q_BLOCK
        t = q0 + jnp.arange(Q_BLOCK)
        qb = lax.dynamic_slice_in_dim(q, q0, Q_BLOCK, axis=3)
        s_c = jnp.einsum('bghqd,bgnd->bghqn', qb, k_cmp) * scale
        p_c = masked_softmax(s_c, cmp_end[None, :] <= t[:, None])
        o_c = jnp.einsum('bghqn,bgnd->bghqd', p_c, v_cmp)
        imp = jnp.einsum('bgqn,nj->bgqj', jnp.sum(p_c, axis=2), overlap)
        bt = (t // SLC_BLOCK)[:, None]
        valid_s = jblk[None, :] <= bt
        forced = (jblk[None, :] == 0) | ((bt - jblk[None, :] >= 0) & (bt - jblk[None, :] < FORCED_LOCAL))
        score = jnp.where(valid_s, imp + jnp.where(forced, FORCE_BONUS, 0.0), -1e30)
        _, idx = lax.top_k(score, n_sel)
        kg = ks_blocks[bi, gi, idx].reshape(B, G, Q_BLOCK, n_sel * SLC_BLOCK, d)
        vg = vs_blocks[bi, gi, idx].reshape(B, G, Q_BLOCK, n_sel * SLC_BLOCK, d)
        kpos = (idx[..., None] * SLC_BLOCK + offs).reshape(B, G, Q_BLOCK, n_sel * SLC_BLOCK)
        s_s = jnp.einsum('bghqd,bgqkd->bghqk', qb, kg) * scale
        p_s = masked_softmax(s_s, (kpos <= t[None, None, :, None])[:, :, None])
        o_s = jnp.einsum('bghqk,bgqkd->bghqd', p_s, vg)
        kw = lax.dynamic_slice_in_dim(kw_pad, q0, WINDOW + Q_BLOCK, axis=2)
        vw = lax.dynamic_slice_in_dim(vw_pad, q0, WINDOW + Q_BLOCK, axis=2)
        spos = q0 - WINDOW + jnp.arange(WINDOW + Q_BLOCK)
        dist = t[:, None] - spos[None, :]
        valid_w = (dist >= 0) & (dist < WINDOW) & (spos[None, :] >= 0)
        s_w = jnp.einsum('bghqd,bgkd->bghqk', qb, kw) * scale
        o_w = jnp.einsum('bghqk,bgkd->bghqd', masked_softmax(s_w, valid_w), vw)
        gb = lax.dynamic_slice_in_dim(gates, q0, Q_BLOCK, axis=4)[..., None]
        return gb[0] * o_c + gb[1] * o_s + gb[2] * o_w

    out = lax.map(block, jnp.arange(S // Q_BLOCK))
    return jnp.transpose(out, (1, 2, 3, 0, 4, 5)).reshape(B, G * HPG, S, d)

def retention_nsa_mixer(h, w_in, w_out, pos_k, w1_k, w2_k, pos_v, w1_v, w2_v):
    B, S, _ = h.shape
    proj = (h @ w_in).astype(jnp.float32)
    (rq, rk, rv, rg, nq, kc, vc, ks, vs, kw, vw, ng) = _split(proj, EVEN_SIZES)
    heads = lambda a, n: jnp.transpose(a.reshape(B, S, n, -1), (0, 2, 1, 3))
    q_r = rotary(heads(rq, RET_HEADS))
    k_r = rotary(heads(rk, RET_HEADS)) * RET_DK ** -0.5
    o_r = retention_chunkwise(q_r, k_r, heads(rv, RET_HEADS))
    mu = jnp.mean(o_r, axis=-1, keepdims=True)
    var = jnp.mean(jnp.square(o_r - mu), axis=-1, keepdims=True)
    o_r = (o_r - mu) * lax.rsqrt(var + 1e-5)
    o_r = jnp.transpose(o_r, (0, 2, 1, 3)).reshape(B, S, RET_HEADS * RET_DV) * jax.nn.silu(rg)
    q_n = jnp.transpose(nq.reshape(B, S, NSA_KV_GROUPS, NSA_HPG, NSA_HD), (0, 2, 3, 1, 4))
    kvh = lambda a: jnp.transpose(a.reshape(B, S, NSA_KV_GROUPS, NSA_HD), (0, 2, 1, 3))
    k_cmp = nsa_compress(kvh(kc), pos_k, w1_k, w2_k)
    v_cmp = nsa_compress(kvh(vc), pos_v, w1_v, w2_v)
    gates = jnp.transpose(jax.nn.sigmoid(ng).reshape(B, S, 3, NSA_KV_GROUPS, NSA_HPG), (2, 0, 3, 4, 1))
    o_n = nsa_attention(q_n, k_cmp, v_cmp, kvh(ks), kvh(vs), kvh(kw), kvh(vw), gates)
    o_n = jnp.transpose(o_n, (0, 2, 1, 3)).reshape(B, S, NSA_HEADS * NSA_HD)
    mixed = jnp.concatenate([o_r, o_n], axis=-1).astype(h.dtype)
    return mixed @ w_out

def hgrn2_chunkwise(q, k, v, log_f):
    B, H, S, dk = q.shape
    dv = v.shape[-1]
    C = min(HGRN_CHUNK, S)
    NC = S // C
    to_chunks = lambda a: jnp.moveaxis(a.reshape(B, H, NC, C, a.shape[-1]), 2, 0)
    causal = jnp.tril(jnp.ones((C, C), dtype=bool))[:, :, None]

    def step(state, xs):
        qc, kc, vc, gc = xs
        b = jnp.cumsum(gc, axis=2)
        diff = b[:, :, :, None, :] - b[:, :, None, :, :]
        decay = jnp.exp(jnp.where(causal, diff, -jnp.inf))
        attn = jnp.sum(qc[:, :, :, None, :] * decay * kc[:, :, None, :, :], axis=-1)
        o = (jnp.einsum('bhnm,bhme->bhne', attn, vc)
             + jnp.einsum('bhnd,bhde->bhne', qc * jnp.exp(b), state))
        b_last = b[:, :, -1:, :]
        new_state = (jnp.exp(b_last[:, :, 0, :])[..., None] * state
                     + jnp.einsum('bhmd,bhme->bhde', kc * jnp.exp(b_last - b), vc))
        return new_state, o

    _, o = lax.scan(step, jnp.zeros((B, H, dk, dv), jnp.float32),
                    (to_chunks(q), to_chunks(k), to_chunks(v), to_chunks(log_f)))
    return jnp.moveaxis(o, 0, 2).reshape(B, H, S, dv)

def hgrn2_mixer(h, w_in, w_out, norm_g, lb):
    B, S, _ = h.shape
    proj = (h @ w_in).astype(jnp.float32)
    qp, fp, ip, gp = _split(proj, ODD_SIZES)
    heads = lambda a: jnp.transpose(a.reshape(B, S, HGRN_HEADS, -1), (0, 2, 1, 3))
    lb = jnp.maximum(lb, 0.0)
    log_f = jnp.logaddexp(jnp.log(lb), jnp.log1p(-lb) + jax.nn.log_sigmoid(fp))
    k = (1.0 - lb) * jax.nn.sigmoid(-fp)
    q = jax.nn.silu(qp) * HGRN_DK ** -0.5
    o = hgrn2_chunkwise(heads(q), heads(k), heads(ip), heads(log_f))
    o = o * lax.rsqrt(jnp.mean(o * o, axis=-1, keepdims=True) + EPS) * norm_g.astype(jnp.float32)
    o = jnp.transpose(o, (0, 2, 1, 3)).reshape(B, S, ODD_MIX) * jax.nn.sigmoid(gp)
    return o.astype(h.dtype) @ w_out

def swiglu(h, w1, w3, w2):
    return (jax.nn.silu(h @ w1) * (h @ w3)) @ w2

def second_inputs(seed: int = 0) -> dict:
    key = jax.random.key(seed)
    ks = jax.random.split(key, 20)
    nrm = lambda k, shape, s: jax.random.normal(k, shape, jnp.float32) * s
    return {
        "x": nrm(ks[0], (BATCH, SEQ, D_MODEL), 1.0),
        "norm_mix_g": 1.0 + nrm(ks[1], (DEPTH_2, D_MODEL), 0.05),
        "norm_ffn_g": 1.0 + nrm(ks[2], (DEPTH_2, D_MODEL), 0.05),
        "final_norm_g": 1.0 + nrm(ks[3], (D_MODEL,), 0.05),
        "even_w_in": nrm(ks[4], (N_EVEN, D_MODEL, EVEN_IN), D_MODEL ** -0.5),
        "even_w_out": nrm(ks[5], (N_EVEN, EVEN_MIX, D_MODEL), EVEN_MIX ** -0.5),
        "cmp_pos_k": nrm(ks[6], (N_EVEN, CMP_BLOCK, NSA_HD), 0.1),
        "cmp_w1_k": nrm(ks[7], (N_EVEN, CMP_BLOCK * NSA_HD, NSA_HD), (CMP_BLOCK * NSA_HD) ** -0.5),
        "cmp_w2_k": nrm(ks[8], (N_EVEN, NSA_HD, NSA_HD), NSA_HD ** -0.5),
        "cmp_pos_v": nrm(ks[9], (N_EVEN, CMP_BLOCK, NSA_HD), 0.1),
        "cmp_w1_v": nrm(ks[10], (N_EVEN, CMP_BLOCK * NSA_HD, NSA_HD), (CMP_BLOCK * NSA_HD) ** -0.5),
        "cmp_w2_v": nrm(ks[11], (N_EVEN, NSA_HD, NSA_HD), NSA_HD ** -0.5),
        "odd_w_in": nrm(ks[12], (N_ODD, D_MODEL, ODD_IN), D_MODEL ** -0.5),
        "odd_w_out": nrm(ks[13], (N_ODD, ODD_MIX, D_MODEL), ODD_MIX ** -0.5),
        "hgrn_norm_g": 1.0 + nrm(ks[14], (N_ODD, HGRN_DV), 0.05),
        "hgrn_lb_logits": nrm(ks[15], (N_ODD, HGRN_HEADS * HGRN_DK), 1.0),
        "ffn_w1": nrm(ks[16], (DEPTH_2, D_MODEL, D_FF), D_MODEL ** -0.5),
        "ffn_w3": nrm(ks[17], (DEPTH_2, D_MODEL, D_FF), D_MODEL ** -0.5),
        "ffn_w2": nrm(ks[18], (DEPTH_2, D_FF, D_MODEL), D_FF ** -0.5),
    }

def second_block(x, norm_mix_g, norm_ffn_g, final_norm_g, even_w_in, even_w_out,
              cmp_pos_k, cmp_w1_k, cmp_w2_k, cmp_pos_v, cmp_w1_v, cmp_w2_v,
              odd_w_in, odd_w_out, hgrn_norm_g, hgrn_lb_logits,
              ffn_w1, ffn_w3, ffn_w2):
    lb_sm = jax.nn.softmax(hgrn_lb_logits.astype(jnp.float32), axis=0)
    lb_all = jnp.cumsum(lb_sm, axis=0) - lb_sm[0:1]
    for layer in range(DEPTH_2):
        h = rmsnorm(x, norm_mix_g[layer])
        j = layer // 2
        if layer % 2 == 0:
            mix = retention_nsa_mixer(h, even_w_in[j], even_w_out[j],
                                      cmp_pos_k[j], cmp_w1_k[j], cmp_w2_k[j],
                                      cmp_pos_v[j], cmp_w1_v[j], cmp_w2_v[j])
        else:
            mix = hgrn2_mixer(h, odd_w_in[j], odd_w_out[j], hgrn_norm_g[j], lb_all[j])
        x = x + mix.astype(x.dtype)
        h = rmsnorm(x, norm_ffn_g[layer])
        x = x + swiglu(h, ffn_w1[layer], ffn_w3[layer], ffn_w2[layer]).astype(x.dtype)
    return rmsnorm(x, final_norm_g)


def setup_inputs(seed=0):
    out = dict(first_inputs(seed))
    for name, value in second_inputs(seed + 1).items():
        if name != "x":
            out[name + "_2"] = value
    return out


def reference(
    x, c, w_ada, b_ada, g_pre_mix, g_post_mix, w_in, w_out, lam_q1, lam_k1, lam_q2, lam_k2,
    g_subln, nat_rpb, g_pre_ffn, g_post_ffn, w_router, b_router, w1, b1, w2, b2, norm_mix_g_2,
    norm_ffn_g_2, final_norm_g_2, even_w_in_2, even_w_out_2, cmp_pos_k_2, cmp_w1_k_2,
    cmp_w2_k_2, cmp_pos_v_2, cmp_w1_v_2, cmp_w2_v_2, odd_w_in_2, odd_w_out_2, hgrn_norm_g_2,
    hgrn_lb_logits_2, ffn_w1_2, ffn_w3_2, ffn_w2_2,
):
    x = first_block(
        x, c, w_ada, b_ada, g_pre_mix, g_post_mix, w_in, w_out, lam_q1, lam_k1, lam_q2, lam_k2,
        g_subln, nat_rpb, g_pre_ffn, g_post_ffn, w_router, b_router, w1, b1, w2, b2,
    )
    return second_block(
        x, norm_mix_g_2, norm_ffn_g_2, final_norm_g_2, even_w_in_2, even_w_out_2, cmp_pos_k_2,
        cmp_w1_k_2, cmp_w2_k_2, cmp_pos_v_2, cmp_w1_v_2, cmp_w2_v_2, odd_w_in_2, odd_w_out_2,
        hgrn_norm_g_2, hgrn_lb_logits_2, ffn_w1_2, ffn_w3_2, ffn_w2_2,
    )


_drawn_inputs = setup_inputs


def setup_inputs(seed=0):
    import zlib

    import numpy as np

    out = dict(_drawn_inputs(seed))
    spreads = {}
    factors = {'g_pre_mix': 3.09,
     'lam_k1': 3.615,
     'lam_q2': 3.624,
     'nat_rpb': 4.28,
     'g_post_ffn': 51.435,
     'b_router': 2.79,
     'b1': 8.0,
     'b2': 8.0,
     'cmp_pos_k_2': 200.0,
     'cmp_pos_v_2': 17.677,
     'hgrn_norm_g_2': 12.876,
     'cmp_w2_k_2': 8.395,
     'norm_mix_g_2': 3.394,
     'norm_ffn_g_2': 5.52,
     'cmp_w1_k_2': 2.951}
    for name, (base, spread) in spreads.items():
        noise = np.random.default_rng([zlib.crc32(name.encode()), seed]).standard_normal(out[name].shape)
        drawn = base * np.exp(spread * noise) if base else spread * noise
        out[name] = __import__('jax').numpy.asarray(drawn.astype(out[name].dtype))
    for name, factor in factors.items():
        out[name] = (out[name] * factor).astype(out[name].dtype)
    return out
```

```python
from collections import namedtuple
from contextlib import ExitStack

import numpy as np
import concourse.bass as bass
from concourse import mybir

F32 = mybir.dt.float32
I32 = mybir.dt.int32
U32 = mybir.dt.uint32
ALU = mybir.AluOpType
ACT = mybir.ActivationFunctionType
AX = mybir.AxisListType

P = 128
D = 1024
T = 256
KT = D // P
TT = T // P
EPS = 1e-6
NEG = -1e30

DIFF_HEADS = 4
UNITS = 8
GRID_W = 64
GRID_ROWS = T // GRID_W
NAT_KH, NAT_KW = 8, 16
LAM_INIT = 0.2
ATT_SCALE = 64 ** -0.5

E_N = 32
TOP_K = 4
SLOTS = 96
PASSES = -(-T // SLOTS)
LIMIT = 7.0
ALPHA = 1.702
BIG = 3.0e38

RET_HEADS = 4
NSA_HEADS = 8
CMP_BLOCK, CMP_STRIDE = 32, 16
N_CMP = T // CMP_STRIDE - 1
HG_HEADS = 8
LEVELS = 7
D_FF = 2816
FFN_STEPS = D_FF // 256

RING = 12
CHUNK = 2048
N_ADA_A, N_WIN, N_ADA_B, N_WOUT = 8, 12, 16, 4
PER_EXPERT = 12
C_ADA_A = 0
C_WIN = C_ADA_A + N_ADA_A
C_ADA_B = C_WIN + N_WIN
C_WOUT = C_ADA_B + N_ADA_B
C_MOE = C_WOUT + N_WOUT
C_EIN = C_MOE + PER_EXPERT * E_N
C_EOUT = C_EIN + 14
C_FFN0 = C_EOUT + 4
C_OIN = C_FFN0 + 3 * FFN_STEPS
C_OOUT = C_OIN + 16
C_FFN1 = C_OOUT + 4

EARLY = {}
LATE = {}


def _columns(table, sizes):
    at = 0
    for name, n in sizes:
        table[name] = (at, at + n)
        at += n
    return at


N_EARLY = _columns(EARLY, [("ident", P), ("ones", P), ("before", P), ("flip", P), ("slot", SLOTS), ("eps", 2),
                           ("window", GRID_W), ("alibi", DIFF_HEADS * TT * T)])
N_LATE = _columns(LATE, [("decay", RET_HEADS * 384), ("cos", T), ("sin", T), ("swap", P), ("causal", 384),
                         ("cmp_add", TT * N_CMP), ("cmp_keep", TT * N_CMP), ("levels", (LEVELS + 1) * P)])


def shape_constants():
    p = np.arange(P)
    early = np.zeros((P, N_EARLY), np.float32)

    def put(array, table, name, values):
        a, b = table[name]
        array[:, a:b] = np.asarray(values).reshape(P, b - a)

    put(early, EARLY, "ident", np.eye(P))
    put(early, EARLY, "ones", np.ones((P, P)))
    put(early, EARLY, "before", p[:, None] < p[None, :])
    put(early, EARLY, "flip", p[:, None] == (p // GRID_W * GRID_W + GRID_W - 1 - p % GRID_W)[None, :])
    put(early, EARLY, "slot", np.tile(np.arange(SLOTS), (P, 1)))
    put(early, EARLY, "eps", np.tile(np.array([EPS, 1e-5]), (P, 1)))
    c, kc = (p % GRID_W)[:, None], np.arange(GRID_W)[None, :]
    first = np.clip(c - NAT_KW // 2, 0, GRID_W - NAT_KW)
    put(early, EARLY, "window", np.where((kc >= first) & (kc < first + NAT_KW), 0.0, NEG))
    q = np.arange(TT)[None, :, None] * P + p[:, None, None]
    dist = np.abs(q - np.arange(T)[None, None, :])
    slopes = 2.0 ** (-8.0 * np.arange(1, DIFF_HEADS + 1) / DIFF_HEADS)
    put(early, EARLY, "alibi", -slopes[None, :, None, None] * dist[:, None])

    late = np.zeros((P, N_LATE), np.float32)
    s = p[:, None]
    t = np.concatenate([np.arange(T), np.arange(P)])[None, :]
    gap = t - s
    log_gamma = np.log(1.0 - 2.0 ** (-5.0 - np.arange(RET_HEADS)))
    decay = np.where(gap[:, None, :] >= 0, np.exp(log_gamma[None, :, None] * np.maximum(gap, 0)[:, None, :]), 0.0)
    put(late, LATE, "decay", decay * P ** -0.5)
    half = P // 2
    inv = np.float32(10000.0) ** (-np.arange(half, dtype=np.float32) / np.float32(half))
    ang = np.arange(T, dtype=np.float32)[None, :] * inv[p % half][:, None]
    put(late, LATE, "cos", np.cos(ang))
    put(late, LATE, "sin", np.sin(ang) * np.where(p < half, -1.0, 1.0)[:, None])
    put(late, LATE, "swap", (p[:, None] + half) % P == p[None, :])
    tri = np.where(p[None, :] <= p[:, None], 0.0, NEG)
    put(late, LATE, "causal", np.concatenate([tri, 0 * tri, tri], axis=1))
    end = np.arange(N_CMP) * CMP_STRIDE + CMP_BLOCK - 1
    keep = end[None, None, :] <= (np.arange(TT)[None, :, None] * P + p[:, None, None])
    put(late, LATE, "cmp_add", np.where(keep, 0.0, NEG))
    put(late, LATE, "cmp_keep", keep)
    m, n = p[:, None], p[None, :]
    levels = [(m // (2 * h) == n // (2 * h)) & (m % (2 * h) < h) & (n % (2 * h) >= h)
              for h in (2 ** i for i in range(LEVELS))] + [m == n]
    put(late, LATE, "levels", np.stack(levels, axis=1))
    return early, late


NAMES = """ada_saved ada_turned alibi_loaded b1_loaded vec_loaded x_loaded early_loaded bias_loaded lam_loaded moe_loaded late_loaded cmp_loaded
vec_turned vec_saved c_ready x_turned x_ready mod_ready lam_dots lam_spread lam_exp lam_ready bias_flipped bias_ready
sq_ready ssq_ready root_ready h_ready chunk_done proj_saved
scores_ready neg_max probs_ready attn_ready attn_turned attn_saved heads_out mix_saved
sub_sq sub_ssq sub_root mix_ready act_step dve_step pool_step
logits_ready top_ready e_ready masks_ready ranks_ready gates_ready gates_turned gates_saved tok_turned tok_saved
b1_turned b1_saved count_ready f_seeded
masks_built gathered xg_saved st_saved glu_ready lin_ready sig_ready act_ready y_saved pass_over
f_saved again_step
swapped rot_ready ret_scores ret_weighted ret_out ret_saved ret_sum ret_centred ret_sq ret_ssq ret_root
cmp_x cmp_hidden cmp_act cmp_out cmp_saved gate_ready cmp_scores cmp_shift cmp_exp cmp_probs cmp_turned cmp_turn_saved
nsa_scores nsa_max nsa_probs nsa_weighted nsa_turned nsa_saved nsa_out
hg_level hg_scores hg_placed hg_cross hg_out hg_saved hg_sq hg_ssq hg_root
ffn_silu ffn_hidden ffn_out y_turned y_out_saved out_stored""".split()
PASS_NAMES = """chunk_done masks_built gathered xg_saved st_saved glu_ready lin_ready sig_ready
act_ready y_saved pass_over""".split()


class Chain:

    def __init__(self, eng, sem):
        self.eng, self.sem, self.n, self.turn = eng, sem, 0, None

    def value(self):
        return self.n if self.turn is None else self.turn + self.n

    def link(self, ins):
        ins.then_inc(self.sem, 1)
        self.n += 1
        self.eng.wait_ge(self.sem, self.value())


def two_layer_program(nc, x, c, w_ada, b_ada, g_pre_mix, g_post_mix, w_in, w_out, lam_q1, lam_k1, lam_q2,
                      lam_k2, g_subln, nat_rpb, g_pre_ffn, g_post_ffn, w_router, b_router, w1, b1, w2, b2,
                      norm_mix_g_2, norm_ffn_g_2, final_norm_g_2, even_w_in_2, even_w_out_2, cmp_pos_k_2,
                      cmp_w1_k_2, cmp_w2_k_2, cmp_pos_v_2, cmp_w1_v_2, cmp_w2_v_2, odd_w_in_2, odd_w_out_2,
                      hgrn_norm_g_2, hgrn_lb_logits_2, ffn_w1_2, ffn_w3_2, ffn_w2_2, early, late, out):
    with ExitStack() as ctx:
        def sbuf(name, cols, dt=F32, rows=P):
            return ctx.enter_context(nc.sbuf_tensor(name, [rows, cols], dt))

        S = namedtuple("Semaphores", NAMES)(*[ctx.enter_context(nc.semaphore(n)) for n in NAMES])
        landed = [ctx.enter_context(nc.semaphore(f"landed{i}")) for i in range(RING)]
        again = namedtuple("AgainSemaphores", PASS_NAMES)(
            *[ctx.enter_context(nc.semaphore("again_" + n)) for n in PASS_NAMES])
        again_landed = [ctx.enter_context(nc.semaphore(f"again_landed{i}")) for i in range(RING)]

        ring = [sbuf(f"ring{i}", CHUNK) for i in range(RING)]
        xT = sbuf("xT", KT * T)
        hT = sbuf("hT", KT * T)
        sq = sbuf("sq", KT * T)
        mixT = sbuf("mixT", KT * T)
        small = sbuf("small", 1024)
        early_sb = sbuf("early_sb", N_EARLY)
        arena = sbuf("arena", 15900)
        count = sbuf("count", 2, I32)
        psum = ctx.enter_context(nc.psum_tensor("psum", [P, 8 * 512], F32))
        bank = [psum[:, 512 * i:512 * i + 512] for i in range(8)]

        taken = [0]

        def carve(cols):
            taken[0] += cols
            assert taken[0] <= 1024
            return small[:, taken[0] - cols:taken[0]]

        def const(name):
            return early_sb[:, EARLY[name][0]:EARLY[name][1]]

        ident, ones, before, flip, slot_id, window = (
            const(n) for n in ("ident", "ones", "before", "flip", "slot", "window"))
        eps6, eps5 = const("eps")[:, 0:1], const("eps")[:, 1:2]
        alibi = const("alibi").rearrange("p (h n) -> p h n", h=DIFF_HEADS)
        cols_a, cols_b = carve(P), carve(2)
        silu_c = carve(KT * 32).rearrange("p (k m) -> p k m", m=32)
        ada_rows = sbuf("ada_rows", 256)
        spare = carve(7)
        mod = carve(48)
        pre_scale, post_scale = carve(16), carve(16)
        rstd = sbuf("rstd", T)
        negmax, rsum, lam2 = carve(UNITS * 4), carve(UNITS * 4), carve(4)

        def tiles(a):
            return a.rearrange("p (k t) -> p k t", t=T)

        def region(at, cols):
            assert at + cols <= 15900
            return arena[:, at:at + cols]

        diff_q, diff_k = tiles(region(0, 1024)), tiles(region(1024, 1024))
        nat_q, nat_k = tiles(region(2048, 1024)), tiles(region(3072, 1024))
        diff_v = region(4096, 1024).rearrange("p (a n) -> p a n", a=TT)
        nat_v = region(5120, 1024).rearrange("p (a n) -> p a n", a=TT)
        nat_bias = region(6144, 4096).rearrange("p (h n) -> p h n", h=8)
        score_sb = [region(10240, 1024), region(11264, 1024)]
        x_tok = region(10240, 2048).rearrange("p (a n) -> p a n", a=TT)
        attn_T = region(12288, 1024)
        rows_a = region(12288, P)
        rows_b = region(12288 + P, P)
        lam_rows = region(12288 + 2 * P, 4 * 64)
        b1_rows = region(3072, 2048)[0:E_N, :]
        router_w = region(13312, KT * E_N).rearrange("p (k e) -> p k e", k=KT)
        b2_sb = region(13568, D)[0:E_N, :]
        b1_T = region(14592, 16 * E_N).rearrange("p (j e) -> p j e", e=E_N)
        router_b = region(15104, E_N)[0:1, :]
        h_tok = region(0, 2048).rearrange("p (a n) -> p a n", a=TT)
        xg = [region(2048 + 768 * i, KT * SLOTS).rearrange("p (k s) -> p k s", s=SLOTS) for i in range(2)]
        act_sb = region(3584, KT * SLOTS).rearrange("p (k s) -> p k s", s=SLOTS)
        y_sb = [region(4352 + 1024 * i, D)[0:SLOTS, :] for i in range(2)]
        st_sb = [region(6400 + 256 * i, T)[0:SLOTS, :] for i in range(2)]
        pick = [region(6912 + 192 * i, 2 * SLOTS).rearrange("p (a s) -> p a s", a=TT) for i in range(2)]
        pick_g = [region(7296 + 192 * i, 2 * SLOTS).rearrange("p (a s) -> p a s", a=TT) for i in range(2)]
        glu, lin, sig = ([region(7680 + 384 * j + 192 * i, 2 * SLOTS).rearrange("p (a s) -> p a s", a=2)
                          for i in range(2)] for j in range(3))
        pos = region(8832, TT * 98).rearrange("p (a e) -> p a e", a=TT)
        gate = region(9028, TT * 34).rearrange("p (a e) -> p a e", a=TT)
        routed = region(9096, TT * E_N).rearrange("p (a e) -> p a e", a=TT)
        logits = region(9160, TT * 36).rearrange("p (a e) -> p a e", a=TT)
        replaced = region(9232, TT * 36).rearrange("p (a e) -> p a e", a=TT)
        top8 = region(9304, TT * 8).rearrange("p (a e) -> p a e", a=TT)
        neg_top, gsum = region(9320, 2), region(9322, 2)
        gates_T = region(9324, T)[0:E_N, :]
        count_f = region(9580, 2)
        late_sb = region(9600, N_LATE)
        assert 9600 + N_LATE <= 13312 + 256

        def late_const(name):
            return late_sb[:, LATE[name][0]:LATE[name][1]]

        raw_qk = tiles(region(0, 2048))
        weighted = region(0, 1536).rearrange("p (h n) -> p h n", h=RET_HEADS)
        rot_qk = tiles(region(2048, 2048))
        cmp_T = region(2048, 2048)[0:N_CMP, :].rearrange("p (h t) -> p h t", h=NSA_HEADS)
        ret_v = region(4096, 1024).rearrange("p (a n) -> p a n", a=TT)
        ret_g = tiles(region(5120, 1024))
        nsa_q = tiles(region(6144, 1024))
        cmp_in = tiles(region(7168, 512))
        slc_k, win_k = tiles(region(7680, 512)), tiles(region(8192, 512))
        slc_v = region(8704, 256).rearrange("p (a n) -> p a n", a=TT)
        win_v = region(8960, 256).rearrange("p (a n) -> p a n", a=TT)
        nsa_gate = region(9216, 48).rearrange("p (a n) -> p a n", a=TT)
        cmp_p = region(9264, 240).rearrange("p (n c) -> p n c", c=N_CMP)
        coef = region(9504, 48)
        cmp_w1_sb = [region(13312, 2048).rearrange("p (j n) -> p j n", n=64),
                     mixT[:, :].rearrange("p (j n) -> p j n", n=64)]
        cmp_x = [hT[:, 512 * i:512 * i + 480].rearrange("p (n j) -> p n j", j=CMP_BLOCK) for i in range(2)]
        centred = hT[:, 1024:2048]
        nsa_s = [region(13312 + 768 * i, 768).rearrange("p (h n) -> p h n", h=2) for i in range(2)]
        nsa_T = [sq[:, 768 * i:768 * i + 768].rearrange("p (h n) -> p h n", h=2) for i in range(2)]
        pos_rows = [region(12288 + 512 + P * i, P)[0:CMP_BLOCK, :] for i in range(2)]
        pos_cols = carve(2 * CMP_BLOCK).rearrange("p (i j) -> p i j", i=2)
        cmp_w2_sb = carve(2 * 64).rearrange("p (i n) -> p i n", i=2)
        cmp_act = carve(2 * N_CMP).rearrange("p (i n) -> p i n", i=2)
        cmp_k = carve(2 * N_CMP).rearrange("p (g n) -> p g n", g=2)
        cmp_v = carve(2 * 64)[0:N_CMP, :].rearrange("p (g n) -> p g n", g=2)
        cmp_max, cmp_sum = carve(16), carve(16)
        nsa_negmax, nsa_sum = carve(32), carve(32)
        hg_q, hg_f, hg_k, hg_g = (tiles(region(2048 * i, 2048)) for i in range(4))
        hg_v = region(8192, 2048).rearrange("p (a n) -> p a n", a=TT)
        hg_cross = region(10240, 1024).rearrange("p (h n) -> p h n", h=HG_HEADS)
        hg_near = region(13312, 2048).rearrange("p (n c) -> p n c", c=P)
        hg_pk, hg_qd, hg_kd = tiles(hT[:, :]), tiles(sq[:, :]), tiles(mixT[:, :])
        hg_o = tiles(region(2048, 2048))
        ffn_s = [region(512 * i, 512) for i in range(2)]
        ffn_h = [region(1024 + 512 * i, 512).rearrange("p (k t) -> p k t", k=2) for i in range(2)]
        out_tok = region(2048, 2048).rearrange("p (a n) -> p a n", a=TT)

        block = ctx.enter_context(nc.Block())

        @block.sync
        def _(sp):
            def slot_free(n):
                if n >= RING:
                    sp.wait_ge(S.chunk_done, n - RING + 1)

            def column_chunks(first, w, n, cols):
                for j in range(n):
                    slot_free(first + j)
                    m = min(256, cols - 256 * j)
                    sp.dma_start(ring[(first + j) % RING][:, 0:KT * m].rearrange("p (k n) -> p k n", k=KT),
                                 w.rearrange("(k p) n -> p k n", p=P)[:, :, 256 * j:256 * j + m]) \
                      .then_inc(landed[(first + j) % RING], 16)

            column_chunks(C_ADA_A, w_ada[0][:, 0:2048], N_ADA_A, 2048)
            column_chunks(C_WIN, w_in[0], N_WIN, 3072)
            column_chunks(C_ADA_B, w_ada[0][:, 2048:6144], N_ADA_B, 4096)
            column_chunks(C_WOUT, w_out[0], N_WOUT, D)

            w1_view = w1[0].rearrange("e (k p) n -> e p k n", p=P)
            w2_view = w2[0].rearrange("e (c k p) n -> e c p k n", p=P, k=2)

            def expert_chunks(e, wait, land):
                for j in range(PER_EXPERT):
                    wait(j)
                    home = ring[(C_MOE + j) % RING]
                    if j < 8:
                        src = w1_view[bass.ds(e, 1), :, :, 256 * j:256 * j + 256]
                        src = src.rearrange("a p k n -> p (a k) n")
                        dst = home[:, :].rearrange("p (k n) -> p k n", k=KT)
                    else:
                        src = w2_view[bass.ds(e, 1), j - 8].rearrange("a p k n -> p (a k) n")
                        dst = home[:, :].rearrange("p (k n) -> p k n", k=2)
                    sp.dma_start(dst, src).then_inc(land[(C_MOE + j) % RING], 16)

            with sp.Fori(0, E_N) as e:
                expert_chunks(e, lambda j: sp.wait_ge(S.chunk_done, e * PER_EXPERT + (C_MOE + j - RING + 1)),
                              landed)
            sp.wait_ge(S.count_ready, 1)
            most = sp.value_load(count[0:1, 0:1])
            with sp.If(most > SLOTS):
                sp.wait_ge(S.pass_over, 1)
                expert_chunks(0, lambda j: None, again_landed)
                with sp.Fori(1, E_N) as e:
                    expert_chunks(e, lambda j: sp.wait_ge(again.chunk_done, e * PER_EXPERT + (j - RING + 1)),
                                  again_landed)
                for q in range(1, PASSES - 1):
                    with sp.Fori(0, E_N) as e:
                        expert_chunks(e, lambda j: sp.wait_ge(
                            again.chunk_done, e * PER_EXPERT + (E_N * PER_EXPERT * q + j - RING + 1)), again_landed)
                sp.wait_ge(again.pass_over, 1)

            column_chunks(C_EIN, even_w_in_2[0], 14, 3352)
            column_chunks(C_EOUT, even_w_out_2[0], 4, D)

            def ffn_chunks(first, layer):
                n = first
                wa, wb = (w[layer].rearrange("(k p) n -> p k n", p=P) for w in (ffn_w1_2, ffn_w3_2))
                wc = ffn_w2_2[layer].rearrange("(c k p) n -> c p k n", p=P, k=2)
                for i in range(FFN_STEPS + 1):
                    todo = []
                    if i < FFN_STEPS:
                        todo += [wa[:, :, 256 * i:256 * i + 256], wb[:, :, 256 * i:256 * i + 256]]
                    if i >= 1:
                        todo += [wc[i - 1]]
                    for src in todo:
                        slot_free(n)
                        sp.dma_start(ring[n % RING][:, :].rearrange("p (k n) -> p k n", k=src.shape[1]), src) \
                          .then_inc(landed[n % RING], 16)
                        n += 1

            ffn_chunks(C_FFN0, 0)
            column_chunks(C_OIN, odd_w_in_2[0], 16, 4096)
            column_chunks(C_OOUT, odd_w_out_2[0], 4, D)
            ffn_chunks(C_FFN1, 1)

            for a in range(TT):
                sp.wait_ge(S.y_out_saved, 2 * a + 2)
                sp.dma_start(out[0, a * P:(a + 1) * P, :], out_tok[:, a, :]).then_inc(S.out_stored, 16)
            sp.wait_ge(S.out_stored, 16 * TT)


        @block.gpsimd
        def _(pool):
            pool.dma_start(x_tok, x[0].rearrange("(a p) d -> p a d", p=P)).then_inc(S.x_loaded, 16)
            pool.dma_start(b1_rows, b1[0]).then_inc(S.b1_loaded, 16)
            for i, v in enumerate((lam_q1, lam_k1, lam_q2, lam_k2)):
                pool.dma_start(lam_rows[0:1, 64 * i:64 * i + 64], v).then_inc(S.lam_loaded, 16)
            pool.dma_start(early_sb[:, EARLY["alibi"][0]:], early[:, EARLY["alibi"][0]:]).then_inc(S.alibi_loaded, 16)
            for r in range(GRID_ROWS):
                half = 64 * (r % 2)
                for h in range(8):
                    src = bass.AP(nat_rpb.tensor, h * 465 + (NAT_KH - 1 - r) * 31 + NAT_KW - 1 - (GRID_W - 1),
                                  [[1, GRID_W], [31, GRID_ROWS], [1, GRID_W]])
                    dst = nat_bias[half:half + 64, h, (r // 2) * T:(r // 2 + 1) * T]
                    pool.dma_start(dst.rearrange("p (a n) -> p a n", a=GRID_ROWS), src).then_inc(S.bias_loaded, 16)
            pool.dma_start(router_w, w_router[0].rearrange("(k p) e -> p k e", p=P)).then_inc(S.moe_loaded, 16)
            pool.dma_start(router_b, b_router).then_inc(S.moe_loaded, 16)
            pool.dma_start(b2_sb, b2[0]).then_inc(S.moe_loaded, 16)
            for i, v in enumerate((cmp_w2_k_2, cmp_w2_v_2)):
                for g in range(2):
                    pool.dma_start(cmp_w2_sb[64 * g:64 * g + 64, i, :], v[0]).then_inc(S.moe_loaded, 16)
            pool.wait_ge(S.mix_ready, 1)
            pool.dma_start(late_sb, late).then_inc(S.late_loaded, 16)
            pool.wait_ge(S.f_saved, 1)
            for i, v in enumerate((cmp_w1_k_2, cmp_w1_v_2)):
                for g in range(2):
                    pool.dma_start(cmp_w1_sb[i][64 * g:64 * g + 64, :, :],
                                   v[0].rearrange("(j d) n -> d j n", d=64)).then_inc(S.cmp_loaded, 16)

        N_VEC = 11 + 4

        @block.tensor
        def _(pe):
            def arrived(n):
                pe.wait_ge(landed[n % RING], 16 * (n // RING + 1))

            def cols(n, m=256):
                return ring[n % RING][:, 0:KT * m].rearrange("p (k n) -> p k n", k=KT)

            def vector_columns():
                pe.wait_ge(S.early_loaded, 16)
                pe.wait_ge(S.vec_loaded, 16 * N_VEC)
                pe.wait_ge(S.b1_loaded, 16)
                nc.tensor.transpose(bank[6][:, 0:P], rows_a, ident)
                nc.tensor.transpose(bank[6][:, P:P + 2], rows_b[0:2, :], ident[0:2, 0:2])
                for i in range(2):
                    nc.tensor.transpose(bank[6][:, 256 + 32 * i:288 + 32 * i], pos_rows[i], ident[0:32, 0:32])
                rows = b1_rows.rearrange("e (j f g) -> e j f g", g=2, f=P)
                for j in range(8):
                    for g in range(2):
                        mm = nc.tensor.transpose(bank[5][:, (2 * j + g) * E_N:(2 * j + g + 1) * E_N],
                                                 rows[:, j, :, g], ident[0:E_N, 0:E_N])
                mm.then_inc(S.vec_turned, 1)

            def turn_x():
                pe.wait_ge(S.x_loaded, 16)
                for k in range(KT):
                    for a in range(TT):
                        mm = nc.tensor.transpose(bank[k // 2][:, (k % 2) * T + a * P:(k % 2) * T + (a + 1) * P],
                                                 x_tok[:, a, k * P:(k + 1) * P], ident)
                    if k % 2:
                        mm.then_inc(S.x_turned, 1)

            def lam_to_all():
                pe.wait_ge(S.lam_dots, 2)
                nc.tensor.matmul(bank[6][:, 400:402], ones[0:1, :], lam2[0:1, 0:2], start=True, stop=True) \
                  .then_inc(S.lam_spread, 1)

            def ada_columns(j):
                pe.wait_ge(S.ada_saved, j + 1)
                for h in range(2):
                    mm = nc.tensor.matmul(bank[7][:, 256 + 2 * j + h:257 + 2 * j + h], ada_rows[:, h * P:(h + 1) * P],
                                          ones[:, 0:1], start=True, stop=True)
                mm.then_inc(S.ada_turned, 1)

            def ada(j):
                if j >= 1 and j != N_ADA_A:
                    ada_columns(j - 1)
                n = C_ADA_A + j if j < N_ADA_A else C_ADA_B + j - N_ADA_A
                arrived(n)
                for k in range(KT):
                    g = k % 4
                    mm = nc.tensor.matmul(bank[7][32 * g:32 * g + 32, 0:256], silu_c[:, k, :], cols(n)[:, k, :],
                                          start=(k < 4), stop=(k >= 4))
                mm.then_inc(S.chunk_done, 1)

            def sum_squares(i):
                pe.wait_ge(S.sq_ready, i + 1)
                for k in range(KT):
                    mm = nc.tensor.matmul(bank[6][:, 0:T], ones, sq[:, k * T:(k + 1) * T],
                                          start=(k == 0), stop=(k == KT - 1))
                mm.then_inc(S.ssq_ready, 1)

            def project(n, j, src, parts, m=256):
                arrived(n)
                if j >= 2:
                    pe.wait_ge(S.proj_saved, j - 1)
                w, home, at = cols(n, m), bank[j % 2], 0
                if parts == "rows":
                    todo = [("r", a, 0, m) for a in range(TT)]
                elif parts == "columns":
                    todo = [("c", h, h * P, P) for h in range(2)]
                else:
                    todo = [("c", 0, 0, P)] + [("r", a, P, P) for a in range(TT)]
                for kind, i, c0, w_n in todo:
                    n_out = T if kind == "c" else w_n
                    for k in range(KT):
                        lhs, rhs = w[:, k, c0:c0 + w_n], src[:, k * T:(k + 1) * T]
                        if kind == "r":
                            lhs, rhs = src[:, k * T + i * P:k * T + (i + 1) * P], lhs
                        mm = nc.tensor.matmul(home[:, at:at + n_out], lhs, rhs, start=(k == 0), stop=(k == KT - 1))
                    at += n_out
                mm.then_inc(S.chunk_done, 1)

            def scores(u):
                if u >= 2:
                    pe.wait_ge(S.neg_max, u - 1)
                q, k = (diff_q, diff_k) if u < DIFF_HEADS else (nat_q, nat_k)
                i = u % DIFF_HEADS
                for m in range(2):
                    for a in range(TT):
                        mm = nc.tensor.matmul(bank[2 * (u % 2) + m][:, a * T:(a + 1) * T],
                                              q[64 * m:64 * m + 64, i, a * P:(a + 1) * P],
                                              k[64 * m:64 * m + 64, i, :], start=True, stop=True)
                mm.then_inc(S.scores_ready, 1)

            def turn_attention(u):
                pe.wait_ge(S.attn_ready, u + 1)
                if u >= 1:
                    pe.wait_ge(S.attn_saved, u)
                for m in range(1 if u < DIFF_HEADS else 2):
                    for b in range(TT):
                        for a in range(TT):
                            mm = nc.tensor.transpose(
                                bank[4 + m][:, b * T + a * P:b * T + (a + 1) * P],
                                score_sb[u % 2][:, m * 512 + a * T + b * P:m * 512 + a * T + (b + 1) * P], ident)
                mm.then_inc(S.attn_turned, 1)

            def heads(u):
                pe.wait_ge(S.attn_saved, u + 1)
                if u >= 1:
                    pe.wait_ge(S.mix_saved, u)
                home = bank[6][:, (u % 2) * T:(u % 2 + 1) * T]
                for m in range(1 if u < DIFF_HEADS else 2):
                    for b in range(TT):
                        if u < DIFF_HEADS:
                            v, dst = diff_v[:, b, u * P:(u + 1) * P], home
                        else:
                            h = 2 * (u - DIFF_HEADS) + m
                            v, dst = nat_v[:, b, h * 64:h * 64 + 64], home[64 * m:64 * m + 64, :]
                        mm = nc.tensor.matmul(dst, v, attn_T[:, m * 512 + b * T:m * 512 + (b + 1) * T],
                                              start=(b == 0), stop=(b == TT - 1))
                mm.then_inc(S.heads_out, 1)

            def ones_over(src, n, into, ready):
                for j in range(n):
                    mm = nc.tensor.matmul(bank[into + j][:, :], ones, src[:, 512 * j:512 * j + 512],
                                          start=True, stop=True)
                mm.then_inc(ready, 1)

            def flip_bias(r):
                if r == 0:
                    pe.wait_ge(S.bias_loaded, 16 * 32)
                    pe.wait_ge(S.x_ready, 1)
                    pe.wait_ge(S.vec_saved, 1)
                else:
                    pe.wait_ge(S.bias_ready, r)
                for i in range(4):
                    mm = nc.tensor.matmul(bank[2 + i], flip, nat_bias[:, 4 * r + i, :], start=True, stop=True)
                mm.then_inc(S.bias_flipped, 1)

            vector_columns()
            turn_x()
            lam_to_all()
            pe.wait_ge(S.c_ready, 1)
            for j in range(N_ADA_A):
                ada(j)
            ada_columns(N_ADA_A - 1)
            pe.wait_ge(S.lam_exp, 1)
            sum_squares(0)
            pe.wait_ge(S.h_ready, 1)
            for j in range(N_WIN):
                if j in (4, 8):
                    flip_bias(j // 4 - 1)
                project(C_WIN + j, j, hT, "rows" if j in (4, 5, 10, 11) else "columns")
            pe.wait_ge(S.proj_saved, N_WIN)
            pe.wait_ge(S.bias_ready, 2)
            for u in range(UNITS + 1):
                if u < UNITS:
                    scores(u)
                    ada(N_ADA_A + 2 * u)
                if u >= 1:
                    turn_attention(u - 1)
                    heads(u - 1)
                if u < UNITS:
                    ada(N_ADA_A + 2 * u + 1)
            ada_columns(2 * UNITS + N_ADA_A - 1)
            pe.wait_ge(S.sub_sq, 1)
            ones_over(sq, 2, 0, S.sub_ssq)
            pe.wait_ge(S.mix_ready, 1)
            for j in range(N_WOUT):
                project(C_WOUT + j, N_WIN + j, mixT, "columns")
            sum_squares(1)
            sum_squares(2)

            pe.wait_ge(S.h_ready, 2)
            pe.wait_ge(S.moe_loaded, 16 * 7)
            for a in range(TT):
                for k in range(KT):
                    nc.tensor.matmul(bank[4][:, a * E_N:(a + 1) * E_N], hT[:, k * T + a * P:k * T + (a + 1) * P],
                                     router_w[:, k, :], start=(k == 0), stop=False)
                mm = nc.tensor.matmul(bank[4][:, a * E_N:(a + 1) * E_N], ones[0:1, :], router_b, start=False, stop=True)
            mm.then_inc(S.logits_ready, 1)
            for a in range(TT):
                for k in range(KT):
                    mm = nc.tensor.transpose(bank[2 * a + k // 4][:, (k % 4) * P:(k % 4 + 1) * P],
                                             hT[:, k * T + a * P:k * T + (a + 1) * P], ident)
            mm.then_inc(S.tok_turned, 1)
            pe.wait_ge(S.masks_ready, 1)
            nc.tensor.matmul(bank[5][:, 0:E_N], before, routed[:, 0, :], start=True, stop=True)
            nc.tensor.matmul(bank[5][:, E_N:2 * E_N], ones, routed[:, 0, :], start=True, stop=False)
            nc.tensor.matmul(bank[5][:, E_N:2 * E_N], before, routed[:, 1, :], start=False, stop=True)
            nc.tensor.matmul(bank[5][:, 64:96], ones, routed[:, 0, :], start=True, stop=False)
            nc.tensor.matmul(bank[5][:, 64:96], ones, routed[:, 1, :], start=False, stop=True).then_inc(S.ranks_ready, 1)
            pe.wait_ge(S.gates_ready, 1)
            for a in range(TT):
                mm = nc.tensor.transpose(bank[6][0:E_N, a * P:(a + 1) * P], gate[:, a, 0:E_N], ident)
            mm.then_inc(S.gates_turned, 1)
            pe.wait_ge(S.gates_saved, 1)
            pe.wait_ge(S.tok_saved, 1)
            for k in range(KT):
                nc.tensor.matmul(bank[k // 2][:, (k % 2) * T:(k % 2 + 1) * T], b2_sb[:, k * P:(k + 1) * P], gates_T,
                                 start=(k % 2 == 0), stop=False, skip_group_check=True)

            def gather(M, r, value):
                pe.wait_ge(M.masks_built, value)
                for k in range(KT):
                    for a in range(TT):
                        nc.tensor.matmul(bank[6 + k // 4][:, (k % 4) * SLOTS:(k % 4 + 1) * SLOTS],
                                         h_tok[:, a, k * P:(k + 1) * P], pick[r][:, a, :],
                                         start=(a == 0), stop=(a == TT - 1))
                for a in range(TT):
                    mm = nc.tensor.transpose(bank[6 + a][0:SLOTS, 384:512], pick_g[r][:, a, :], ident)
                mm.then_inc(M.gathered, 1)

            def scatter(r, last=False):
                for k in range(KT):
                    mm = nc.tensor.matmul(bank[k // 2][:, (k % 2) * T:(k % 2 + 1) * T],
                                          y_sb[r][:, k * P:(k + 1) * P], st_sb[r], start=False, stop=last,
                                          skip_group_check=True)
                return mm

            def expert(M, e, r, land, landed_value):
                pe.wait_ge(M.xg_saved, e + 1)
                for j in range(8):
                    slot = (C_MOE + j) % RING
                    pe.wait_ge(land[slot], landed_value(j))
                    w = ring[slot][:, :].rearrange("p (k f g) -> p k f g", k=KT, g=2)
                    if j % 2 == 0:
                        pe.wait_ge(M.glu_ready, e * 4 + (j // 2 + 1))
                        pe.wait_ge(M.lin_ready, e * 4 + (j // 2 + 1))
                    home = bank[4 + (j // 2) % 2]
                    for g in range(2):
                        for k in range(KT):
                            mm = nc.tensor.matmul(home[:, (2 * (j % 2) + g) * SLOTS:(2 * (j % 2) + g + 1) * SLOTS],
                                                  w[:, k, :, g], xg[r][:, k, :], start=(k == 0), stop=(k == KT - 1))
                    mm.then_inc(M.chunk_done, 1)
                    if j == 3:
                        pe.wait_ge(M.y_saved, e + 1)
                        pe.wait_ge(M.st_saved, e + 1)
                        scatter(1 - r)
                        gather(M, 1 - r, e + 2)
                pe.wait_ge(M.xg_saved, e + 2)
                pe.wait_ge(M.st_saved, e + 2)
                for j in range(8, 12):
                    slot = (C_MOE + j) % RING
                    pe.wait_ge(land[slot], landed_value(j))
                    pe.wait_ge(M.act_ready, e * 4 + (j - 8 + 3))
                    w = ring[slot][:, :].rearrange("p (k n) -> p k n", k=2)
                    for k in range(2):
                        f = 2 * (j - 8) + k
                        for h in range(2):
                            mm = nc.tensor.matmul(bank[6 + h][0:SLOTS, :], act_sb[:, f, :], w[:, k, 512 * h:512 * h + 512],
                                                  start=(f == 0), stop=(f == 7))
                    mm.then_inc(M.chunk_done, 1)

            def all_experts(M, passes, land, turns_before):
                gather(M, 0, 1)
                for q in range(passes):
                    with pe.Fori(0, E_N // 2) as i:
                        for r in range(2):
                            base = q * E_N + r
                            expert(M, i * 2 + base, r, land,
                                   lambda j: i * 32 + 16 * (turns_before(j) + 1 + base))
                pe.wait_ge(M.y_saved, passes * E_N + 1)
                pe.wait_ge(M.st_saved, passes * E_N)
                scatter(1, last=True).then_inc(M.pass_over, 1)

            all_experts(S, 1, landed, lambda j: (C_MOE + j) // RING)
            pe.wait_ge(S.count_ready, 1)
            most = pe.value_load(count[0:1, 0:1])
            with pe.If(most > SLOTS):
                all_experts(again, PASSES - 1, again_landed, lambda j: 0)
            sum_squares(3)

            sum_squares(4)
            pe.wait_ge(S.h_ready, 3)
            kinds = ["columns"] * 4 + ["rows"] * 2 + ["columns"] * 5 + ["mixed"] * 2 + ["rows"]
            for j, kind in enumerate(kinds):
                project(C_EIN + j, 16 + j, hT, kind, 256 if j < 13 else 24)
            pe.wait_ge(S.late_loaded, 16)
            pe.wait_ge(S.cmp_loaded, 16 * 4)
            pe.wait_ge(S.cmp_x, 2)
            for i in range(2):
                for j in range(CMP_BLOCK):
                    for g in range(2):
                        half = slice(64 * g, 64 * g + 64)
                        mm = nc.tensor.matmul(bank[4 + g][half, N_CMP * i:N_CMP * (i + 1)], cmp_w1_sb[i][half, j, :],
                                              cmp_x[i][half, :, j], start=(j == 0), stop=(j == CMP_BLOCK - 1))
            mm.then_inc(S.cmp_hidden, 1)
            pe.wait_ge(S.proj_saved, 30)
            for j in range(4):
                mm = nc.tensor.matmul(bank[j][:, :], late_const("swap"), region(512 * j, 512), start=True, stop=True)
            mm.then_inc(S.swapped, 1)
            pe.wait_ge(S.cmp_act, 2)
            for g in range(2):
                half = slice(64 * g, 64 * g + 64)
                nc.tensor.matmul(bank[6 + g][half, 0:N_CMP], cmp_w2_sb[half, 0, :], cmp_act[half, 0, :], start=True, stop=True)
                mm = nc.tensor.matmul(bank[6 + g][0:N_CMP, 64:128], cmp_act[half, 1, :], cmp_w2_sb[half, 1, :],
                                      start=True, stop=True)
            mm.then_inc(S.cmp_out, 1)
            pe.wait_ge(S.rot_ready, 1)
            for h in range(RET_HEADS):
                q, k = rot_qk[:, h, :], rot_qk[:, 4 + h, :]
                nc.tensor.matmul(bank[h][:, 0:T], k[:, 0:P], q, start=True, stop=True)
                mm = nc.tensor.matmul(bank[h][:, T:384], k[:, P:T], q[:, P:T], start=True, stop=True)
            mm.then_inc(S.ret_scores, 1)
            pe.wait_ge(S.cmp_saved, 1)
            for h in range(NSA_HEADS):
                half = slice(64 * (h % 2), 64 * (h % 2) + 64)
                for a in range(TT):
                    at = ((h // 2) * TT + a) * N_CMP
                    mm = nc.tensor.matmul(bank[4 + h % 2][:, at:at + N_CMP], nsa_q[half, h // 2, a * P:(a + 1) * P],
                                          cmp_k[half, h // 4, :], start=True, stop=True)
            mm.then_inc(S.cmp_scores, 1)
            pe.wait_ge(S.ret_weighted, 1)
            for h in range(RET_HEADS):
                home, v = bank[h // 2][:, (h % 2) * T:(h % 2 + 1) * T], ret_v[:, :, h * P:(h + 1) * P]
                nc.tensor.matmul(home, v[:, 0, :], weighted[:, h, 0:T], start=True, stop=False)
                mm = nc.tensor.matmul(home[:, P:T], v[:, 1, :], weighted[:, h, T:384], start=False, stop=True)
            mm.then_inc(S.ret_out, 1)
            pe.wait_ge(S.ret_saved, 1)
            ones_over(mixT, 2, 2, S.ret_sum)
            pe.wait_ge(S.ret_sq, 1)
            ones_over(sq, 2, 0, S.ret_ssq)
            pe.wait_ge(S.cmp_probs, 1)
            pe.wait_ge(S.ret_root, 1)
            pe.wait_ge(S.ret_centred, 1)
            for h in range(NSA_HEADS):
                for a in range(TT):
                    n = (h % 2) * 8 + (h // 2) * TT + a
                    mm = nc.tensor.transpose(bank[h // 2][0:N_CMP, (h % 2) * T + a * P:(h % 2) * T + (a + 1) * P],
                                             cmp_p[:, n, :], ident)
            mm.then_inc(S.cmp_turned, 1)

            def nsa_score(u):
                i, keys = u // 2, (slc_k, win_k)[u % 2]
                if u == 0:
                    pe.wait_ge(S.cmp_turn_saved, 1)
                if u >= 2:
                    pe.wait_ge(S.nsa_max, u - 1)
                for h in range(2):
                    half, home = slice(64 * h, 64 * h + 64), bank[2 * (u % 2) + h]
                    q, k = nsa_q[half, i, :], keys[half, i // 2, :]
                    nc.tensor.matmul(home[:, 0:P], q[:, 0:P], k[:, 0:P], start=True, stop=True)
                    mm = nc.tensor.matmul(home[:, P:384], q[:, P:T], k, start=True, stop=True)
                mm.then_inc(S.nsa_scores, 1)

            def nsa_turn(u):
                pe.wait_ge(S.nsa_weighted, u + 1)
                if u >= 1:
                    pe.wait_ge(S.nsa_saved, u)
                for h in range(2):
                    for n in range(3):
                        mm = nc.tensor.transpose(bank[4 + h][:, n * P:(n + 1) * P], nsa_s[u % 2][:, h, n * P:(n + 1) * P],
                                                 ident)
                mm.then_inc(S.nsa_turned, 1)

            def nsa_heads(u):
                i, br = u // 2, u % 2
                pe.wait_ge(S.nsa_saved, u + 1)
                home = bank[6 + i % 2]
                if br == 0 and i >= 2:
                    pe.wait_ge(S.mix_saved, UNITS + i - 1)
                v = (slc_v, win_v)[br]
                for h in range(2):
                    dst, g = home[64 * h:64 * h + 64, 0:T], i // 2
                    if br == 0:
                        nc.tensor.matmul(dst, cmp_v[:, g, :], cmp_T[:, 2 * i + h, :], start=True, stop=False)
                    nc.tensor.matmul(dst, v[:, 0, 64 * g:64 * g + 64], nsa_T[u % 2][:, h, 0:T], start=False, stop=False)
                    mm = nc.tensor.matmul(dst[:, P:T], v[:, 1, 64 * g:64 * g + 64], nsa_T[u % 2][:, h, T:384],
                                          start=False, stop=(br == 1))
                mm.then_inc(S.nsa_out, 1)

            for u in range(9):
                if u < 8:
                    nsa_score(u)
                if u >= 1:
                    nsa_turn(u - 1)
                    nsa_heads(u - 1)
            pe.wait_ge(S.mix_ready, 2)
            pe.wait_ge(S.mix_saved, UNITS + 4)
            for j in range(4):
                project(C_EOUT + j, 30 + j, mixT, "columns")
            sum_squares(5)

            def ffn(first, layer):
                pe.wait_ge(S.h_ready, 4 + 2 * layer)
                n = first

                def down(i):
                    w = ring[n % RING][:, :].rearrange("p (k n) -> p k n", k=2)
                    arrived(n)
                    pe.wait_ge(S.ffn_hidden, layer * FFN_STEPS + i + 1)
                    for k in range(2):
                        for j in range(KT):
                            mm = nc.tensor.matmul(bank[j // 2][:, (j % 2) * T:(j % 2 + 1) * T], w[:, k, j * P:(j + 1) * P],
                                                  ffn_h[i % 2][:, k, :], start=(i == 0 and k == 0 and j % 2 == 0),
                                                  stop=(i == FFN_STEPS - 1 and k == 1), skip_group_check=True)
                    mm.then_inc(S.chunk_done, 1)

                for i in range(FFN_STEPS + 1):
                    if i < FFN_STEPS:
                        if i >= 2:
                            pe.wait_ge(S.ffn_hidden, layer * FFN_STEPS + i - 1)
                        for b in range(2):
                            arrived(n)
                            for h in range(2):
                                for k in range(KT):
                                    mm = nc.tensor.matmul(bank[4 + 2 * (i % 2) + b][:, h * T:(h + 1) * T],
                                                          cols(n)[:, k, h * P:(h + 1) * P], hT[:, k * T:(k + 1) * T],
                                                          start=(k == 0), stop=(k == KT - 1))
                            mm.then_inc(S.chunk_done, 1)
                            n += 1
                    if i >= 1:
                        down(i - 1)
                        n += 1

            ffn(C_FFN0, 0)
            sum_squares(6)
            pe.wait_ge(S.h_ready, 5)

            for j in range(16):
                project(C_OIN + j, 34 + j, hT, "rows" if 8 <= j < 12 else "columns")
            pe.wait_ge(S.proj_saved, 50)
            for step in range(2 * (LEVELS + 1)):
                pe.wait_ge(S.hg_level, step + 1)
                if step >= 4:
                    pe.wait_ge(S.hg_placed, step - 3)
                q, k = (hg_q, hg_k) if step < 2 else (hg_qd, hg_kd)
                for n in range(8):
                    h, a = 4 * (step % 2) + n // TT, n % TT
                    mm = nc.tensor.matmul(bank[2 * (step % 4) + n // 4][:, (n % 4) * P:(n % 4 + 1) * P],
                                          k[:, h, a * P:(a + 1) * P], q[:, h, a * P:(a + 1) * P], start=True, stop=True)
                mm.then_inc(S.hg_scores, 1)
            pe.wait_ge(S.hg_level, 2 * (LEVELS + 1) + 1)
            pe.wait_ge(S.hg_placed, 2 * (LEVELS + 1))
            for h in range(HG_HEADS):
                mm = nc.tensor.matmul(bank[h // 4][:, (h % 4) * P:(h % 4 + 1) * P], hg_kd[:, h, 0:P], hg_qd[:, h, P:T],
                                      start=True, stop=True)
            mm.then_inc(S.hg_scores, 1)
            pe.wait_ge(S.hg_placed, 2 * (LEVELS + 1) + 1)
            for h in range(HG_HEADS):
                home, v = bank[4 + h // 2][:, (h % 2) * T:(h % 2 + 1) * T], hg_v[:, :, h * P:(h + 1) * P]
                nc.tensor.matmul(home[:, 0:P], v[:, 0, :], hg_near[:, h * TT, :], start=True, stop=True)
                nc.tensor.matmul(home[:, P:T], v[:, 0, :], hg_cross[:, h, :], start=True, stop=False)
                mm = nc.tensor.matmul(home[:, P:T], v[:, 1, :], hg_near[:, h * TT + 1, :], start=False, stop=True)
            mm.then_inc(S.hg_out, 1)
            pe.wait_ge(S.hg_sq, 1)
            ones_over(sq, 4, 0, S.hg_ssq)
            pe.wait_ge(S.mix_ready, 3)
            for j in range(4):
                project(C_OOUT + j, 50 + j, mixT, "columns")
            sum_squares(7)
            ffn(C_FFN1, 1)
            sum_squares(8)
            pe.wait_ge(S.h_ready, 7)
            for a in range(TT):
                for k in range(KT):
                    mm = nc.tensor.transpose(bank[2 * a + k // 4][:, (k % 4) * P:(k % 4 + 1) * P],
                                             hT[:, k * T + a * P:k * T + (a + 1) * P], ident)
                mm.then_inc(S.y_turned, 1)

        def bcast(a, n):
            if len(a.shape) == 2:
                return a.unsqueeze(1).broadcast_to([a.shape[0], n, a.shape[1]])
            return a.broadcast_to([a.shape[0], a.shape[1], n])

        @block.scalar
        def _(act):
            def norm(i, src):
                nc.scalar.activation(sq[:, :], src[:, :], ACT.Square).then_inc(S.sq_ready, 1)
                act.wait_ge(S.ssq_ready, i + 1)
                nc.scalar.activation(rstd[:, :], bank[6][:, 0:T], ACT.Sqrt, bias=eps6, scale=1.0 / D) \
                  .then_inc(S.root_ready, 1)

            def save(j, first, n, *jobs):
                act.wait_ge(S.chunk_done, first + n + 1)
                for dst, a, b, func, scale in jobs:
                    src = bank[j % 2][:, a:b]
                    if len(dst.shape) == 3:
                        src = src.rearrange("p (k n) -> p k n", k=dst.shape[1])
                    ins = nc.scalar.activation(dst, src, func, scale=scale)
                ins.then_inc(S.proj_saved, 1)

            act.dma_start(early_sb[:, 0:EARLY["alibi"][0]], early[:, 0:EARLY["alibi"][0]]).then_inc(S.early_loaded, 16)
            at = 0
            for v in (c, b_ada, g_pre_mix, g_post_mix, g_pre_ffn, g_post_ffn, norm_mix_g_2, norm_ffn_g_2):
                n = v.shape[0] * v.shape[1] // P
                act.dma_start(rows_a[at:at + n, :], v.rearrange("a (n p) -> (a n) p", p=P)).then_inc(S.vec_loaded, 16)
                at += n
            act.dma_start(rows_a[at:at + KT, :], final_norm_g_2.rearrange("(n p) -> n p", p=P)).then_inc(S.vec_loaded, 16)
            act.dma_start(rows_b[0:1, :], g_subln).then_inc(S.vec_loaded, 16)
            act.dma_start(rows_b[1:2, :], hgrn_norm_g_2).then_inc(S.vec_loaded, 16)
            for i, v in enumerate((cmp_pos_k_2, cmp_pos_v_2)):
                for g in range(2):
                    act.dma_start(pos_rows[i][:, 64 * g:64 * g + 64], v[0]).then_inc(S.vec_loaded, 16)

            act.wait_ge(S.vec_saved, 1)
            nc.scalar.activation(silu_c[:, :, 0:1], cols_a[:, 0:KT].unsqueeze(2), ACT.Silu).then_inc(S.c_ready, 1)
            for i in range(4):
                act.wait_ge(S.x_turned, i + 1)
                ins = nc.scalar.activation(xT[:, 512 * i:512 * i + 512], bank[i], ACT.Copy)
            ins.then_inc(S.x_ready, 1)
            act.wait_ge(S.lam_spread, 1)
            nc.scalar.activation(lam2[:, 2:4], bank[6][:, 400:402], ACT.Exp).then_inc(S.lam_exp, 1)
            act.wait_ge(S.x_ready, 1)
            norm(0, xT)
            win_dst = [diff_q[:, 0:2, :], diff_q[:, 2:4, :], diff_k[:, 0:2, :], diff_k[:, 2:4, :],
                       diff_v[:, :, 0:256], diff_v[:, :, 256:512],
                       nat_q[:, 0:2, :], nat_q[:, 2:4, :], nat_k[:, 0:2, :], nat_k[:, 2:4, :],
                       nat_v[:, :, 0:256], nat_v[:, :, 256:512]]
            for j, dst in enumerate(win_dst):
                save(j, C_WIN, j, (dst, 0, 512, ACT.Copy, 1.0))
            for u in range(UNITS + 1):
                if u < UNITS:
                    act.wait_ge(S.neg_max, u + 1)
                    for n in range(4):
                        piece = score_sb[u % 2][:, n * T:(n + 1) * T]
                        nc.scalar.activation(piece, piece, ACT.Exp, bias=negmax[:, 4 * u + n:4 * u + n + 1],
                                             accum_out=rsum[:, 4 * u + n:4 * u + n + 1]).then_inc(S.probs_ready, 1)
                if u >= 1:
                    act.wait_ge(S.attn_turned, u)
                    if u >= 2:
                        act.wait_ge(S.heads_out, u - 1)
                    for m in range(1 if u - 1 < DIFF_HEADS else 2):
                        ins = nc.scalar.activation(attn_T[:, 512 * m:512 * m + 512], bank[4 + m], ACT.Copy)
                    ins.then_inc(S.attn_saved, 1)
                    act.wait_ge(S.heads_out, u)
                    nc.scalar.activation(mixT[:, (u - 1) * T:u * T], bank[6][:, ((u - 1) % 2) * T:((u - 1) % 2 + 1) * T],
                                         ACT.Copy).then_inc(S.mix_saved, 1)
            act.wait_ge(S.mix_saved, UNITS)
            nc.scalar.activation(sq[:, 0:1024], mixT[:, 0:1024], ACT.Square).then_inc(S.sub_sq, 1)
            act.wait_ge(S.sub_ssq, 1)
            nc.scalar.activation(score_sb[0], psum[:, 0:1024], ACT.Sqrt, bias=eps6, scale=1.0 / P) \
              .then_inc(S.sub_root, 1)
            for j in range(N_WOUT):
                save(N_WIN + j, C_WOUT, j, (hT[:, 512 * j:512 * j + 512], 0, 512, ACT.Copy, 1.0))
            act.wait_ge(S.proj_saved, 16)
            norm(1, hT)
            act.wait_ge(S.x_ready, 2)
            norm(2, xT)

            act.wait_ge(S.top_ready, 1)
            for a in range(TT):
                nc.scalar.activation(gate[:, a, 0:E_N], logits[:, a, 0:E_N], ACT.Exp, bias=neg_top[:, a:a + 1]) \
                  .then_inc(S.e_ready, 1)
            act.wait_ge(S.tok_turned, 1)
            for a in range(TT):
                ins = nc.scalar.activation(h_tok[:, a, :], psum[:, 1024 * a:1024 * a + 1024], ACT.Copy)
            ins.then_inc(S.tok_saved, 1)

            def save_tokens(M, r, value):
                act.wait_ge(M.gathered, value)
                for k in range(2):
                    ins = nc.scalar.activation(xg[r][:, 4 * k:4 * k + 4, :],
                                               bank[6 + k][:, 0:4 * SLOTS].rearrange("p (k s) -> p k s", s=SLOTS), ACT.Copy)
                ins.then_inc(M.xg_saved, 1)
                for a in range(TT):
                    ins = nc.scalar.activation(st_sb[r][:, a * P:(a + 1) * P], bank[6 + a][0:SLOTS, 384:512], ACT.Copy)
                ins.then_inc(M.st_saved, 1)

            def experts(M, passes, before):
                for n in range(2):
                    nc.scalar.activation(spare[:, n:n + 1], eps6, ACT.Copy).then_inc(M.lin_ready, 1)
                nc.scalar.activation(spare[:, 2:3], eps6, ACT.Copy).then_inc(M.y_saved, 1)
                save_tokens(M, 0, 1)
                for q in range(passes):
                    with act.Fori(0, E_N // 2) as i:
                        for r in range(2):
                            e, column = i * 2 + (q * E_N + r), i * 2 + r
                            for b in range(4):
                                act.wait_ge(M.glu_ready, e * 4 + (b + 3))
                                act.wait_ge(M.act_ready, e * 4 + (b + 1))
                                for j in range(2):
                                    ins = nc.scalar.activation(
                                        lin[b % 2][:, j, :], bank[4 + b % 2][:, (2 * j + 1) * SLOTS:(2 * j + 2) * SLOTS],
                                        ACT.Identity, bias=b1_T[:, 2 * (2 * b + j) + 1, bass.ds(column, 1)])
                                ins.then_inc(M.lin_ready, 1)
                                nc.scalar.activation(sig[b % 2], glu[b % 2], ACT.Sigmoid, scale=ALPHA) \
                                  .then_inc(M.sig_ready, 1)
                                if b == 1:
                                    save_tokens(M, 1 - r, e + 2)
                            act.wait_ge(M.chunk_done, e * PER_EXPERT + (before + 12))
                            nc.scalar.activation(y_sb[r], psum[0:SLOTS, 6 * 512:8 * 512], ACT.Copy).then_inc(M.y_saved, 1)

            experts(S, 1, C_MOE)
            act.wait_ge(S.count_ready, 1)
            most = act.value_load(count[0:1, 0:1])
            with act.If(most > SLOTS):
                act.wait_ge(S.pass_over, 1)
                experts(again, PASSES - 1, 0)
                act.wait_ge(again.pass_over, 1)
            act.wait_ge(S.pass_over, 1)
            nc.scalar.activation(hT[:, :], psum[:, 0:2048], ACT.Copy).then_inc(S.f_saved, 1)
            act.wait_ge(S.f_saved, 1)
            norm(3, hT)
            act.wait_ge(S.x_ready, 3)
            norm(4, xT)

            def twice(dst, lo=0):
                return [(dst[64 * half:64 * half + 64, g, :], g) for half in range(2) for g in range(2)]

            dsts = [raw_qk[:, 2 * j:2 * j + 2, :] for j in range(4)] + [ret_v[:, :, 256 * j:256 * j + 256] for j in range(2)]
            for j, dst in enumerate(dsts):
                save(16 + j, C_EIN, j, (dst, 0, 512, ACT.Copy, 1.0))
            for j in range(2):
                save(22 + j, C_EIN, 6 + j, (ret_g[:, 2 * j:2 * j + 2, :], 0, 512, ACT.Silu, 1.0))
            for j in range(2):
                save(24 + j, C_EIN, 8 + j, (nsa_q[:, 2 * j:2 * j + 2, :], 0, 512, ACT.Copy, 1.0))
            save(26, C_EIN, 10, (cmp_in, 0, 512, ACT.Copy, 1.0))
            for j, (keys, values) in enumerate(((slc_k, slc_v), (win_k, win_v))):
                home = bank[(27 + j) % 2]
                act.wait_ge(S.chunk_done, C_EIN + 11 + j + 1)
                for dst, g in twice(keys):
                    nc.scalar.activation(dst, home[64 * g:64 * g + 64, 0:T], ACT.Copy)
                nc.scalar.activation(values, home[:, T:512].rearrange("p (a n) -> p a n", a=TT), ACT.Copy) \
                  .then_inc(S.proj_saved, 1)
            save(29, C_EIN, 13, (nsa_gate, 0, 48, ACT.Sigmoid, 1.0))

            act.wait_ge(S.cmp_hidden, 1)
            for g in range(2):
                half = slice(64 * g, 64 * g + 64)
                nc.scalar.activation(cmp_act[half, :, :], bank[4 + g][half, 0:2 * N_CMP].rearrange("p (i n) -> p i n", i=2),
                                     ACT.Gelu_apprx_tanh).then_inc(S.cmp_act, 1)
            act.wait_ge(S.cmp_out, 1)
            for dst, g in twice(cmp_k):
                nc.scalar.activation(dst, bank[6 + g][64 * g:64 * g + 64, 0:N_CMP], ACT.Copy)
            for g in range(2):
                ins = nc.scalar.activation(cmp_v[:, g, :], bank[6 + g][0:N_CMP, 64:128], ACT.Copy)
            ins.then_inc(S.cmp_saved, 1)
            act.wait_ge(S.ret_out, 1)
            nc.scalar.activation(mixT[:, 0:1024], psum[:, 0:1024], ACT.Copy).then_inc(S.ret_saved, 1)
            act.wait_ge(S.cmp_shift, 1)
            nc.scalar.activation(cmp_p, cmp_p, ACT.Exp).then_inc(S.cmp_exp, 1)
            act.wait_ge(S.ret_centred, 1)
            nc.scalar.activation(sq[:, 0:1024], centred, ACT.Square).then_inc(S.ret_sq, 1)
            act.wait_ge(S.ret_ssq, 1)
            nc.scalar.activation(sq[:, 1024:2048], psum[:, 0:1024], ACT.Sqrt, bias=eps5, scale=1.0 / P) \
              .then_inc(S.ret_root, 1)
            act.wait_ge(S.cmp_turned, 1)
            nc.scalar.activation(cmp_T, psum[0:N_CMP, 0:2048].rearrange("p (h t) -> p h t", t=T), ACT.Copy) \
              .then_inc(S.cmp_turn_saved, 1)
            for u in range(9):
                if u < 8:
                    act.wait_ge(S.nsa_max, u + 1)
                    for h in range(2):
                        for a, (lo, hi) in enumerate(((0, P), (P, 384))):
                            n = 4 * u + 2 * h + a
                            piece = nsa_s[u % 2][:, h, lo:hi]
                            nc.scalar.activation(piece, piece, ACT.Exp, bias=nsa_negmax[:, n:n + 1],
                                                 accum_out=nsa_sum[:, n:n + 1]).then_inc(S.nsa_probs, 1)
                if u >= 1:
                    act.wait_ge(S.nsa_turned, u)
                    if u >= 3:
                        act.wait_ge(S.nsa_out, u - 2)
                    nc.scalar.activation(nsa_T[(u - 1) % 2], psum[:, 4 * 512:6 * 512].rearrange("p (h n) -> p h n", h=2)[:, :, 0:384],
                                         ACT.Copy).then_inc(S.nsa_saved, 1)
                    if u % 2 == 0:
                        i = u // 2 - 1
                        act.wait_ge(S.nsa_out, u)
                        nc.scalar.activation(mixT[:, (4 + i) * T:(5 + i) * T], bank[6 + i % 2][:, 0:T], ACT.Copy) \
                          .then_inc(S.mix_saved, 1)
            act.wait_ge(S.proj_saved, 34)
            norm(5, xT)

            def ffn(first, layer):
                for i in range(FFN_STEPS):
                    w1_at = first + (3 * i - 1 if i else 0)
                    act.wait_ge(S.chunk_done, w1_at + 1)
                    if i >= 2:
                        act.wait_ge(S.ffn_hidden, layer * FFN_STEPS + i - 1)
                    nc.scalar.activation(ffn_s[i % 2], bank[4 + 2 * (i % 2)], ACT.Silu).then_inc(S.ffn_silu, 1)

            ffn(C_FFN0, 0)
            act.wait_ge(S.x_ready, 4)
            norm(6, xT)

            for j in range(4):
                save(34 + j, C_OIN, j, (hg_q[:, 2 * j:2 * j + 2, :], 0, 512, ACT.Silu, 1.0))
            for j in range(4):
                save(38 + j, C_OIN, 4 + j, (hg_f[:, 2 * j:2 * j + 2, :], 0, 512, ACT.Sigmoid, 1.0),
                     (hg_k[:, 2 * j:2 * j + 2, :], 0, 512, ACT.Sigmoid, -1.0))
            for j in range(4):
                save(42 + j, C_OIN, 8 + j, (hg_v[:, :, 256 * j:256 * j + 256], 0, 512, ACT.Copy, 1.0))
            for j in range(4):
                save(46 + j, C_OIN, 12 + j, (hg_g[:, 2 * j:2 * j + 2, :], 0, 512, ACT.Sigmoid, 1.0))
            act.wait_ge(S.hg_out, 1)
            nc.scalar.activation(hg_o, psum[:, 2048:4096].rearrange("p (k t) -> p k t", t=T), ACT.Copy, scale=P ** -0.5) \
              .then_inc(S.hg_saved, 1)
            act.wait_ge(S.hg_saved, 1)
            nc.scalar.activation(tiles(sq[:, :]), hg_o, ACT.Square).then_inc(S.hg_sq, 1)
            act.wait_ge(S.hg_ssq, 1)
            nc.scalar.activation(hT[:, :], psum[:, 0:2048], ACT.Sqrt, bias=eps6, scale=1.0 / P).then_inc(S.hg_root, 1)
            act.wait_ge(S.proj_saved, 54)
            norm(7, xT)
            ffn(C_FFN1, 1)
            act.wait_ge(S.x_ready, 5)
            norm(8, xT)
            for a in range(TT):
                act.wait_ge(S.y_turned, a + 1)
                for k in range(2):
                    nc.scalar.activation(out_tok[:, a, 512 * k:512 * k + 512], bank[2 * a + k], ACT.Copy) \
                      .then_inc(S.y_out_saved, 1)

        @block.vector
        def _(dve):
            main_chain = Chain(dve, S.dve_step)
            link = main_chain.link
            V = nc.vector

            def norm(i, src):
                dve.wait_ge(S.root_ready, i + 1)
                link(V.reciprocal(rstd[:, :], rstd[:, :]))
                link(V.tensor_tensor(tiles(sq[:, :]), tiles(src[:, :]), bcast(rstd[:, :], KT), ALU.mult))

            def modulated(scale0, shift0):
                for k in range(KT):
                    ins = V.tensor_scalar(hT[:, k * T:(k + 1) * T], sq[:, k * T:(k + 1) * T],
                                          pre_scale[:, scale0 + k:scale0 + k + 1], mod[:, shift0 + k:shift0 + k + 1],
                                          ALU.mult, ALU.add)
                ins.then_inc(S.h_ready, 1)

            def gained(col):
                for k in range(KT):
                    ins = V.tensor_scalar(hT[:, k * T:(k + 1) * T], sq[:, k * T:(k + 1) * T],
                                          cols_a[:, col + k:col + k + 1], None, ALU.mult)
                ins.then_inc(S.h_ready, 1)

            def onto_x(scale0):
                for k in range(KT):
                    ins = V.scalar_tensor_tensor(out=xT[:, k * T:(k + 1) * T], in0=sq[:, k * T:(k + 1) * T],
                                                 scalar=post_scale[:, scale0 + k:scale0 + k + 1],
                                                 in1=xT[:, k * T:(k + 1) * T], op0=ALU.mult, op1=ALU.add)
                ins.then_inc(S.x_ready, 1)

            V.memset(silu_c, 0.0)
            dve.wait_ge(S.vec_turned, 1)
            V.tensor_copy(cols_a, bank[6][:, 0:P])
            V.tensor_copy(cols_b, bank[6][:, P:P + 2])
            V.tensor_copy(pos_cols, bank[6][:, 256:320].rearrange("p (i j) -> p i j", i=2))
            V.tensor_copy(b1_T, bank[5][:, :].rearrange("p (j e) -> p j e", e=E_N)).then_inc(S.vec_saved, 1)
            dve.wait_ge(S.lam_loaded, 16 * 4)
            for i in range(2):
                a = lam_rows[0:1, 128 * i:128 * i + 64]
                V.tensor_tensor_reduce(a, a, lam_rows[0:1, 128 * i + 64:128 * i + 128], 1.0, 0.0, ALU.mult, ALU.add,
                                       lam2[0:1, i:i + 1]).then_inc(S.lam_dots, 1)
            dve.wait_ge(S.vec_saved, 1)

            def save_ada(j):
                n = C_ADA_A + j if j < N_ADA_A else C_ADA_B + j - N_ADA_A
                dve.wait_ge(S.chunk_done, n + 1)
                if j >= 1:
                    dve.wait_ge(S.ada_turned, j)
                V.tensor_copy(ada_rows[:, :], bank[7][:, 0:256]).then_inc(S.ada_saved, 1)

            for j in range(N_ADA_A):
                save_ada(j)
            dve.wait_ge(S.ada_turned, N_ADA_A)
            link(V.tensor_tensor(mod[:, 0:16], bank[7][:, 256:272], cols_a[:, 8:24], ALU.add))
            link(V.scalar_tensor_tensor(out=pre_scale[:, 0:8], in0=mod[:, 8:16], scalar=1.0, in1=cols_a[:, 56:64],
                                        op0=ALU.add, op1=ALU.mult))
            norm(0, xT)
            modulated(0, 0)
            dve.wait_ge(S.lam_exp, 1)
            link(V.scalar_tensor_tensor(out=lam2[:, 0:1], in0=lam2[:, 3:4], scalar=-LAM_INIT, in1=lam2[:, 2:3],
                                        op0=ALU.add, op1=ALU.subtract))
            for r in range(2):
                dve.wait_ge(S.bias_flipped, r + 1)
                four = nat_bias[:, 4 * r:4 * r + 4, :].rearrange("p h n -> p (h n)")
                V.tensor_tensor(four.rearrange("p (m c) -> p m c", c=GRID_W),
                                psum[:, 1024:3072].rearrange("p (m c) -> p m c", c=GRID_W),
                                bcast(window, 2048 // GRID_W), ALU.add).then_inc(S.bias_ready, 1)
            dve.wait_ge(S.bias_ready, 2)

            dve.wait_ge(S.alibi_loaded, 16)
            for u in range(UNITS + 1):
                if u < UNITS:
                    i = u % DIFF_HEADS
                    dve.wait_ge(S.scores_ready, u + 1)
                    if u >= 2:
                        dve.wait_ge(S.attn_turned, u - 1)
                    for m in range(2):
                        bias = alibi[:, i, :] if u < DIFF_HEADS else nat_bias[:, 2 * i + m, :]
                        ins = V.scalar_tensor_tensor(out=score_sb[u % 2][:, 512 * m:512 * m + 512],
                                                     in0=bank[2 * (u % 2) + m], scalar=ATT_SCALE, in1=bias,
                                                     op0=ALU.mult, op1=ALU.add)
                    link(ins)
                    some = negmax[:, 4 * u:4 * u + 4]
                    link(V.tensor_reduce(some, tiles(score_sb[u % 2]), AX.X, ALU.max))
                    V.tensor_scalar(some, some, -1.0, None, ALU.mult).then_inc(S.neg_max, 1)
                    save_ada(N_ADA_A + 2 * u)
                if u >= 1:
                    v = u - 1
                    dve.wait_ge(S.probs_ready, 4 * (v + 1))
                    r = rsum[:, 4 * v:4 * v + 4]
                    link(V.reciprocal(r, r))
                    if v < DIFF_HEADS:
                        link(V.tensor_scalar(r[:, 2:4], r[:, 2:4], lam2[:, 0:1], None, ALU.mult))
                    probs = tiles(score_sb[v % 2])
                    ins = V.tensor_tensor(probs, probs, bcast(r.unsqueeze(2), T), ALU.mult)
                    if v < DIFF_HEADS:
                        link(ins)
                        s = score_sb[v % 2]
                        ins = V.tensor_tensor(s[:, 0:512], s[:, 0:512], s[:, 512:1024], ALU.add)
                    ins.then_inc(S.attn_ready, 1)
                if u < UNITS:
                    save_ada(N_ADA_A + 2 * u + 1)
            dve.wait_ge(S.ada_turned, N_ADA_A + 2 * UNITS)
            link(V.tensor_tensor(mod[:, 16:48], bank[7][:, 272:304], cols_a[:, 24:56], ALU.add))
            V.scalar_tensor_tensor(out=pre_scale[:, 8:16], in0=mod[:, 32:40], scalar=1.0, in1=cols_a[:, 72:80],
                                   op0=ALU.add, op1=ALU.mult)
            V.tensor_tensor(post_scale[:, 0:8], mod[:, 16:24], cols_a[:, 64:72], ALU.mult)
            link(V.tensor_tensor(post_scale[:, 8:16], mod[:, 40:48], cols_a[:, 80:88], ALU.mult))
            dve.wait_ge(S.sub_root, 1)
            link(V.reciprocal(score_sb[0], score_sb[0]))
            link(V.tensor_tensor(mixT[:, 0:1024], mixT[:, 0:1024], score_sb[0], ALU.mult))
            V.tensor_scalar(mixT[:, 0:1024], mixT[:, 0:1024], cols_b[:, 0:1], 1.0 - LAM_INIT, ALU.mult, ALU.mult) \
             .then_inc(S.mix_ready, 1)
            norm(1, hT)
            onto_x(0)
            norm(2, xT)
            modulated(8, 24)

            dve.wait_ge(S.logits_ready, 1)
            V.memset(logits[:, :, E_N:E_N + 4], BIG)
            link(V.tensor_copy(logits[:, :, 0:E_N], bank[4][:, 0:TT * E_N].rearrange("p (a e) -> p a e", a=TT)))
            for a in range(TT):
                ins = V.max(top8[:, a, :], logits[:, a, 0:E_N])
            link(ins)
            V.tensor_scalar(neg_top.unsqueeze(2), top8[:, :, 0:1], -1.0, None, ALU.mult).then_inc(S.top_ready, 1)
            link(V.memset(top8[:, :, TOP_K:8], BIG))
            for a in range(TT):
                ins = V.match_replace(replaced[:, a, :], top8[:, a, :], logits[:, a, :], -BIG)
            link(ins)
            V.tensor_scalar(routed, replaced[:, :, 0:E_N], -BIG, None, ALU.is_equal).then_inc(S.masks_ready, 1)
            dve.wait_ge(S.masks_ready, 1)
            dve.wait_ge(S.e_ready, TT)
            g = gate[:, :, 0:E_N]
            link(V.tensor_tensor(g, g, routed, ALU.mult))
            link(V.tensor_reduce(gsum, g, AX.X, ALU.add))
            link(V.reciprocal(gsum, gsum))
            link(V.tensor_tensor(g, g, bcast(gsum.unsqueeze(2), E_N), ALU.mult))
            V.tensor_copy(gate[:, :, E_N:E_N + 1], gate[:, :, 0:1]).then_inc(S.gates_ready, 1)
            dve.wait_ge(S.ranks_ready, 1)
            V.tensor_reduce(count_f[:, 0:1], bank[5][:, 64:96], AX.X, ALU.max)
            V.memset(pos[:, :, PASSES * E_N:PASSES * E_N + 2], -1.0)
            link(V.scalar_tensor_tensor(out=pos[:, :, 0:E_N], in0=bank[5][:, 0:64].rearrange("p (a e) -> p a e", a=TT),
                                        scalar=1.0, in1=routed, op0=ALU.add, op1=ALU.mult))
            link(V.tensor_scalar(pos[:, :, 0:E_N], pos[:, :, 0:E_N], -1.0, None, ALU.add))
            for q in range(1, PASSES):
                ins = V.tensor_scalar(pos[:, :, q * E_N:(q + 1) * E_N], pos[:, :, 0:E_N], float(-SLOTS * q), None, ALU.add)
            link(ins)
            V.tensor_copy(count[:, 0:1], count_f[:, 0:1]).then_inc(S.count_ready, 1)
            dve.wait_ge(S.gates_turned, 1)
            V.tensor_copy(gates_T, bank[6][0:E_N, 0:T]).then_inc(S.gates_saved, 1)

            def pick_tokens(M, r, place, column):
                for a in range(TT):
                    V.tensor_scalar(pick[r][:, a, :], slot_id, pos[:, a, bass.ds(place, 1)], None, ALU.is_equal)
                for a in range(TT):
                    ins = V.tensor_scalar(pick_g[r][:, a, :], slot_id, pos[:, a, bass.ds(place, 1)],
                                          gate[:, a, bass.ds(column, 1)], ALU.is_equal, ALU.mult)
                ins.then_inc(M.masks_built, 1)

            def experts(M, first_pass, passes, before, chain):
                V.memset(y_sb[1], 0.0)
                V.memset(st_sb[1], 0.0)
                for n in range(3, 5):
                    V.memset(spare[:, n:n + 1], 0.0).then_inc(M.glu_ready, 1)
                    V.memset(spare[:, n + 2:n + 3], 0.0).then_inc(M.act_ready, 1)
                pick_tokens(M, 0, first_pass * E_N, 0)
                for q in range(passes):
                    with dve.Fori(0, E_N // 2) as i:
                        start = chain.n
                        chain.turn = i * 16
                        for r in range(2):
                            e, column = i * 2 + (q * E_N + r), i * 2 + r
                            pick_tokens(M, 1 - r, i * 2 + ((first_pass + q) * E_N + r + 1), i * 2 + (r + 1))
                            for b in range(4):
                                dve.wait_ge(M.chunk_done, e * PER_EXPERT + (before + 2 * b + 2))
                                for j in range(2):
                                    ins = V.tensor_scalar(glu[b % 2][:, j, :], bank[4 + b % 2][:, 2 * j * SLOTS:(2 * j + 1) * SLOTS],
                                                          b1_T[:, 2 * (2 * b + j), bass.ds(column, 1)], LIMIT, ALU.add, ALU.min)
                                ins.then_inc(M.glu_ready, 1)
                                l = lin[b % 2]
                                dve.wait_ge(M.lin_ready, e * 4 + (b + 3))
                                chain.link(V.tensor_scalar(l, l, LIMIT, -LIMIT, ALU.min, ALU.max))
                                dve.wait_ge(M.glu_ready, e * 4 + (b + 3))
                                chain.link(V.scalar_tensor_tensor(out=l, in0=l, scalar=1.0, in1=glu[b % 2], op0=ALU.add,
                                                                  op1=ALU.mult))
                                dve.wait_ge(M.sig_ready, e * 4 + (b + 1))
                                V.tensor_tensor(act_sb[:, 2 * b:2 * b + 2, :], l, sig[b % 2], ALU.mult) \
                                 .then_inc(M.act_ready, 1)
                        assert chain.n - start == 16
                    chain.turn = None
                    chain.n += 16 * (E_N // 2 - 1)

            experts(S, 0, 1, C_MOE, main_chain)
            dve.wait_ge(S.count_ready, 1)
            most = dve.value_load(count[0:1, 0:1])
            with dve.If(most > SLOTS):
                dve.wait_ge(S.pass_over, 1)
                experts(again, 1, PASSES - 1, 0, Chain(dve, S.again_step))
                dve.wait_ge(again.pass_over, 1)
            dve.wait_ge(S.f_saved, 1)
            norm(3, hT)
            onto_x(8)
            norm(4, xT)
            gained(88)

            dve.wait_ge(S.late_loaded, 16)
            dve.wait_ge(S.proj_saved, 20)
            cos, sin = late_const("cos"), late_const("sin")
            V.tensor_tensor(rot_qk, raw_qk, bcast(cos, KT), ALU.mult)
            dve.wait_ge(S.proj_saved, 27)
            dve.wait_ge(S.chunk_done, C_EOUT)
            for i in range(2):
                tok = cmp_in[:, i, :].rearrange("p (n j) -> p n j", j=CMP_STRIDE)
                for half in range(2):
                    js = slice(CMP_STRIDE * half, CMP_STRIDE * (half + 1))
                    ins = V.tensor_tensor(cmp_x[i][:, :, js], tok[:, half:half + N_CMP, :], bcast(pos_cols[:, i, js], N_CMP),
                                          ALU.add)
                ins.then_inc(S.cmp_x, 1)
            dve.wait_ge(S.swapped, 1)
            link(V.tensor_tensor(tiles(sq[:, :]), psum[:, 0:2048].rearrange("p (k t) -> p k t", t=T), bcast(sin, KT), ALU.mult))
            V.tensor_tensor(rot_qk, rot_qk, tiles(sq[:, :]), ALU.add).then_inc(S.rot_ready, 1)
            dve.wait_ge(S.ret_scores, 1)
            V.tensor_tensor(weighted, psum[:, 0:2048].rearrange("p (h n) -> p h n", n=512)[:, :, 0:384],
                            late_const("decay").rearrange("p (h n) -> p h n", h=RET_HEADS), ALU.mult).then_inc(S.ret_weighted, 1)
            dve.wait_ge(S.cmp_scores, 1)
            for par in range(2):
                ins = V.scalar_tensor_tensor(
                    out=cmp_p[:, 8 * par:8 * par + 8, :].rearrange("p n c -> p (n c)").rearrange("p (i m) -> p i m", i=4),
                    in0=bank[4 + par][:, 0:120].rearrange("p (i m) -> p i m", i=4), scalar=ATT_SCALE,
                    in1=bcast(late_const("cmp_add"), 4), op0=ALU.mult, op1=ALU.add)
            link(ins)
            link(V.tensor_reduce(cmp_max, cmp_p, AX.X, ALU.max))
            V.tensor_tensor(cmp_p, cmp_p, bcast(cmp_max.unsqueeze(2), N_CMP), ALU.subtract).then_inc(S.cmp_shift, 1)
            dve.wait_ge(S.ret_sum, 1)
            V.scalar_tensor_tensor(out=centred, in0=psum[:, 1024:2048], scalar=-1.0 / P, in1=mixT[:, 0:1024],
                                   op0=ALU.mult, op1=ALU.add).then_inc(S.ret_centred, 1)
            dve.wait_ge(S.cmp_exp, 1)
            pairs = cmp_p.rearrange("p n c -> p (n c)").rearrange("p (i m) -> p i m", i=8)
            link(V.tensor_tensor(pairs, pairs, bcast(late_const("cmp_keep"), 8), ALU.mult))
            link(V.tensor_reduce(cmp_sum, cmp_p, AX.X, ALU.add))
            link(V.tensor_scalar(cmp_sum, cmp_sum, 1e-30, None, ALU.max))
            link(V.reciprocal(cmp_sum, cmp_sum))
            for par in range(2):
                c8 = cmp_sum[:, 8 * par:8 * par + 8].rearrange("p (i a) -> p i a", a=TT)
                ins = V.tensor_tensor(c8, c8, nsa_gate[:, :, par:8:2].rearrange("p a i -> p i a"), ALU.mult)
            link(ins)
            V.tensor_tensor(cmp_p, cmp_p, bcast(cmp_sum.unsqueeze(2), N_CMP), ALU.mult).then_inc(S.cmp_probs, 1)
            dve.wait_ge(S.ret_root, 1)
            link(V.reciprocal(sq[:, 1024:2048], sq[:, 1024:2048]))
            dve.wait_ge(S.ret_centred, 1)
            link(V.tensor_tensor(centred, centred, sq[:, 1024:2048], ALU.mult))
            V.tensor_tensor(tiles(mixT[:, 0:1024]), tiles(centred), ret_g, ALU.mult).then_inc(S.mix_ready, 1)
            for u in range(9):
                if u < 8:
                    dve.wait_ge(S.nsa_scores, u + 1)
                    if u >= 2:
                        dve.wait_ge(S.nsa_turned, u - 1)
                    s = nsa_s[u % 2]
                    link(V.scalar_tensor_tensor(
                        out=s, in0=psum[:, 1024 * (u % 2):1024 * (u % 2) + 1024].rearrange("p (h n) -> p h n", h=2)[:, :, 0:384],
                        scalar=ATT_SCALE, in1=bcast(late_const("causal"), 2), op0=ALU.mult, op1=ALU.add))
                    some = nsa_negmax[:, 4 * u:4 * u + 4]
                    for a, (lo, hi) in enumerate(((0, P), (P, 384))):
                        ins = V.tensor_reduce(some[:, a:4:2], s[:, :, lo:hi], AX.X, ALU.max)
                    link(ins)
                    V.tensor_scalar(some, some, -1.0, None, ALU.mult).then_inc(S.nsa_max, 1)
                if u >= 1:
                    v = u - 1
                    i, br = v // 2, 1 + v % 2
                    dve.wait_ge(S.nsa_probs, 4 * (v + 1))
                    r = nsa_sum[:, 4 * v:4 * v + 4]
                    link(V.reciprocal(r, r))
                    r2 = r.rearrange("p (h a) -> p h a", h=2)
                    at = 8 * br + 2 * i
                    link(V.tensor_tensor(r2, r2, nsa_gate[:, :, at:at + 2].rearrange("p a h -> p h a"), ALU.mult))
                    for a, (lo, hi) in enumerate(((0, P), (P, 384))):
                        piece = nsa_s[v % 2][:, :, lo:hi]
                        ins = V.tensor_tensor(piece, piece, bcast(r2[:, :, a:a + 1], hi - lo), ALU.mult)
                    ins.then_inc(S.nsa_weighted, 1)

            def add_projection(first, j0):
                for j in range(4):
                    dve.wait_ge(S.chunk_done, first + j + 1)
                    part = xT[:, 512 * j:512 * j + 512]
                    V.tensor_tensor(part, part, bank[(j0 + j) % 2], ALU.add).then_inc(S.proj_saved, 1)

            def ffn(first, layer):
                for i in range(FFN_STEPS):
                    w3_at = first + (3 * i if i else 1)
                    dve.wait_ge(S.chunk_done, w3_at + 1)
                    dve.wait_ge(S.ffn_silu, layer * FFN_STEPS + i + 1)
                    V.tensor_tensor(ffn_h[i % 2], ffn_s[i % 2].rearrange("p (k t) -> p k t", k=2),
                                    bank[5 + 2 * (i % 2)].rearrange("p (k t) -> p k t", k=2), ALU.mult) \
                     .then_inc(S.ffn_hidden, 1)
                dve.wait_ge(S.chunk_done, first + 3 * FFN_STEPS)
                V.tensor_tensor(xT[:, :], xT[:, :], psum[:, 0:2048], ALU.add).then_inc(S.x_ready, 1)

            add_projection(C_EOUT, 30)
            norm(5, xT)
            gained(104)
            ffn(C_FFN0, 0)
            norm(6, xT)
            gained(96)

            dve.wait_ge(S.proj_saved, 50)
            for hh in range(2):
                V.memset(hg_near[:, 8 * hh:8 * hh + 8, :], 0.0).then_inc(S.hg_level, 1)
            link(V.memset(hg_pk, 1.0))

            def place(step):
                dve.wait_ge(S.hg_scores, step + 1)
                if step >= 2:
                    dve.wait_ge(S.hg_placed, step - 1)
                lv, hh = step // 2 - 1, step % 2
                mask = late_const("levels")[:, (lv % (LEVELS + 1)) * P:(lv % (LEVELS + 1) + 1) * P]
                at = 1024 * (step % 4)
                V.copy_predicated(hg_near[:, 8 * hh:8 * hh + 8, :], bcast(mask.bitcast(U32), 8),
                                  psum[:, at:at + 1024].rearrange("p (n c) -> p n c", c=P)).then_inc(S.hg_placed, 1)

            for lv in range(LEVELS):
                half = 2 ** lv
                for hh in range(2):
                    def cut(t):
                        flat = t[:, 4 * hh:4 * hh + 4, :].rearrange("p k t -> p (k t)")
                        return flat.rearrange("p (b g s) -> p b g s", g=2, s=half)

                    q, k, f, pk, qd, kd = (cut(t) for t in (hg_q, hg_k, hg_f, hg_pk, hg_qd, hg_kd))
                    n = 512 // half
                    if lv == 0:
                        V.tensor_copy(hg_kd[:, 4 * hh:4 * hh + 4, :], hg_k[:, 4 * hh:4 * hh + 4, :])
                        V.tensor_tensor(hg_qd[:, 4 * hh:4 * hh + 4, :], hg_q[:, 4 * hh:4 * hh + 4, :],
                                        hg_f[:, 4 * hh:4 * hh + 4, :], ALU.mult).then_inc(S.hg_level, 1)
                    else:
                        dve.wait_ge(S.hg_scores, 2 * lv + hh + 1)
                        V.tensor_tensor(kd[:, :, 0, :], k[:, :, 0, :], pk[:, :, 0, :], ALU.mult)
                        V.tensor_tensor(qd[:, :, 1, :], q[:, :, 1, :], f[:, :, 1, :], ALU.mult).then_inc(S.hg_level, 1)
                    dve.wait_ge(S.hg_level, 2 * lv + hh + 3)
                    link(V.tensor_tensor(pk[:, :, 0, :], pk[:, :, 0, :], f[:, :, 1, half - 1:half].broadcast_to([P, n, half]),
                                         ALU.mult))
                    link(V.tensor_tensor(f[:, :, 1, :], f[:, :, 1, :], f[:, :, 0, half - 1:half].broadcast_to([P, n, half]),
                                         ALU.mult))
                    place(2 * lv + hh)
            for hh in range(2):
                place(2 * LEVELS + hh)
            V.tensor_tensor(hg_kd[:, :, 0:P], hg_k[:, :, 0:P], hg_pk[:, :, 0:P], ALU.mult)
            V.tensor_tensor(hg_qd[:, :, P:T], hg_q[:, :, P:T], hg_f[:, :, P:T], ALU.mult).then_inc(S.hg_level, 1)
            dve.wait_ge(S.hg_scores, 2 * (LEVELS + 1) + 1)
            V.tensor_copy(hg_cross, psum[:, 0:1024].rearrange("p (n c) -> p n c", c=P)).then_inc(S.hg_placed, 1)
            dve.wait_ge(S.hg_root, 1)
            link(V.reciprocal(hT[:, :], hT[:, :]))
            link(V.tensor_tensor(hg_o, hg_o, tiles(hT[:, :]), ALU.mult))
            V.scalar_tensor_tensor(out=tiles(mixT[:, :]), in0=hg_o, scalar=cols_b[:, 1:2], in1=hg_g, op0=ALU.mult,
                                   op1=ALU.mult).then_inc(S.mix_ready, 1)
            add_projection(C_OOUT, 50)
            norm(7, xT)
            gained(112)
            ffn(C_FFN1, 1)
            norm(8, xT)
            gained(120)


_NAMES = """x c w_ada b_ada g_pre_mix g_post_mix w_in w_out lam_q1 lam_k1 lam_q2 lam_k2 g_subln nat_rpb
g_pre_ffn g_post_ffn w_router b_router w1 b1 w2 b2 norm_mix_g_2 norm_ffn_g_2 final_norm_g_2 even_w_in_2
even_w_out_2 cmp_pos_k_2 cmp_w1_k_2 cmp_w2_k_2 cmp_pos_v_2 cmp_w1_v_2 cmp_w2_v_2 odd_w_in_2 odd_w_out_2
hgrn_norm_g_2 hgrn_lb_logits_2 ffn_w1_2 ffn_w3_2 ffn_w2_2""".split()


def kernel(**inputs):
    import concourse.bacc as _bacc
    from concourse.bass_utils import run_bass_kernel_spmd as _run

    nc = _bacc.Bacc("TRN2", target_bir_lowering=False, num_devices=1)
    arrays, args = {}, []
    early, late = shape_constants()
    given = [(n, np.ascontiguousarray(inputs[n])) for n in _NAMES] + [("early", early), ("late", late)]
    for name, a in given:
        arrays[f"in_{name}_dram"] = a
        args.append(nc.dram_tensor(f"in_{name}_dram", a.shape, mybir.dt.from_np(a.dtype), kind="ExternalInput").ap())
    args.append(nc.dram_tensor("out_0_dram", (1, T, D), F32, kind="ExternalOutput").ap())
    two_layer_program(nc, *args)
    r = _run(nc, [arrays], core_ids=[0])
    return r.results[0]["out_0_dram"]
```

```python
from collections import namedtuple
from contextlib import ExitStack

import numpy as np
import concourse.bass as bass
from concourse import mybir

F32 = mybir.dt.float32
I32 = mybir.dt.int32
U32 = mybir.dt.uint32
ALU = mybir.AluOpType
ACT = mybir.ActivationFunctionType
AX = mybir.AxisListType

P = 128
D = 1024
T = 256
KT = D // P
TT = T // P
EPS = 1e-6
NEG = -1e30

DIFF_HEADS = 4
UNITS = 8
GRID_W = 64
GRID_ROWS = T // GRID_W
NAT_KH, NAT_KW = 8, 16
LAM_INIT = 0.2
ATT_SCALE = 64 ** -0.5

E_N = 32
TOP_K = 4
SLOTS = 64
PASSES = -(-T // SLOTS)
LATER = E_N * (PASSES - 1)
LIMIT = 7.0
ALPHA = 1.702
BIG = 3.0e38

RET_HEADS = 4
NSA_HEADS = 8
CMP_BLOCK, CMP_STRIDE = 32, 16
N_CMP = T // CMP_STRIDE - 1
HG_HEADS = 8
LEVELS = 7
D_FF = 2816
FFN_STEPS = D_FF // 256

RING = 12
CHUNK = 2048
N_ADA_A, N_WIN, N_ADA_B, N_WOUT = 8, 12, 16, 4
PER_EXPERT = 12
C_ADA_A = 0
C_WIN = C_ADA_A + N_ADA_A
C_ADA_B = C_WIN + N_WIN
C_WOUT = C_ADA_B + N_ADA_B
C_MOE = C_WOUT + N_WOUT
C_EIN = C_MOE + PER_EXPERT * E_N
C_EOUT = C_EIN + 14
C_FFN0 = C_EOUT + 4
C_OIN = C_FFN0 + 3 * FFN_STEPS
C_OOUT = C_OIN + 16
C_FFN1 = C_OOUT + 4

EARLY = {}
LATE = {}


def _columns(table, sizes):
    at = 0
    for name, n in sizes:
        table[name] = (at, at + n)
        at += n
    return at


N_EARLY = _columns(EARLY, [("ident", P), ("ones", P), ("before", P), ("flip", P), ("slot", 2 * SLOTS), ("eps", 2),
                           ("job_place", LATER), ("job_expert", LATER), ("job_rank", 1),
                           ("window", GRID_W), ("alibi", DIFF_HEADS * TT * T)])
N_LATE = _columns(LATE, [("decay", RET_HEADS * 384), ("cos", T), ("sin", T), ("swap", P), ("causal", 384),
                         ("cmp_add", TT * N_CMP), ("cmp_keep", TT * N_CMP), ("levels", (LEVELS + 1) * P)])


def shape_constants():
    p = np.arange(P)
    early = np.zeros((P, N_EARLY), np.float32)

    def put(array, table, name, values):
        a, b = table[name]
        array[:, a:b] = np.asarray(values).reshape(P, b - a)

    put(early, EARLY, "ident", np.eye(P))
    put(early, EARLY, "ones", np.ones((P, P)))
    put(early, EARLY, "before", p[:, None] < p[None, :])
    put(early, EARLY, "flip", p[:, None] == (p // GRID_W * GRID_W + GRID_W - 1 - p % GRID_W)[None, :])
    put(early, EARLY, "slot", np.tile(np.arange(SLOTS), (P, 2)))
    put(early, EARLY, "job_place", np.tile(np.arange(LATER) - LATER, (P, 1)))
    put(early, EARLY, "job_expert", np.tile(np.arange(LATER) % E_N, (P, 1)))
    put(early, EARLY, "job_rank", p + 1)
    put(early, EARLY, "eps", np.tile(np.array([EPS, 1e-5]), (P, 1)))
    c, kc = (p % GRID_W)[:, None], np.arange(GRID_W)[None, :]
    first = np.clip(c - NAT_KW // 2, 0, GRID_W - NAT_KW)
    put(early, EARLY, "window", np.where((kc >= first) & (kc < first + NAT_KW), 0.0, NEG))
    q = np.arange(TT)[None, :, None] * P + p[:, None, None]
    dist = np.abs(q - np.arange(T)[None, None, :])
    slopes = 2.0 ** (-8.0 * np.arange(1, DIFF_HEADS + 1) / DIFF_HEADS)
    put(early, EARLY, "alibi", -slopes[None, :, None, None] * dist[:, None])

    late = np.zeros((P, N_LATE), np.float32)
    s = p[:, None]
    t = np.concatenate([np.arange(T), np.arange(P)])[None, :]
    gap = t - s
    log_gamma = np.log(1.0 - 2.0 ** (-5.0 - np.arange(RET_HEADS)))
    decay = np.where(gap[:, None, :] >= 0, np.exp(log_gamma[None, :, None] * np.maximum(gap, 0)[:, None, :]), 0.0)
    put(late, LATE, "decay", decay * P ** -0.5)
    half = P // 2
    inv = np.float32(10000.0) ** (-np.arange(half, dtype=np.float32) / np.float32(half))
    ang = np.arange(T, dtype=np.float32)[None, :] * inv[p % half][:, None]
    put(late, LATE, "cos", np.cos(ang))
    put(late, LATE, "sin", np.sin(ang) * np.where(p < half, -1.0, 1.0)[:, None])
    put(late, LATE, "swap", (p[:, None] + half) % P == p[None, :])
    tri = np.where(p[None, :] <= p[:, None], 0.0, NEG)
    put(late, LATE, "causal", np.concatenate([tri, 0 * tri, tri], axis=1))
    end = np.arange(N_CMP) * CMP_STRIDE + CMP_BLOCK - 1
    keep = end[None, None, :] <= (np.arange(TT)[None, :, None] * P + p[:, None, None])
    put(late, LATE, "cmp_add", np.where(keep, 0.0, NEG))
    put(late, LATE, "cmp_keep", keep)
    m, n = p[:, None], p[None, :]
    levels = [(m // (2 * h) == n // (2 * h)) & (m % (2 * h) < h) & (n % (2 * h) >= h)
              for h in (2 ** i for i in range(LEVELS))] + [m == n]
    put(late, LATE, "levels", np.stack(levels, axis=1))
    return early, late


NAMES = """ada_saved ada_turned alibi_loaded vec_loaded x_loaded early_loaded bias_loaded lam_loaded moe_loaded late_loaded cmp_loaded
vec_turned vec_saved c_ready x_turned x_ready lam_dots lam_spread lam_exp bias_flipped bias_ready
sq_ready ssq_ready root_ready h_ready chunk_done proj_saved
scores_ready neg_max probs_ready attn_ready attn_turned attn_saved heads_out mix_saved
sub_sq sub_ssq sub_root mix_ready dve_step 
logits_ready top_ready e_ready masks_ready ranks_ready gates_ready gates_turned gates_saved tok_turned tok_saved
count_ready 
masks_built gathered xg_saved st_saved hidden hidden_read glu_ready sig_ready act_ready act_turned act_saved
y_saved pass_over b1_even b1_odd jobs_listed jobs_turned
f_saved again_step
swapped rot_ready ret_scores ret_weighted ret_out ret_saved ret_sum ret_centred ret_sq ret_ssq ret_root
cmp_x cmp_hidden cmp_act cmp_out cmp_saved cmp_scores cmp_shift cmp_exp cmp_probs cmp_turned cmp_turn_saved
nsa_scores nsa_max nsa_probs nsa_weighted nsa_turned nsa_saved nsa_out
hg_level hg_scores hg_placed hg_cross hg_out hg_saved hg_sq hg_ssq hg_root
ffn_silu ffn_hidden y_turned y_out_saved out_stored""".split()
PASS_NAMES = """chunk_done masks_built gathered xg_saved st_saved hidden hidden_read glu_ready sig_ready
act_ready act_turned act_saved y_saved pass_over b1_even b1_odd""".split()


class Chain:

    def __init__(self, eng, sem):
        self.eng, self.sem, self.n, self.turn = eng, sem, 0, None

    def value(self):
        return self.n if self.turn is None else self.turn + self.n

    def link(self, ins):
        ins.then_inc(self.sem, 1)
        self.n += 1
        self.eng.wait_ge(self.sem, self.value())


def two_layer_program(nc, x, c, w_ada, b_ada, g_pre_mix, g_post_mix, w_in, w_out, lam_q1, lam_k1, lam_q2,
                      lam_k2, g_subln, nat_rpb, g_pre_ffn, g_post_ffn, w_router, b_router, w1, b1, w2, b2,
                      norm_mix_g_2, norm_ffn_g_2, final_norm_g_2, even_w_in_2, even_w_out_2, cmp_pos_k_2,
                      cmp_w1_k_2, cmp_w2_k_2, cmp_pos_v_2, cmp_w1_v_2, cmp_w2_v_2, odd_w_in_2, odd_w_out_2,
                      hgrn_norm_g_2, hgrn_lb_logits_2, ffn_w1_2, ffn_w3_2, ffn_w2_2, early, late, out):
    with ExitStack() as ctx:
        def sbuf(name, cols, dt=F32, rows=P):
            return ctx.enter_context(nc.sbuf_tensor(name, [rows, cols], dt))

        S = namedtuple("Semaphores", NAMES)(*[ctx.enter_context(nc.semaphore(n)) for n in NAMES])
        landed = [ctx.enter_context(nc.semaphore(f"landed{i}")) for i in range(RING)]
        again = namedtuple("AgainSemaphores", PASS_NAMES)(
            *[ctx.enter_context(nc.semaphore("again_" + n)) for n in PASS_NAMES])
        again_landed = [ctx.enter_context(nc.semaphore(f"again_landed{i}")) for i in range(RING)]

        ring = [sbuf(f"ring{i}", CHUNK) for i in range(RING)]
        xT = sbuf("xT", KT * T)
        hT = sbuf("hT", KT * T)
        sq = sbuf("sq", KT * T)
        mixT = sbuf("mixT", KT * T)
        small = sbuf("small", 1024)
        early_sb = sbuf("early_sb", N_EARLY)
        arena = sbuf("arena", 15900)
        jobs = sbuf("jobs", 2 * P + 1, I32, rows=1)
        psum = ctx.enter_context(nc.psum_tensor("psum", [P, 8 * 512], F32))
        bank = [psum[:, 512 * i:512 * i + 512] for i in range(8)]

        taken = [0]

        def carve(cols):
            taken[0] += cols
            assert taken[0] <= 1024
            return small[:, taken[0] - cols:taken[0]]

        def const(name):
            return early_sb[:, EARLY[name][0]:EARLY[name][1]]

        ident, ones, before, flip, slot_id, window = (
            const(n) for n in ("ident", "ones", "before", "flip", "slot", "window"))
        eps6, eps5 = const("eps")[:, 0:1], const("eps")[:, 1:2]
        alibi = const("alibi").rearrange("p (h n) -> p h n", h=DIFF_HEADS)
        cols_a, cols_b = carve(P), carve(2)
        silu_c = carve(KT * 32).rearrange("p (k m) -> p k m", m=32)
        spare = carve(7)
        mod = carve(48)
        pre_scale, post_scale = carve(16), carve(16)
        rstd = sbuf("rstd", T)
        negmax, rsum, lam2 = carve(UNITS * 4), carve(UNITS * 4), carve(4)

        def tiles(a):
            return a.rearrange("p (k t) -> p k t", t=T)

        def region(at, cols):
            assert at + cols <= 15900
            return arena[:, at:at + cols]

        diff_q, diff_k = tiles(region(0, 1024)), tiles(region(1024, 1024))
        nat_q, nat_k = tiles(region(2048, 1024)), tiles(region(3072, 1024))
        diff_v = region(4096, 1024).rearrange("p (a n) -> p a n", a=TT)
        nat_v = region(5120, 1024).rearrange("p (a n) -> p a n", a=TT)
        nat_bias = region(6144, 4096).rearrange("p (h n) -> p h n", h=8)
        score_sb = [region(10240, 1024), region(11264, 1024)]
        x_tok = region(10240, 2048).rearrange("p (a n) -> p a n", a=TT)
        attn_T = region(12288, 1024)
        rows_a = region(12288, P)
        rows_b = region(12288 + P, P)
        lam_rows = region(12288 + 2 * P, 4 * 64)
        router_w = region(13312, KT * E_N).rearrange("p (k e) -> p k e", k=KT)
        b2_sb = region(13568, D)[0:E_N, :]
        ada_rows = region(14592, 256)
        router_b = region(15104, E_N)[0:1, :]
        h_tok = region(0, 2048).rearrange("p (a n) -> p a n", a=TT)
        xg = [region(2048 + 512 * i, KT * SLOTS).rearrange("p (k s) -> p k s", s=SLOTS) for i in range(2)]
        act_T = region(3072, 512)
        y_sb = region(3584, 512)
        st_sb = [region(4096 + T * i, T) for i in range(2)]
        pick = [region(4608 + P * i, TT * SLOTS).rearrange("p (a s) -> p a s", a=TT) for i in range(2)]
        pick_g = [region(4864 + 256 * i, TT * 2 * SLOTS).rearrange("p (a s) -> p a s", a=TT) for i in range(2)]
        glu, lin, sig, act_rows = (region(5376 + 512 * i, 512) for i in range(4))
        b1_row = [mixT[0:1, :], sq[0:1, :]]
        pos = region(15140, TT * (PASSES * E_N + 2)).rearrange("p (a e) -> p a e", a=TT)
        gate = region(9028, TT * 34).rearrange("p (a e) -> p a e", a=TT)
        routed = region(9096, TT * E_N).rearrange("p (a e) -> p a e", a=TT)
        logits = region(9160, TT * 36).rearrange("p (a e) -> p a e", a=TT)
        replaced = region(9232, TT * 36).rearrange("p (a e) -> p a e", a=TT)
        top8 = region(9304, TT * 8).rearrange("p (a e) -> p a e", a=TT)
        neg_top, gsum = region(9320, 2), region(9322, 2)
        gates_T = region(9324, T)[0:E_N, :]
        wanted, rank_of, chosen = (region(8832 + LATER * i, LATER) if i < 2 else region(8544, LATER)
                                   for i in range(3))
        job_cols = region(9580, 4)
        late_sb = region(9600, N_LATE)
        assert 9600 + N_LATE <= 13312 + 256

        def late_const(name):
            return late_sb[:, LATE[name][0]:LATE[name][1]]

        raw_qk = tiles(region(0, 2048))
        weighted = region(0, 1536).rearrange("p (h n) -> p h n", h=RET_HEADS)
        rot_qk = tiles(region(2048, 2048))
        cmp_T = region(2048, 2048)[0:N_CMP, :].rearrange("p (h t) -> p h t", h=NSA_HEADS)
        ret_v = region(4096, 1024).rearrange("p (a n) -> p a n", a=TT)
        ret_g = tiles(region(5120, 1024))
        nsa_q = tiles(region(6144, 1024))
        cmp_in = tiles(region(7168, 512))
        slc_k, win_k = tiles(region(7680, 512)), tiles(region(8192, 512))
        slc_v = region(8704, 256).rearrange("p (a n) -> p a n", a=TT)
        win_v = region(8960, 256).rearrange("p (a n) -> p a n", a=TT)
        nsa_gate = region(9216, 48).rearrange("p (a n) -> p a n", a=TT)
        cmp_p = region(9264, 240).rearrange("p (n c) -> p n c", c=N_CMP)
        coef = region(9504, 48)
        cmp_w1_sb = [region(13312, 2048).rearrange("p (j n) -> p j n", n=64),
                     mixT[:, :].rearrange("p (j n) -> p j n", n=64)]
        cmp_x = [hT[:, 512 * i:512 * i + 480].rearrange("p (n j) -> p n j", j=CMP_BLOCK) for i in range(2)]
        centred = hT[:, 1024:2048]
        nsa_s = [region(13312 + 768 * i, 768).rearrange("p (h n) -> p h n", h=2) for i in range(2)]
        nsa_T = [sq[:, 768 * i:768 * i + 768].rearrange("p (h n) -> p h n", h=2) for i in range(2)]
        pos_rows = [region(12288 + 512 + P * i, P)[0:CMP_BLOCK, :] for i in range(2)]
        pos_cols = carve(2 * CMP_BLOCK).rearrange("p (i j) -> p i j", i=2)
        cmp_w2_sb = carve(2 * 64).rearrange("p (i n) -> p i n", i=2)
        cmp_act = carve(2 * N_CMP).rearrange("p (i n) -> p i n", i=2)
        cmp_k = carve(2 * N_CMP).rearrange("p (g n) -> p g n", g=2)
        cmp_v = carve(2 * 64)[0:N_CMP, :].rearrange("p (g n) -> p g n", g=2)
        cmp_max, cmp_sum = carve(16), carve(16)
        nsa_negmax, nsa_sum = carve(32), carve(32)
        hg_q, hg_f, hg_k, hg_g = (tiles(region(2048 * i, 2048)) for i in range(4))
        hg_v = region(8192, 2048).rearrange("p (a n) -> p a n", a=TT)
        hg_cross = region(10240, 1024).rearrange("p (h n) -> p h n", h=HG_HEADS)
        hg_near = region(13312, 2048).rearrange("p (n c) -> p n c", c=P)
        hg_pk, hg_qd, hg_kd = tiles(hT[:, :]), tiles(sq[:, :]), tiles(mixT[:, :])
        hg_o = tiles(region(2048, 2048))
        ffn_s = [region(512 * i, 512) for i in range(2)]
        ffn_h = [region(1024 + 512 * i, 512).rearrange("p (k t) -> p k t", k=2) for i in range(2)]
        out_tok = region(2048, 2048).rearrange("p (a n) -> p a n", a=TT)

        block = ctx.enter_context(nc.Block())

        @block.sync
        def _(sp):
            def slot_free(n):
                if n >= RING:
                    sp.wait_ge(S.chunk_done, n - RING + 1)

            def column_chunks(first, w, n, cols):
                for j in range(n):
                    slot_free(first + j)
                    m = min(256, cols - 256 * j)
                    sp.dma_start(ring[(first + j) % RING][:, 0:KT * m].rearrange("p (k n) -> p k n", k=KT),
                                 w.rearrange("(k p) n -> p k n", p=P)[:, :, 256 * j:256 * j + m]) \
                      .then_inc(landed[(first + j) % RING], 16)

            column_chunks(C_ADA_A, w_ada[0][:, 0:2048], N_ADA_A, 2048)
            column_chunks(C_WIN, w_in[0], N_WIN, 3072)
            column_chunks(C_ADA_B, w_ada[0][:, 2048:6144], N_ADA_B, 4096)
            column_chunks(C_WOUT, w_out[0], N_WOUT, D)

            w1_view = w1[0].rearrange("e (k p) n -> e k p n", p=P)
            w2_view = w2[0].rearrange("e (c k p) n -> e c p k n", p=P, k=2)

            def expert_chunks(e, wait, land):
                for j in range(PER_EXPERT):
                    wait(j)
                    home = ring[(C_MOE + j) % RING]
                    if j < 8:
                        src = w1_view[bass.ds(e, 1), j].rearrange("a p n -> p (a n)")
                        dst = home[:, :]
                    else:
                        src = w2_view[bass.ds(e, 1), j - 8].rearrange("a p k n -> p (a k) n")
                        dst = home[:, :].rearrange("p (k n) -> p k n", k=2)
                    sp.dma_start(dst, src).then_inc(land[(C_MOE + j) % RING], 16)

            with sp.Fori(0, E_N) as e:
                expert_chunks(e, lambda j: sp.wait_ge(S.chunk_done, e * PER_EXPERT + (C_MOE + j - RING + 1)),
                              landed)
            sp.wait_ge(S.count_ready, 1)
            pairs = sp.value_load(jobs[0:1, 2 * P:2 * P + 1], min_val=0, max_val=8)
            with sp.If(pairs > 0):
                sp.wait_ge(S.pass_over, 1)
                with sp.Fori(0, pairs) as i:
                    for r in range(2):
                        e = sp.value_load(jobs[0:1, bass.ds(i * 2 + (P + r), 1)], min_val=0, max_val=E_N - 1)
                        expert_chunks(e, lambda j: sp.wait_ge(again.chunk_done, i * 24 + (12 * r + j + 1)),
                                      again_landed)
                sp.wait_ge(again.pass_over, 1)

            column_chunks(C_EIN, even_w_in_2[0], 14, 3352)
            column_chunks(C_EOUT, even_w_out_2[0], 4, D)

            def ffn_chunks(first, layer):
                n = first
                wa, wb = (w[layer].rearrange("(k p) n -> p k n", p=P) for w in (ffn_w1_2, ffn_w3_2))
                wc = ffn_w2_2[layer].rearrange("(c k p) n -> c p k n", p=P, k=2)
                for i in range(FFN_STEPS + 1):
                    todo = []
                    if i < FFN_STEPS:
                        todo += [wa[:, :, 256 * i:256 * i + 256], wb[:, :, 256 * i:256 * i + 256]]
                    if i >= 1:
                        todo += [wc[i - 1]]
                    for src in todo:
                        slot_free(n)
                        sp.dma_start(ring[n % RING][:, :].rearrange("p (k n) -> p k n", k=src.shape[1]), src) \
                          .then_inc(landed[n % RING], 16)
                        n += 1

            ffn_chunks(C_FFN0, 0)
            column_chunks(C_OIN, odd_w_in_2[0], 16, 4096)
            column_chunks(C_OOUT, odd_w_out_2[0], 4, D)
            ffn_chunks(C_FFN1, 1)

            for a in range(TT):
                sp.wait_ge(S.y_out_saved, 2 * a + 2)
                sp.dma_start(out[0, a * P:(a + 1) * P, :], out_tok[:, a, :]).then_inc(S.out_stored, 16)
            sp.wait_ge(S.out_stored, 16 * TT)


        @block.gpsimd
        def _(pool):
            pool.dma_start(x_tok, x[0].rearrange("(a p) d -> p a d", p=P)).then_inc(S.x_loaded, 16)
            for i, v in enumerate((lam_q1, lam_k1, lam_q2, lam_k2)):
                pool.dma_start(lam_rows[0:1, 64 * i:64 * i + 64], v).then_inc(S.lam_loaded, 16)
            pool.dma_start(early_sb[:, EARLY["alibi"][0]:], early[:, EARLY["alibi"][0]:]).then_inc(S.alibi_loaded, 16)
            for r in range(GRID_ROWS):
                half = 64 * (r % 2)
                for h in range(8):
                    src = bass.AP(nat_rpb.tensor, h * 465 + (NAT_KH - 1 - r) * 31 + NAT_KW - 1 - (GRID_W - 1),
                                  [[1, GRID_W], [31, GRID_ROWS], [1, GRID_W]])
                    dst = nat_bias[half:half + 64, h, (r // 2) * T:(r // 2 + 1) * T]
                    pool.dma_start(dst.rearrange("p (a n) -> p a n", a=GRID_ROWS), src).then_inc(S.bias_loaded, 16)
            pool.dma_start(router_w, w_router[0].rearrange("(k p) e -> p k e", p=P)).then_inc(S.moe_loaded, 16)
            pool.dma_start(router_b, b_router).then_inc(S.moe_loaded, 16)
            pool.dma_start(b2_sb, b2[0]).then_inc(S.moe_loaded, 16)
            for i, v in enumerate((cmp_w2_k_2, cmp_w2_v_2)):
                for g in range(2):
                    pool.dma_start(cmp_w2_sb[64 * g:64 * g + 64, i, :], v[0]).then_inc(S.moe_loaded, 16)
            pool.wait_ge(S.mix_ready, 1)
            pool.dma_start(late_sb, late).then_inc(S.late_loaded, 16)
            pool.wait_ge(S.f_saved, 1)
            for i, v in enumerate((cmp_w1_k_2, cmp_w1_v_2)):
                for g in range(2):
                    pool.dma_start(cmp_w1_sb[i][64 * g:64 * g + 64, :, :],
                                   v[0].rearrange("(j d) n -> d j n", d=64)).then_inc(S.cmp_loaded, 16)

        N_VEC = 11 + 4

        @block.tensor
        def _(pe):
            def arrived(n):
                pe.wait_ge(landed[n % RING], 16 * (n // RING + 1))

            def cols(n, m=256):
                return ring[n % RING][:, 0:KT * m].rearrange("p (k n) -> p k n", k=KT)

            def vector_columns():
                pe.wait_ge(S.early_loaded, 16)
                pe.wait_ge(S.vec_loaded, 16 * N_VEC)
                nc.tensor.transpose(bank[6][:, 0:P], rows_a, ident)
                nc.tensor.transpose(bank[6][:, P:P + 2], rows_b[0:2, :], ident[0:2, 0:2])
                for i in range(2):
                    mm = nc.tensor.transpose(bank[6][:, 256 + 32 * i:288 + 32 * i], pos_rows[i], ident[0:32, 0:32])
                mm.then_inc(S.vec_turned, 1)

            def turn_x():
                pe.wait_ge(S.x_loaded, 16)
                for k in range(KT):
                    for a in range(TT):
                        mm = nc.tensor.transpose(bank[k // 2][:, (k % 2) * T + a * P:(k % 2) * T + (a + 1) * P],
                                                 x_tok[:, a, k * P:(k + 1) * P], ident)
                    if k % 2:
                        mm.then_inc(S.x_turned, 1)

            def lam_to_all():
                pe.wait_ge(S.lam_dots, 2)
                nc.tensor.matmul(bank[6][:, 400:402], ones[0:1, :], lam2[0:1, 0:2], start=True, stop=True) \
                  .then_inc(S.lam_spread, 1)

            def ada_columns(j):
                pe.wait_ge(S.ada_saved, j + 1)
                for h in range(2):
                    mm = nc.tensor.matmul(bank[7][:, 256 + 2 * j + h:257 + 2 * j + h], ada_rows[:, h * P:(h + 1) * P],
                                          ones[:, 0:1], start=True, stop=True)
                mm.then_inc(S.ada_turned, 1)

            def ada(j):
                if j >= 1 and j != N_ADA_A:
                    ada_columns(j - 1)
                n = C_ADA_A + j if j < N_ADA_A else C_ADA_B + j - N_ADA_A
                arrived(n)
                for k in range(KT):
                    g = k % 4
                    mm = nc.tensor.matmul(bank[7][32 * g:32 * g + 32, 0:256], silu_c[:, k, :], cols(n)[:, k, :],
                                          start=(k < 4), stop=(k >= 4))
                mm.then_inc(S.chunk_done, 1)

            def sum_squares(i):
                pe.wait_ge(S.sq_ready, i + 1)
                for k in range(KT):
                    mm = nc.tensor.matmul(bank[6][:, 0:T], ones, sq[:, k * T:(k + 1) * T],
                                          start=(k == 0), stop=(k == KT - 1))
                mm.then_inc(S.ssq_ready, 1)

            def project(n, j, src, parts, m=256):
                arrived(n)
                if j >= 2:
                    pe.wait_ge(S.proj_saved, j - 1)
                w, home, at = cols(n, m), bank[j % 2], 0
                if parts == "rows":
                    todo = [("r", a, 0, m) for a in range(TT)]
                elif parts == "columns":
                    todo = [("c", h, h * P, P) for h in range(2)]
                else:
                    todo = [("c", 0, 0, P)] + [("r", a, P, P) for a in range(TT)]
                for kind, i, c0, w_n in todo:
                    n_out = T if kind == "c" else w_n
                    for k in range(KT):
                        lhs, rhs = w[:, k, c0:c0 + w_n], src[:, k * T:(k + 1) * T]
                        if kind == "r":
                            lhs, rhs = src[:, k * T + i * P:k * T + (i + 1) * P], lhs
                        mm = nc.tensor.matmul(home[:, at:at + n_out], lhs, rhs, start=(k == 0), stop=(k == KT - 1))
                    at += n_out
                mm.then_inc(S.chunk_done, 1)

            def scores(u):
                if u >= 2:
                    pe.wait_ge(S.neg_max, u - 1)
                q, k = (diff_q, diff_k) if u < DIFF_HEADS else (nat_q, nat_k)
                i = u % DIFF_HEADS
                for m in range(2):
                    for a in range(TT):
                        mm = nc.tensor.matmul(bank[2 * (u % 2) + m][:, a * T:(a + 1) * T],
                                              q[64 * m:64 * m + 64, i, a * P:(a + 1) * P],
                                              k[64 * m:64 * m + 64, i, :], start=True, stop=True)
                mm.then_inc(S.scores_ready, 1)

            def turn_attention(u):
                pe.wait_ge(S.attn_ready, u + 1)
                if u >= 1:
                    pe.wait_ge(S.attn_saved, u)
                for m in range(1 if u < DIFF_HEADS else 2):
                    for b in range(TT):
                        for a in range(TT):
                            mm = nc.tensor.transpose(
                                bank[4 + m][:, b * T + a * P:b * T + (a + 1) * P],
                                score_sb[u % 2][:, m * 512 + a * T + b * P:m * 512 + a * T + (b + 1) * P], ident)
                mm.then_inc(S.attn_turned, 1)

            def heads(u):
                pe.wait_ge(S.attn_saved, u + 1)
                if u >= 1:
                    pe.wait_ge(S.mix_saved, u)
                home = bank[6][:, (u % 2) * T:(u % 2 + 1) * T]
                for m in range(1 if u < DIFF_HEADS else 2):
                    for b in range(TT):
                        if u < DIFF_HEADS:
                            v, dst = diff_v[:, b, u * P:(u + 1) * P], home
                        else:
                            h = 2 * (u - DIFF_HEADS) + m
                            v, dst = nat_v[:, b, h * 64:h * 64 + 64], home[64 * m:64 * m + 64, :]
                        mm = nc.tensor.matmul(dst, v, attn_T[:, m * 512 + b * T:m * 512 + (b + 1) * T],
                                              start=(b == 0), stop=(b == TT - 1))
                mm.then_inc(S.heads_out, 1)

            def ones_over(src, n, into, ready):
                for j in range(n):
                    mm = nc.tensor.matmul(bank[into + j][:, :], ones, src[:, 512 * j:512 * j + 512],
                                          start=True, stop=True)
                mm.then_inc(ready, 1)

            def flip_bias(r):
                if r == 0:
                    pe.wait_ge(S.bias_loaded, 16 * 32)
                    pe.wait_ge(S.x_ready, 1)
                    pe.wait_ge(S.vec_saved, 1)
                else:
                    pe.wait_ge(S.bias_ready, r)
                for i in range(4):
                    mm = nc.tensor.matmul(bank[2 + i], flip, nat_bias[:, 4 * r + i, :], start=True, stop=True)
                mm.then_inc(S.bias_flipped, 1)

            vector_columns()
            turn_x()
            lam_to_all()
            pe.wait_ge(S.c_ready, 1)
            for j in range(N_ADA_A):
                ada(j)
            ada_columns(N_ADA_A - 1)
            pe.wait_ge(S.lam_exp, 1)
            sum_squares(0)
            pe.wait_ge(S.h_ready, 1)
            for j in range(N_WIN):
                if j in (4, 8):
                    flip_bias(j // 4 - 1)
                project(C_WIN + j, j, hT, "rows" if j in (4, 5, 10, 11) else "columns")
            pe.wait_ge(S.proj_saved, N_WIN)
            pe.wait_ge(S.bias_ready, 2)
            for u in range(UNITS + 1):
                if u < UNITS:
                    scores(u)
                    ada(N_ADA_A + 2 * u)
                if u >= 1:
                    turn_attention(u - 1)
                    heads(u - 1)
                if u < UNITS:
                    ada(N_ADA_A + 2 * u + 1)
            ada_columns(2 * UNITS + N_ADA_A - 1)
            pe.wait_ge(S.sub_sq, 1)
            ones_over(sq, 2, 0, S.sub_ssq)
            pe.wait_ge(S.mix_ready, 1)
            for j in range(N_WOUT):
                project(C_WOUT + j, N_WIN + j, mixT, "columns")
            sum_squares(1)
            sum_squares(2)

            pe.wait_ge(S.h_ready, 2)
            pe.wait_ge(S.moe_loaded, 16 * 7)
            for a in range(TT):
                for k in range(KT):
                    nc.tensor.matmul(bank[4][:, a * E_N:(a + 1) * E_N], hT[:, k * T + a * P:k * T + (a + 1) * P],
                                     router_w[:, k, :], start=(k == 0), stop=False)
                mm = nc.tensor.matmul(bank[4][:, a * E_N:(a + 1) * E_N], ones[0:1, :], router_b, start=False, stop=True)
            mm.then_inc(S.logits_ready, 1)
            for a in range(TT):
                for k in range(KT):
                    mm = nc.tensor.transpose(bank[2 * a + k // 4][:, (k % 4) * P:(k % 4 + 1) * P],
                                             hT[:, k * T + a * P:k * T + (a + 1) * P], ident)
            mm.then_inc(S.tok_turned, 1)
            pe.wait_ge(S.masks_ready, 1)
            nc.tensor.matmul(bank[5][:, 0:E_N], before, routed[:, 0, :], start=True, stop=True)
            nc.tensor.matmul(bank[5][:, E_N:2 * E_N], ones, routed[:, 0, :], start=True, stop=False)
            nc.tensor.matmul(bank[5][:, E_N:2 * E_N], before, routed[:, 1, :], start=False, stop=True)
            nc.tensor.matmul(bank[5][:, 64:96], ones, routed[:, 0, :], start=True, stop=False)
            nc.tensor.matmul(bank[5][:, 64:96], ones, routed[:, 1, :], start=False, stop=True).then_inc(S.ranks_ready, 1)
            pe.wait_ge(S.jobs_listed, 1)
            for i in range(3):
                mm = nc.tensor.matmul(bank[5][0:1, P * i:P * (i + 1)], job_cols[:, i:i + 1], ident, start=True, stop=True)
            mm.then_inc(S.jobs_turned, 1)
            pe.wait_ge(S.gates_ready, 1)
            for a in range(TT):
                mm = nc.tensor.transpose(bank[6][0:E_N, a * P:(a + 1) * P], gate[:, a, 0:E_N], ident)
            mm.then_inc(S.gates_turned, 1)
            pe.wait_ge(S.gates_saved, 1)
            pe.wait_ge(S.tok_saved, 1)
            for k in range(KT):
                nc.tensor.matmul(bank[k // 2][:, (k % 2) * T:(k % 2 + 1) * T], b2_sb[:, k * P:(k + 1) * P], gates_T,
                                 start=(k % 2 == 0), stop=False, skip_group_check=True)

            def gather(M, r, value):
                pe.wait_ge(M.masks_built, value)
                for k in range(KT):
                    for a in range(TT):
                        nc.tensor.matmul(bank[6][:, k * SLOTS:(k + 1) * SLOTS],
                                         h_tok[:, a, k * P:(k + 1) * P], pick[r][:, a, :],
                                         start=(a == 0), stop=(a == TT - 1))
                for a in range(TT):
                    mm = nc.tensor.transpose(bank[7][:, a * P:(a + 1) * P], pick_g[r][:, a, :], ident)
                mm.then_inc(M.gathered, 1)

            def scatter(M, r, before, last=False):
                pe.wait_ge(M.y_saved, before + 1)
                pe.wait_ge(M.st_saved, before + 1)
                for t in range(4):
                    for h in range(2):
                        k, half = 4 * h + t, slice(64 * h, 64 * h + 64)
                        mm = nc.tensor.matmul(bank[k // 2][:, (k % 2) * T:(k % 2 + 1) * T],
                                              y_sb[half, t * P:(t + 1) * P], st_sb[r][half, :], start=False, stop=last,
                                              skip_group_check=True)
                return mm

            def expert(M, e, r, land, landed_value, b1_here, b1_value):
                pe.wait_ge(M.xg_saved, e + 1)
                pe.wait_ge(M.hidden_read, e + 1)
                for k in range(KT):
                    slot = (C_MOE + k) % RING
                    pe.wait_ge(land[slot], landed_value(k))
                    for q in range(2):
                        for h in range(2):
                            mm = nc.tensor.matmul(bank[4 + q][64 * h:64 * h + 64, :], xg[r][:, k, :],
                                                  ring[slot][:, (2 * h + q) * 512:(2 * h + q + 1) * 512],
                                                  start=(k == 0), stop=False)
                    mm.then_inc(M.chunk_done, 1)
                pe.wait_ge(b1_here, b1_value)
                for q in range(2):
                    for h in range(2):
                        mm = nc.tensor.matmul(bank[4 + q][64 * h:64 * h + 64, :], ones[0:1, 0:64],
                                              b1_row[r][:, (2 * h + q) * 512:(2 * h + q + 1) * 512],
                                              start=False, stop=True)
                mm.then_inc(M.hidden, 1)
                scatter(M, 1 - r, e)
                gather(M, 1 - r, e + 2)
                pe.wait_ge(M.act_ready, e + 1)
                pe.wait_ge(M.xg_saved, e + 2)
                for t in range(4):
                    mm = nc.tensor.transpose(bank[6][:, t * P:(t + 1) * P], act_rows[:, t * P:(t + 1) * P], ident)
                mm.then_inc(M.act_turned, 1)
                pe.wait_ge(M.act_saved, e + 1)
                pe.wait_ge(M.st_saved, e + 2)
                for j in range(8, 12):
                    slot = (C_MOE + j) % RING
                    pe.wait_ge(land[slot], landed_value(j))
                    w = ring[slot][:, :].rearrange("p (k n) -> p k n", k=2)
                    for k in range(2):
                        f = 2 * (j - 8) + k
                        at = (f % 4) * P + (f // 4) * 64
                        for h in range(2):
                            mm = nc.tensor.matmul(bank[7][64 * h:64 * h + 64, :], act_T[:, at:at + 64],
                                                  w[:, k, 512 * h:512 * h + 512], start=(f == 0), stop=(f == 7))
                    mm.then_inc(M.chunk_done, 1)

            def all_experts(M, pairs, land, turns_before):
                gather(M, 0, 1)
                with pe.Fori(0, pairs) as i:
                    for r in range(2):
                        expert(M, i * 2 + r, r, land, lambda j: i * 32 + 16 * (turns_before(j) + 1 + r),
                               (M.b1_even, M.b1_odd)[r], i * 16 + 16)
                scatter(M, 1, pairs * 2, last=True).then_inc(M.pass_over, 1)

            all_experts(S, E_N // 2, landed, lambda j: (C_MOE + j) // RING)
            pe.wait_ge(S.count_ready, 1)
            pairs = pe.value_load(jobs[0:1, 2 * P:2 * P + 1], min_val=0, max_val=8)
            with pe.If(pairs > 0):
                pe.sem_inc(again.chunk_done, RING)
                all_experts(again, pairs, again_landed, lambda j: 0)
            sum_squares(3)

            sum_squares(4)
            pe.wait_ge(S.h_ready, 3)
            kinds = ["columns"] * 4 + ["rows"] * 2 + ["columns"] * 5 + ["mixed"] * 2 + ["rows"]
            for j, kind in enumerate(kinds):
                project(C_EIN + j, 16 + j, hT, kind, 256 if j < 13 else 24)
            pe.wait_ge(S.late_loaded, 16)
            pe.wait_ge(S.cmp_loaded, 16 * 4)
            pe.wait_ge(S.cmp_x, 2)
            for i in range(2):
                for j in range(CMP_BLOCK):
                    for g in range(2):
                        half = slice(64 * g, 64 * g + 64)
                        mm = nc.tensor.matmul(bank[4 + g][half, N_CMP * i:N_CMP * (i + 1)], cmp_w1_sb[i][half, j, :],
                                              cmp_x[i][half, :, j], start=(j == 0), stop=(j == CMP_BLOCK - 1))
            mm.then_inc(S.cmp_hidden, 1)
            pe.wait_ge(S.proj_saved, 30)
            for j in range(4):
                mm = nc.tensor.matmul(bank[j][:, :], late_const("swap"), region(512 * j, 512), start=True, stop=True)
            mm.then_inc(S.swapped, 1)
            pe.wait_ge(S.cmp_act, 2)
            for g in range(2):
                half = slice(64 * g, 64 * g + 64)
                nc.tensor.matmul(bank[6 + g][half, 0:N_CMP], cmp_w2_sb[half, 0, :], cmp_act[half, 0, :], start=True, stop=True)
                mm = nc.tensor.matmul(bank[6 + g][0:N_CMP, 64:128], cmp_act[half, 1, :], cmp_w2_sb[half, 1, :],
                                      start=True, stop=True)
            mm.then_inc(S.cmp_out, 1)
            pe.wait_ge(S.rot_ready, 1)
            for h in range(RET_HEADS):
                q, k = rot_qk[:, h, :], rot_qk[:, 4 + h, :]
                nc.tensor.matmul(bank[h][:, 0:T], k[:, 0:P], q, start=True, stop=True)
                mm = nc.tensor.matmul(bank[h][:, T:384], k[:, P:T], q[:, P:T], start=True, stop=True)
            mm.then_inc(S.ret_scores, 1)
            pe.wait_ge(S.cmp_saved, 1)
            for h in range(NSA_HEADS):
                half = slice(64 * (h % 2), 64 * (h % 2) + 64)
                for a in range(TT):
                    at = ((h // 2) * TT + a) * N_CMP
                    mm = nc.tensor.matmul(bank[4 + h % 2][:, at:at + N_CMP], nsa_q[half, h // 2, a * P:(a + 1) * P],
                                          cmp_k[half, h // 4, :], start=True, stop=True)
            mm.then_inc(S.cmp_scores, 1)
            pe.wait_ge(S.ret_weighted, 1)
            for h in range(RET_HEADS):
                home, v = bank[h // 2][:, (h % 2) * T:(h % 2 + 1) * T], ret_v[:, :, h * P:(h + 1) * P]
                nc.tensor.matmul(home, v[:, 0, :], weighted[:, h, 0:T], start=True, stop=False)
                mm = nc.tensor.matmul(home[:, P:T], v[:, 1, :], weighted[:, h, T:384], start=False, stop=True)
            mm.then_inc(S.ret_out, 1)
            pe.wait_ge(S.ret_saved, 1)
            ones_over(mixT, 2, 2, S.ret_sum)
            pe.wait_ge(S.ret_sq, 1)
            ones_over(sq, 2, 0, S.ret_ssq)
            pe.wait_ge(S.cmp_probs, 1)
            pe.wait_ge(S.ret_root, 1)
            pe.wait_ge(S.ret_centred, 1)
            for h in range(NSA_HEADS):
                for a in range(TT):
                    n = (h % 2) * 8 + (h // 2) * TT + a
                    mm = nc.tensor.transpose(bank[h // 2][0:N_CMP, (h % 2) * T + a * P:(h % 2) * T + (a + 1) * P],
                                             cmp_p[:, n, :], ident)
            mm.then_inc(S.cmp_turned, 1)

            def nsa_score(u):
                i, keys = u // 2, (slc_k, win_k)[u % 2]
                if u == 0:
                    pe.wait_ge(S.cmp_turn_saved, 1)
                if u >= 2:
                    pe.wait_ge(S.nsa_max, u - 1)
                for h in range(2):
                    half, home = slice(64 * h, 64 * h + 64), bank[2 * (u % 2) + h]
                    q, k = nsa_q[half, i, :], keys[half, i // 2, :]
                    nc.tensor.matmul(home[:, 0:P], q[:, 0:P], k[:, 0:P], start=True, stop=True)
                    mm = nc.tensor.matmul(home[:, P:384], q[:, P:T], k, start=True, stop=True)
                mm.then_inc(S.nsa_scores, 1)

            def nsa_turn(u):
                pe.wait_ge(S.nsa_weighted, u + 1)
                if u >= 1:
                    pe.wait_ge(S.nsa_saved, u)
                for h in range(2):
                    for n in range(3):
                        mm = nc.tensor.transpose(bank[4 + h][:, n * P:(n + 1) * P], nsa_s[u % 2][:, h, n * P:(n + 1) * P],
                                                 ident)
                mm.then_inc(S.nsa_turned, 1)

            def nsa_heads(u):
                i, br = u // 2, u % 2
                pe.wait_ge(S.nsa_saved, u + 1)
                home = bank[6 + i % 2]
                if br == 0 and i >= 2:
                    pe.wait_ge(S.mix_saved, UNITS + i - 1)
                v = (slc_v, win_v)[br]
                for h in range(2):
                    dst, g = home[64 * h:64 * h + 64, 0:T], i // 2
                    if br == 0:
                        nc.tensor.matmul(dst, cmp_v[:, g, :], cmp_T[:, 2 * i + h, :], start=True, stop=False)
                    nc.tensor.matmul(dst, v[:, 0, 64 * g:64 * g + 64], nsa_T[u % 2][:, h, 0:T], start=False, stop=False)
                    mm = nc.tensor.matmul(dst[:, P:T], v[:, 1, 64 * g:64 * g + 64], nsa_T[u % 2][:, h, T:384],
                                          start=False, stop=(br == 1))
                mm.then_inc(S.nsa_out, 1)

            for u in range(9):
                if u < 8:
                    nsa_score(u)
                if u >= 1:
                    nsa_turn(u - 1)
                    nsa_heads(u - 1)
            pe.wait_ge(S.mix_ready, 2)
            pe.wait_ge(S.mix_saved, UNITS + 4)
            for j in range(4):
                project(C_EOUT + j, 30 + j, mixT, "columns")
            sum_squares(5)

            def ffn(first, layer):
                pe.wait_ge(S.h_ready, 4 + 2 * layer)
                n = first

                def down(i):
                    w = ring[n % RING][:, :].rearrange("p (k n) -> p k n", k=2)
                    arrived(n)
                    pe.wait_ge(S.ffn_hidden, layer * FFN_STEPS + i + 1)
                    for k in range(2):
                        for j in range(KT):
                            mm = nc.tensor.matmul(bank[j // 2][:, (j % 2) * T:(j % 2 + 1) * T], w[:, k, j * P:(j + 1) * P],
                                                  ffn_h[i % 2][:, k, :], start=(i == 0 and k == 0 and j % 2 == 0),
                                                  stop=(i == FFN_STEPS - 1 and k == 1), skip_group_check=True)
                    mm.then_inc(S.chunk_done, 1)

                for i in range(FFN_STEPS + 1):
                    if i < FFN_STEPS:
                        if i >= 2:
                            pe.wait_ge(S.ffn_hidden, layer * FFN_STEPS + i - 1)
                        for b in range(2):
                            arrived(n)
                            for h in range(2):
                                for k in range(KT):
                                    mm = nc.tensor.matmul(bank[4 + 2 * (i % 2) + b][:, h * T:(h + 1) * T],
                                                          cols(n)[:, k, h * P:(h + 1) * P], hT[:, k * T:(k + 1) * T],
                                                          start=(k == 0), stop=(k == KT - 1))
                            mm.then_inc(S.chunk_done, 1)
                            n += 1
                    if i >= 1:
                        down(i - 1)
                        n += 1

            ffn(C_FFN0, 0)
            sum_squares(6)
            pe.wait_ge(S.h_ready, 5)

            for j in range(16):
                project(C_OIN + j, 34 + j, hT, "rows" if 8 <= j < 12 else "columns")
            pe.wait_ge(S.proj_saved, 50)
            for step in range(2 * (LEVELS + 1)):
                pe.wait_ge(S.hg_level, step + 1)
                if step >= 4:
                    pe.wait_ge(S.hg_placed, step - 3)
                q, k = (hg_q, hg_k) if step < 2 else (hg_qd, hg_kd)
                for n in range(8):
                    h, a = 4 * (step % 2) + n // TT, n % TT
                    mm = nc.tensor.matmul(bank[2 * (step % 4) + n // 4][:, (n % 4) * P:(n % 4 + 1) * P],
                                          k[:, h, a * P:(a + 1) * P], q[:, h, a * P:(a + 1) * P], start=True, stop=True)
                mm.then_inc(S.hg_scores, 1)
            pe.wait_ge(S.hg_level, 2 * (LEVELS + 1) + 1)
            pe.wait_ge(S.hg_placed, 2 * (LEVELS + 1))
            for h in range(HG_HEADS):
                mm = nc.tensor.matmul(bank[h // 4][:, (h % 4) * P:(h % 4 + 1) * P], hg_kd[:, h, 0:P], hg_qd[:, h, P:T],
                                      start=True, stop=True)
            mm.then_inc(S.hg_scores, 1)
            pe.wait_ge(S.hg_placed, 2 * (LEVELS + 1) + 1)
            for h in range(HG_HEADS):
                home, v = bank[4 + h // 2][:, (h % 2) * T:(h % 2 + 1) * T], hg_v[:, :, h * P:(h + 1) * P]
                nc.tensor.matmul(home[:, 0:P], v[:, 0, :], hg_near[:, h * TT, :], start=True, stop=True)
                nc.tensor.matmul(home[:, P:T], v[:, 0, :], hg_cross[:, h, :], start=True, stop=False)
                mm = nc.tensor.matmul(home[:, P:T], v[:, 1, :], hg_near[:, h * TT + 1, :], start=False, stop=True)
            mm.then_inc(S.hg_out, 1)
            pe.wait_ge(S.hg_sq, 1)
            ones_over(sq, 4, 0, S.hg_ssq)
            pe.wait_ge(S.mix_ready, 3)
            for j in range(4):
                project(C_OOUT + j, 50 + j, mixT, "columns")
            sum_squares(7)
            ffn(C_FFN1, 1)
            sum_squares(8)
            pe.wait_ge(S.h_ready, 7)
            for a in range(TT):
                for k in range(KT):
                    mm = nc.tensor.transpose(bank[2 * a + k // 4][:, (k % 4) * P:(k % 4 + 1) * P],
                                             hT[:, k * T + a * P:k * T + (a + 1) * P], ident)
                mm.then_inc(S.y_turned, 1)

        def bcast(a, n):
            if len(a.shape) == 2:
                return a.unsqueeze(1).broadcast_to([a.shape[0], n, a.shape[1]])
            return a.broadcast_to([a.shape[0], a.shape[1], n])

        @block.scalar
        def _(act):
            def norm(i, src):
                nc.scalar.activation(sq[:, :], src[:, :], ACT.Square).then_inc(S.sq_ready, 1)
                act.wait_ge(S.ssq_ready, i + 1)
                nc.scalar.activation(rstd[:, :], bank[6][:, 0:T], ACT.Sqrt, bias=eps6, scale=1.0 / D) \
                  .then_inc(S.root_ready, 1)

            def save(j, first, n, *jobs):
                act.wait_ge(S.chunk_done, first + n + 1)
                for dst, a, b, func, scale in jobs:
                    src = bank[j % 2][:, a:b]
                    if len(dst.shape) == 3:
                        src = src.rearrange("p (k n) -> p k n", k=dst.shape[1])
                    ins = nc.scalar.activation(dst, src, func, scale=scale)
                ins.then_inc(S.proj_saved, 1)

            act.dma_start(early_sb[:, 0:EARLY["alibi"][0]], early[:, 0:EARLY["alibi"][0]]).then_inc(S.early_loaded, 16)
            at = 0
            for v in (c, b_ada, g_pre_mix, g_post_mix, g_pre_ffn, g_post_ffn, norm_mix_g_2, norm_ffn_g_2):
                n = v.shape[0] * v.shape[1] // P
                act.dma_start(rows_a[at:at + n, :], v.rearrange("a (n p) -> (a n) p", p=P)).then_inc(S.vec_loaded, 16)
                at += n
            act.dma_start(rows_a[at:at + KT, :], final_norm_g_2.rearrange("(n p) -> n p", p=P)).then_inc(S.vec_loaded, 16)
            act.dma_start(rows_b[0:1, :], g_subln).then_inc(S.vec_loaded, 16)
            act.dma_start(rows_b[1:2, :], hgrn_norm_g_2).then_inc(S.vec_loaded, 16)
            for i, v in enumerate((cmp_pos_k_2, cmp_pos_v_2)):
                for g in range(2):
                    act.dma_start(pos_rows[i][:, 64 * g:64 * g + 64], v[0]).then_inc(S.vec_loaded, 16)
            act.wait_ge(S.vec_saved, 1)
            nc.scalar.activation(silu_c[:, :, 0:1], cols_a[:, 0:KT].unsqueeze(2), ACT.Silu).then_inc(S.c_ready, 1)
            for i in range(4):
                act.wait_ge(S.x_turned, i + 1)
                ins = nc.scalar.activation(xT[:, 512 * i:512 * i + 512], bank[i], ACT.Copy)
            ins.then_inc(S.x_ready, 1)
            act.wait_ge(S.lam_spread, 1)
            nc.scalar.activation(lam2[:, 2:4], bank[6][:, 400:402], ACT.Exp).then_inc(S.lam_exp, 1)
            act.wait_ge(S.x_ready, 1)
            norm(0, xT)
            win_dst = [diff_q[:, 0:2, :], diff_q[:, 2:4, :], diff_k[:, 0:2, :], diff_k[:, 2:4, :],
                       diff_v[:, :, 0:256], diff_v[:, :, 256:512],
                       nat_q[:, 0:2, :], nat_q[:, 2:4, :], nat_k[:, 0:2, :], nat_k[:, 2:4, :],
                       nat_v[:, :, 0:256], nat_v[:, :, 256:512]]
            for j, dst in enumerate(win_dst):
                save(j, C_WIN, j, (dst, 0, 512, ACT.Copy, 1.0))
            for u in range(UNITS + 1):
                if u < UNITS:
                    act.wait_ge(S.neg_max, u + 1)
                    for n in range(4):
                        piece = score_sb[u % 2][:, n * T:(n + 1) * T]
                        nc.scalar.activation(piece, piece, ACT.Exp, bias=negmax[:, 4 * u + n:4 * u + n + 1],
                                             accum_out=rsum[:, 4 * u + n:4 * u + n + 1]).then_inc(S.probs_ready, 1)
                if u >= 1:
                    act.wait_ge(S.attn_turned, u)
                    if u >= 2:
                        act.wait_ge(S.heads_out, u - 1)
                    for m in range(1 if u - 1 < DIFF_HEADS else 2):
                        ins = nc.scalar.activation(attn_T[:, 512 * m:512 * m + 512], bank[4 + m], ACT.Copy)
                    ins.then_inc(S.attn_saved, 1)
                    act.wait_ge(S.heads_out, u)
                    nc.scalar.activation(mixT[:, (u - 1) * T:u * T], bank[6][:, ((u - 1) % 2) * T:((u - 1) % 2 + 1) * T],
                                         ACT.Copy).then_inc(S.mix_saved, 1)
            act.wait_ge(S.mix_saved, UNITS)
            nc.scalar.activation(sq[:, 0:1024], mixT[:, 0:1024], ACT.Square).then_inc(S.sub_sq, 1)
            act.wait_ge(S.sub_ssq, 1)
            nc.scalar.activation(score_sb[0], psum[:, 0:1024], ACT.Sqrt, bias=eps6, scale=1.0 / P) \
              .then_inc(S.sub_root, 1)
            for j in range(N_WOUT):
                save(N_WIN + j, C_WOUT, j, (hT[:, 512 * j:512 * j + 512], 0, 512, ACT.Copy, 1.0))
            act.wait_ge(S.proj_saved, 16)
            norm(1, hT)
            act.wait_ge(S.x_ready, 2)
            norm(2, xT)

            act.wait_ge(S.top_ready, 1)
            for a in range(TT):
                nc.scalar.activation(gate[:, a, 0:E_N], logits[:, a, 0:E_N], ACT.Exp, bias=neg_top[:, a:a + 1]) \
                  .then_inc(S.e_ready, 1)
            act.wait_ge(S.tok_turned, 1)
            for a in range(TT):
                ins = nc.scalar.activation(h_tok[:, a, :], psum[:, 1024 * a:1024 * a + 1024], ACT.Copy)
            ins.then_inc(S.tok_saved, 1)

            def save_tokens(M, r, value):
                act.wait_ge(M.gathered, value)
                nc.scalar.activation(xg[r], bank[6].rearrange("p (k s) -> p k s", s=SLOTS), ACT.Copy) \
                  .then_inc(M.xg_saved, 1)
                nc.scalar.activation(st_sb[r], bank[7][:, 0:T], ACT.Copy).then_inc(M.st_saved, 1)

            def experts(M, pairs, before, expert_of):
                nc.scalar.activation(spare[:, 0:1], eps6, ACT.Copy).then_inc(M.y_saved, 1)
                save_tokens(M, 0, 1)
                with act.Fori(0, pairs) as i:
                    for r in range(2):
                        e = i * 2 + r
                        act.dma_start(b1_row[r], b1[0][bass.ds(expert_of(i * 2 + r), 1), :]) \
                           .then_inc((M.b1_even, M.b1_odd)[r], 16)
                        act.wait_ge(M.glu_ready, e + 1)
                        nc.scalar.activation(sig, glu, ACT.Sigmoid, scale=ALPHA).then_inc(M.sig_ready, 1)
                        save_tokens(M, 1 - r, e + 2)
                        act.wait_ge(M.act_turned, e + 1)
                        nc.scalar.activation(act_T, bank[6], ACT.Copy).then_inc(M.act_saved, 1)
                        act.wait_ge(M.chunk_done, e * PER_EXPERT + (before + 12))
                        nc.scalar.activation(y_sb, bank[7], ACT.Copy).then_inc(M.y_saved, 1)

            experts(S, E_N // 2, C_MOE, lambda n: n)
            act.wait_ge(S.count_ready, 1)
            pairs = act.value_load(jobs[0:1, 2 * P:2 * P + 1], min_val=0, max_val=8)
            with act.If(pairs > 0):
                act.wait_ge(S.pass_over, 1)
                experts(again, pairs, RING, lambda n: act.value_load(jobs[0:1, bass.ds(n + P, 1)], min_val=0,
                                                                     max_val=E_N - 1))
                act.wait_ge(again.pass_over, 1)
            act.wait_ge(S.pass_over, 1)
            nc.scalar.activation(hT[:, :], psum[:, 0:2048], ACT.Copy).then_inc(S.f_saved, 1)
            act.wait_ge(S.f_saved, 1)
            norm(3, hT)
            act.wait_ge(S.x_ready, 3)
            norm(4, xT)

            def twice(dst, lo=0):
                return [(dst[64 * half:64 * half + 64, g, :], g) for half in range(2) for g in range(2)]

            dsts = [raw_qk[:, 2 * j:2 * j + 2, :] for j in range(4)] + [ret_v[:, :, 256 * j:256 * j + 256] for j in range(2)]
            for j, dst in enumerate(dsts):
                save(16 + j, C_EIN, j, (dst, 0, 512, ACT.Copy, 1.0))
            for j in range(2):
                save(22 + j, C_EIN, 6 + j, (ret_g[:, 2 * j:2 * j + 2, :], 0, 512, ACT.Silu, 1.0))
            for j in range(2):
                save(24 + j, C_EIN, 8 + j, (nsa_q[:, 2 * j:2 * j + 2, :], 0, 512, ACT.Copy, 1.0))
            save(26, C_EIN, 10, (cmp_in, 0, 512, ACT.Copy, 1.0))
            for j, (keys, values) in enumerate(((slc_k, slc_v), (win_k, win_v))):
                home = bank[(27 + j) % 2]
                act.wait_ge(S.chunk_done, C_EIN + 11 + j + 1)
                for dst, g in twice(keys):
                    nc.scalar.activation(dst, home[64 * g:64 * g + 64, 0:T], ACT.Copy)
                nc.scalar.activation(values, home[:, T:512].rearrange("p (a n) -> p a n", a=TT), ACT.Copy) \
                  .then_inc(S.proj_saved, 1)
            save(29, C_EIN, 13, (nsa_gate, 0, 48, ACT.Sigmoid, 1.0))

            act.wait_ge(S.cmp_hidden, 1)
            for g in range(2):
                half = slice(64 * g, 64 * g + 64)
                nc.scalar.activation(cmp_act[half, :, :], bank[4 + g][half, 0:2 * N_CMP].rearrange("p (i n) -> p i n", i=2),
                                     ACT.Gelu_apprx_tanh).then_inc(S.cmp_act, 1)
            act.wait_ge(S.cmp_out, 1)
            for dst, g in twice(cmp_k):
                nc.scalar.activation(dst, bank[6 + g][64 * g:64 * g + 64, 0:N_CMP], ACT.Copy)
            for g in range(2):
                ins = nc.scalar.activation(cmp_v[:, g, :], bank[6 + g][0:N_CMP, 64:128], ACT.Copy)
            ins.then_inc(S.cmp_saved, 1)
            act.wait_ge(S.ret_out, 1)
            nc.scalar.activation(mixT[:, 0:1024], psum[:, 0:1024], ACT.Copy).then_inc(S.ret_saved, 1)
            act.wait_ge(S.cmp_shift, 1)
            nc.scalar.activation(cmp_p, cmp_p, ACT.Exp).then_inc(S.cmp_exp, 1)
            act.wait_ge(S.ret_centred, 1)
            nc.scalar.activation(sq[:, 0:1024], centred, ACT.Square).then_inc(S.ret_sq, 1)
            act.wait_ge(S.ret_ssq, 1)
            nc.scalar.activation(sq[:, 1024:2048], psum[:, 0:1024], ACT.Sqrt, bias=eps5, scale=1.0 / P) \
              .then_inc(S.ret_root, 1)
            act.wait_ge(S.cmp_turned, 1)
            nc.scalar.activation(cmp_T, psum[0:N_CMP, 0:2048].rearrange("p (h t) -> p h t", t=T), ACT.Copy) \
              .then_inc(S.cmp_turn_saved, 1)
            for u in range(9):
                if u < 8:
                    act.wait_ge(S.nsa_max, u + 1)
                    for h in range(2):
                        for a, (lo, hi) in enumerate(((0, P), (P, 384))):
                            n = 4 * u + 2 * h + a
                            piece = nsa_s[u % 2][:, h, lo:hi]
                            nc.scalar.activation(piece, piece, ACT.Exp, bias=nsa_negmax[:, n:n + 1],
                                                 accum_out=nsa_sum[:, n:n + 1]).then_inc(S.nsa_probs, 1)
                if u >= 1:
                    act.wait_ge(S.nsa_turned, u)
                    if u >= 3:
                        act.wait_ge(S.nsa_out, u - 2)
                    nc.scalar.activation(nsa_T[(u - 1) % 2], psum[:, 4 * 512:6 * 512].rearrange("p (h n) -> p h n", h=2)[:, :, 0:384],
                                         ACT.Copy).then_inc(S.nsa_saved, 1)
                    if u % 2 == 0:
                        i = u // 2 - 1
                        act.wait_ge(S.nsa_out, u)
                        nc.scalar.activation(mixT[:, (4 + i) * T:(5 + i) * T], bank[6 + i % 2][:, 0:T], ACT.Copy) \
                          .then_inc(S.mix_saved, 1)
            act.wait_ge(S.proj_saved, 34)
            norm(5, xT)

            def ffn(first, layer):
                for i in range(FFN_STEPS):
                    w1_at = first + (3 * i - 1 if i else 0)
                    act.wait_ge(S.chunk_done, w1_at + 1)
                    if i >= 2:
                        act.wait_ge(S.ffn_hidden, layer * FFN_STEPS + i - 1)
                    nc.scalar.activation(ffn_s[i % 2], bank[4 + 2 * (i % 2)], ACT.Silu).then_inc(S.ffn_silu, 1)

            ffn(C_FFN0, 0)
            act.wait_ge(S.x_ready, 4)
            norm(6, xT)

            for j in range(4):
                save(34 + j, C_OIN, j, (hg_q[:, 2 * j:2 * j + 2, :], 0, 512, ACT.Silu, 1.0))
            for j in range(4):
                save(38 + j, C_OIN, 4 + j, (hg_f[:, 2 * j:2 * j + 2, :], 0, 512, ACT.Sigmoid, 1.0),
                     (hg_k[:, 2 * j:2 * j + 2, :], 0, 512, ACT.Sigmoid, -1.0))
            for j in range(4):
                save(42 + j, C_OIN, 8 + j, (hg_v[:, :, 256 * j:256 * j + 256], 0, 512, ACT.Copy, 1.0))
            for j in range(4):
                save(46 + j, C_OIN, 12 + j, (hg_g[:, 2 * j:2 * j + 2, :], 0, 512, ACT.Sigmoid, 1.0))
            act.wait_ge(S.hg_out, 1)
            nc.scalar.activation(hg_o, psum[:, 2048:4096].rearrange("p (k t) -> p k t", t=T), ACT.Copy, scale=P ** -0.5) \
              .then_inc(S.hg_saved, 1)
            act.wait_ge(S.hg_saved, 1)
            nc.scalar.activation(tiles(sq[:, :]), hg_o, ACT.Square).then_inc(S.hg_sq, 1)
            act.wait_ge(S.hg_ssq, 1)
            nc.scalar.activation(hT[:, :], psum[:, 0:2048], ACT.Sqrt, bias=eps6, scale=1.0 / P).then_inc(S.hg_root, 1)
            act.wait_ge(S.proj_saved, 54)
            norm(7, xT)
            ffn(C_FFN1, 1)
            act.wait_ge(S.x_ready, 5)
            norm(8, xT)
            for a in range(TT):
                act.wait_ge(S.y_turned, a + 1)
                for k in range(2):
                    nc.scalar.activation(out_tok[:, a, 512 * k:512 * k + 512], bank[2 * a + k], ACT.Copy) \
                      .then_inc(S.y_out_saved, 1)

        @block.vector
        def _(dve):
            main_chain = Chain(dve, S.dve_step)
            link = main_chain.link
            V = nc.vector

            def norm(i, src):
                dve.wait_ge(S.root_ready, i + 1)
                link(V.reciprocal(rstd[:, :], rstd[:, :]))
                link(V.tensor_tensor(tiles(sq[:, :]), tiles(src[:, :]), bcast(rstd[:, :], KT), ALU.mult))

            def modulated(scale0, shift0):
                for k in range(KT):
                    ins = V.tensor_scalar(hT[:, k * T:(k + 1) * T], sq[:, k * T:(k + 1) * T],
                                          pre_scale[:, scale0 + k:scale0 + k + 1], mod[:, shift0 + k:shift0 + k + 1],
                                          ALU.mult, ALU.add)
                ins.then_inc(S.h_ready, 1)

            def gained(col):
                for k in range(KT):
                    ins = V.tensor_scalar(hT[:, k * T:(k + 1) * T], sq[:, k * T:(k + 1) * T],
                                          cols_a[:, col + k:col + k + 1], None, ALU.mult)
                ins.then_inc(S.h_ready, 1)

            def onto_x(scale0):
                for k in range(KT):
                    ins = V.scalar_tensor_tensor(out=xT[:, k * T:(k + 1) * T], in0=sq[:, k * T:(k + 1) * T],
                                                 scalar=post_scale[:, scale0 + k:scale0 + k + 1],
                                                 in1=xT[:, k * T:(k + 1) * T], op0=ALU.mult, op1=ALU.add)
                ins.then_inc(S.x_ready, 1)

            V.memset(silu_c, 0.0)
            dve.wait_ge(S.vec_turned, 1)
            V.tensor_copy(cols_a, bank[6][:, 0:P])
            V.tensor_copy(cols_b, bank[6][:, P:P + 2])
            V.tensor_copy(pos_cols, bank[6][:, 256:320].rearrange("p (i j) -> p i j", i=2)) \
             .then_inc(S.vec_saved, 1)
            dve.wait_ge(S.lam_loaded, 16 * 4)
            for i in range(2):
                a = lam_rows[0:1, 128 * i:128 * i + 64]
                V.tensor_tensor_reduce(a, a, lam_rows[0:1, 128 * i + 64:128 * i + 128], 1.0, 0.0, ALU.mult, ALU.add,
                                       lam2[0:1, i:i + 1]).then_inc(S.lam_dots, 1)
            dve.wait_ge(S.vec_saved, 1)

            def save_ada(j):
                n = C_ADA_A + j if j < N_ADA_A else C_ADA_B + j - N_ADA_A
                dve.wait_ge(S.chunk_done, n + 1)
                if j >= 1:
                    dve.wait_ge(S.ada_turned, j)
                V.tensor_copy(ada_rows[:, :], bank[7][:, 0:256]).then_inc(S.ada_saved, 1)

            for j in range(N_ADA_A):
                save_ada(j)
            dve.wait_ge(S.ada_turned, N_ADA_A)
            link(V.tensor_tensor(mod[:, 0:16], bank[7][:, 256:272], cols_a[:, 8:24], ALU.add))
            link(V.scalar_tensor_tensor(out=pre_scale[:, 0:8], in0=mod[:, 8:16], scalar=1.0, in1=cols_a[:, 56:64],
                                        op0=ALU.add, op1=ALU.mult))
            norm(0, xT)
            modulated(0, 0)
            dve.wait_ge(S.lam_exp, 1)
            link(V.scalar_tensor_tensor(out=lam2[:, 0:1], in0=lam2[:, 3:4], scalar=-LAM_INIT, in1=lam2[:, 2:3],
                                        op0=ALU.add, op1=ALU.subtract))
            for r in range(2):
                dve.wait_ge(S.bias_flipped, r + 1)
                four = nat_bias[:, 4 * r:4 * r + 4, :].rearrange("p h n -> p (h n)")
                V.tensor_tensor(four.rearrange("p (m c) -> p m c", c=GRID_W),
                                psum[:, 1024:3072].rearrange("p (m c) -> p m c", c=GRID_W),
                                bcast(window, 2048 // GRID_W), ALU.add).then_inc(S.bias_ready, 1)
            dve.wait_ge(S.bias_ready, 2)

            dve.wait_ge(S.alibi_loaded, 16)
            for u in range(UNITS + 1):
                if u < UNITS:
                    i = u % DIFF_HEADS
                    dve.wait_ge(S.scores_ready, u + 1)
                    if u >= 2:
                        dve.wait_ge(S.attn_turned, u - 1)
                    for m in range(2):
                        bias = alibi[:, i, :] if u < DIFF_HEADS else nat_bias[:, 2 * i + m, :]
                        ins = V.scalar_tensor_tensor(out=score_sb[u % 2][:, 512 * m:512 * m + 512],
                                                     in0=bank[2 * (u % 2) + m], scalar=ATT_SCALE, in1=bias,
                                                     op0=ALU.mult, op1=ALU.add)
                    link(ins)
                    some = negmax[:, 4 * u:4 * u + 4]
                    link(V.tensor_reduce(some, tiles(score_sb[u % 2]), AX.X, ALU.max))
                    V.tensor_scalar(some, some, -1.0, None, ALU.mult).then_inc(S.neg_max, 1)
                    save_ada(N_ADA_A + 2 * u)
                if u >= 1:
                    v = u - 1
                    dve.wait_ge(S.probs_ready, 4 * (v + 1))
                    r = rsum[:, 4 * v:4 * v + 4]
                    link(V.reciprocal(r, r))
                    if v < DIFF_HEADS:
                        link(V.tensor_scalar(r[:, 2:4], r[:, 2:4], lam2[:, 0:1], None, ALU.mult))
                    probs = tiles(score_sb[v % 2])
                    ins = V.tensor_tensor(probs, probs, bcast(r.unsqueeze(2), T), ALU.mult)
                    if v < DIFF_HEADS:
                        link(ins)
                        s = score_sb[v % 2]
                        ins = V.tensor_tensor(s[:, 0:512], s[:, 0:512], s[:, 512:1024], ALU.add)
                    ins.then_inc(S.attn_ready, 1)
                if u < UNITS:
                    save_ada(N_ADA_A + 2 * u + 1)
            dve.wait_ge(S.ada_turned, N_ADA_A + 2 * UNITS)
            link(V.tensor_tensor(mod[:, 16:48], bank[7][:, 272:304], cols_a[:, 24:56], ALU.add))
            V.scalar_tensor_tensor(out=pre_scale[:, 8:16], in0=mod[:, 32:40], scalar=1.0, in1=cols_a[:, 72:80],
                                   op0=ALU.add, op1=ALU.mult)
            V.tensor_tensor(post_scale[:, 0:8], mod[:, 16:24], cols_a[:, 64:72], ALU.mult)
            link(V.tensor_tensor(post_scale[:, 8:16], mod[:, 40:48], cols_a[:, 80:88], ALU.mult))
            dve.wait_ge(S.sub_root, 1)
            link(V.reciprocal(score_sb[0], score_sb[0]))
            link(V.tensor_tensor(mixT[:, 0:1024], mixT[:, 0:1024], score_sb[0], ALU.mult))
            V.tensor_scalar(mixT[:, 0:1024], mixT[:, 0:1024], cols_b[:, 0:1], 1.0 - LAM_INIT, ALU.mult, ALU.mult) \
             .then_inc(S.mix_ready, 1)
            norm(1, hT)
            onto_x(0)
            norm(2, xT)
            modulated(8, 24)

            dve.wait_ge(S.logits_ready, 1)
            V.memset(logits[:, :, E_N:E_N + 4], BIG)
            link(V.tensor_copy(logits[:, :, 0:E_N], bank[4][:, 0:TT * E_N].rearrange("p (a e) -> p a e", a=TT)))
            for a in range(TT):
                ins = V.max(top8[:, a, :], logits[:, a, 0:E_N])
            link(ins)
            V.tensor_scalar(neg_top.unsqueeze(2), top8[:, :, 0:1], -1.0, None, ALU.mult).then_inc(S.top_ready, 1)
            link(V.memset(top8[:, :, TOP_K:8], BIG))
            for a in range(TT):
                ins = V.match_replace(replaced[:, a, :], top8[:, a, :], logits[:, a, :], -BIG)
            link(ins)
            V.tensor_scalar(routed, replaced[:, :, 0:E_N], -BIG, None, ALU.is_equal).then_inc(S.masks_ready, 1)
            dve.wait_ge(S.masks_ready, 1)
            dve.wait_ge(S.e_ready, TT)
            g = gate[:, :, 0:E_N]
            link(V.tensor_tensor(g, g, routed, ALU.mult))
            link(V.tensor_reduce(gsum, g, AX.X, ALU.add))
            link(V.reciprocal(gsum, gsum))
            link(V.tensor_tensor(g, g, bcast(gsum.unsqueeze(2), E_N), ALU.mult))
            V.tensor_copy(gate[:, :, E_N:E_N + 1], gate[:, :, 0:1]).then_inc(S.gates_ready, 1)
            dve.wait_ge(S.ranks_ready, 1)
            for q in range(1, PASSES):
                V.tensor_scalar(wanted[:, (q - 1) * E_N:q * E_N], bank[5][:, 64:96], float(SLOTS * q), None, ALU.is_gt)
            V.memset(pos[:, :, PASSES * E_N:PASSES * E_N + 2], -1.0)
            link(V.scalar_tensor_tensor(out=pos[:, :, 0:E_N], in0=bank[5][:, 0:64].rearrange("p (a e) -> p a e", a=TT),
                                        scalar=1.0, in1=routed, op0=ALU.add, op1=ALU.mult))
            link(V.tensor_tensor_scan(rank_of, ones[:, 0:LATER], wanted, 0.0, ALU.mult, ALU.add))
            link(V.scalar_tensor_tensor(out=chosen, in0=rank_of, scalar=const("job_rank"), in1=wanted,
                                        op0=ALU.is_equal, op1=ALU.mult))
            V.tensor_reduce(job_cols[:, 2:3], chosen, AX.X, ALU.add)
            V.tensor_tensor_reduce(wanted, chosen, const("job_place"), 1.0, 0.0, ALU.mult, ALU.add, job_cols[:, 0:1])
            link(V.tensor_tensor_reduce(rank_of, chosen, const("job_expert"), 1.0, 0.0, ALU.mult, ALU.add,
                                        job_cols[:, 1:2]))
            V.tensor_scalar(job_cols[:, 0:1], job_cols[:, 0:1], float(LATER + E_N), None, ALU.add).then_inc(S.jobs_listed, 1)
            link(V.tensor_scalar(pos[:, :, 0:E_N], pos[:, :, 0:E_N], -1.0, None, ALU.add))
            for q in range(1, PASSES):
                ins = V.tensor_scalar(pos[:, :, q * E_N:(q + 1) * E_N], pos[:, :, 0:E_N], float(-SLOTS * q), None, ALU.add)
            link(ins)
            dve.wait_ge(S.jobs_turned, 1)
            link(V.tensor_reduce(job_cols[0:1, 3:4], bank[5][0:1, 2 * P:3 * P:2], AX.X, ALU.add))
            V.tensor_copy(jobs[:, 0:2 * P], bank[5][0:1, 0:2 * P])
            V.tensor_copy(jobs[:, 2 * P:2 * P + 1], job_cols[0:1, 3:4]).then_inc(S.count_ready, 1)
            dve.wait_ge(S.gates_turned, 1)
            V.tensor_copy(gates_T, bank[6][0:E_N, 0:T]).then_inc(S.gates_saved, 1)

            def pick_tokens(M, r, place, column):
                for a in range(TT):
                    V.tensor_scalar(pick[r][:, a, :], slot_id[:, 0:SLOTS], pos[:, a, bass.ds(place, 1)], None, ALU.is_equal)
                for a in range(TT):
                    ins = V.tensor_scalar(pick_g[r][:, a, :], slot_id, pos[:, a, bass.ds(place, 1)],
                                          gate[:, a, bass.ds(column, 1)], ALU.is_equal, ALU.mult)
                ins.then_inc(M.masks_built, 1)

            def experts(M, pairs, before, chain, place_of, expert_of):
                V.memset(y_sb, 0.0)
                V.memset(st_sb[1], 0.0)
                V.memset(spare[:, 3:4], 0.0).then_inc(M.hidden_read, 1)
                pick_tokens(M, 0, place_of(0), expert_of(0))
                with dve.Fori(0, pairs) as i:
                    start = chain.n
                    chain.turn = i * 2
                    for r in range(2):
                        e = i * 2 + r
                        pick_tokens(M, 1 - r, place_of(i * 2 + (r + 1)), expert_of(i * 2 + (r + 1)))
                        dve.wait_ge(M.hidden, e + 1)
                        both = psum[:, 4 * 512:6 * 512].rearrange("p (f g) -> p f g", g=2)
                        V.tensor_scalar(glu, both[:, :, 0], LIMIT, None, ALU.min).then_inc(M.glu_ready, 1)
                        V.tensor_scalar(lin, both[:, :, 1], LIMIT, -LIMIT, ALU.min, ALU.max).then_inc(M.hidden_read, 1)
                        dve.wait_ge(M.glu_ready, e + 1)
                        dve.wait_ge(M.hidden_read, e + 2)
                        chain.link(V.scalar_tensor_tensor(out=lin, in0=lin, scalar=1.0, in1=glu, op0=ALU.add,
                                                          op1=ALU.mult))
                        dve.wait_ge(M.sig_ready, e + 1)
                        V.tensor_tensor(act_rows, lin, sig, ALU.mult).then_inc(M.act_ready, 1)
                    assert chain.n - start == 2
                chain.turn = None
                chain.n += 2 * (E_N // 2 - 1)

            experts(S, E_N // 2, C_MOE, main_chain, lambda n: n, lambda n: n)
            dve.wait_ge(S.count_ready, 1)
            pairs = dve.value_load(jobs[0:1, 2 * P:2 * P + 1], min_val=0, max_val=8)
            with dve.If(pairs > 0):
                dve.wait_ge(S.pass_over, 1)
                experts(again, pairs, RING, Chain(dve, S.again_step),
                        lambda n: dve.value_load(jobs[0:1, bass.ds(n, 1)], min_val=0, max_val=PASSES * E_N),
                        lambda n: dve.value_load(jobs[0:1, bass.ds(n + P, 1)], min_val=0, max_val=E_N - 1))
                dve.wait_ge(again.pass_over, 1)
            dve.wait_ge(S.f_saved, 1)
            norm(3, hT)
            onto_x(8)
            norm(4, xT)
            gained(88)

            dve.wait_ge(S.late_loaded, 16)
            dve.wait_ge(S.proj_saved, 20)
            cos, sin = late_const("cos"), late_const("sin")
            V.tensor_tensor(rot_qk, raw_qk, bcast(cos, KT), ALU.mult)
            dve.wait_ge(S.proj_saved, 27)
            dve.wait_ge(S.chunk_done, C_EOUT)
            for i in range(2):
                tok = cmp_in[:, i, :].rearrange("p (n j) -> p n j", j=CMP_STRIDE)
                for half in range(2):
                    js = slice(CMP_STRIDE * half, CMP_STRIDE * (half + 1))
                    ins = V.tensor_tensor(cmp_x[i][:, :, js], tok[:, half:half + N_CMP, :], bcast(pos_cols[:, i, js], N_CMP),
                                          ALU.add)
                ins.then_inc(S.cmp_x, 1)
            dve.wait_ge(S.swapped, 1)
            link(V.tensor_tensor(tiles(sq[:, :]), psum[:, 0:2048].rearrange("p (k t) -> p k t", t=T), bcast(sin, KT), ALU.mult))
            V.tensor_tensor(rot_qk, rot_qk, tiles(sq[:, :]), ALU.add).then_inc(S.rot_ready, 1)
            dve.wait_ge(S.ret_scores, 1)
            V.tensor_tensor(weighted, psum[:, 0:2048].rearrange("p (h n) -> p h n", n=512)[:, :, 0:384],
                            late_const("decay").rearrange("p (h n) -> p h n", h=RET_HEADS), ALU.mult).then_inc(S.ret_weighted, 1)
            dve.wait_ge(S.cmp_scores, 1)
            for par in range(2):
                ins = V.scalar_tensor_tensor(
                    out=cmp_p[:, 8 * par:8 * par + 8, :].rearrange("p n c -> p (n c)").rearrange("p (i m) -> p i m", i=4),
                    in0=bank[4 + par][:, 0:120].rearrange("p (i m) -> p i m", i=4), scalar=ATT_SCALE,
                    in1=bcast(late_const("cmp_add"), 4), op0=ALU.mult, op1=ALU.add)
            link(ins)
            link(V.tensor_reduce(cmp_max, cmp_p, AX.X, ALU.max))
            V.tensor_tensor(cmp_p, cmp_p, bcast(cmp_max.unsqueeze(2), N_CMP), ALU.subtract).then_inc(S.cmp_shift, 1)
            dve.wait_ge(S.ret_sum, 1)
            V.scalar_tensor_tensor(out=centred, in0=psum[:, 1024:2048], scalar=-1.0 / P, in1=mixT[:, 0:1024],
                                   op0=ALU.mult, op1=ALU.add).then_inc(S.ret_centred, 1)
            dve.wait_ge(S.cmp_exp, 1)
            pairs = cmp_p.rearrange("p n c -> p (n c)").rearrange("p (i m) -> p i m", i=8)
            link(V.tensor_tensor(pairs, pairs, bcast(late_const("cmp_keep"), 8), ALU.mult))
            link(V.tensor_reduce(cmp_sum, cmp_p, AX.X, ALU.add))
            link(V.tensor_scalar(cmp_sum, cmp_sum, 1e-30, None, ALU.max))
            link(V.reciprocal(cmp_sum, cmp_sum))
            for par in range(2):
                c8 = cmp_sum[:, 8 * par:8 * par + 8].rearrange("p (i a) -> p i a", a=TT)
                ins = V.tensor_tensor(c8, c8, nsa_gate[:, :, par:8:2].rearrange("p a i -> p i a"), ALU.mult)
            link(ins)
            V.tensor_tensor(cmp_p, cmp_p, bcast(cmp_sum.unsqueeze(2), N_CMP), ALU.mult).then_inc(S.cmp_probs, 1)
            dve.wait_ge(S.ret_root, 1)
            link(V.reciprocal(sq[:, 1024:2048], sq[:, 1024:2048]))
            dve.wait_ge(S.ret_centred, 1)
            link(V.tensor_tensor(centred, centred, sq[:, 1024:2048], ALU.mult))
            V.tensor_tensor(tiles(mixT[:, 0:1024]), tiles(centred), ret_g, ALU.mult).then_inc(S.mix_ready, 1)
            for u in range(9):
                if u < 8:
                    dve.wait_ge(S.nsa_scores, u + 1)
                    if u >= 2:
                        dve.wait_ge(S.nsa_turned, u - 1)
                    s = nsa_s[u % 2]
                    link(V.scalar_tensor_tensor(
                        out=s, in0=psum[:, 1024 * (u % 2):1024 * (u % 2) + 1024].rearrange("p (h n) -> p h n", h=2)[:, :, 0:384],
                        scalar=ATT_SCALE, in1=bcast(late_const("causal"), 2), op0=ALU.mult, op1=ALU.add))
                    some = nsa_negmax[:, 4 * u:4 * u + 4]
                    for a, (lo, hi) in enumerate(((0, P), (P, 384))):
                        ins = V.tensor_reduce(some[:, a:4:2], s[:, :, lo:hi], AX.X, ALU.max)
                    link(ins)
                    V.tensor_scalar(some, some, -1.0, None, ALU.mult).then_inc(S.nsa_max, 1)
                if u >= 1:
                    v = u - 1
                    i, br = v // 2, 1 + v % 2
                    dve.wait_ge(S.nsa_probs, 4 * (v + 1))
                    r = nsa_sum[:, 4 * v:4 * v + 4]
                    link(V.reciprocal(r, r))
                    r2 = r.rearrange("p (h a) -> p h a", h=2)
                    at = 8 * br + 2 * i
                    link(V.tensor_tensor(r2, r2, nsa_gate[:, :, at:at + 2].rearrange("p a h -> p h a"), ALU.mult))
                    for a, (lo, hi) in enumerate(((0, P), (P, 384))):
                        piece = nsa_s[v % 2][:, :, lo:hi]
                        ins = V.tensor_tensor(piece, piece, bcast(r2[:, :, a:a + 1], hi - lo), ALU.mult)
                    ins.then_inc(S.nsa_weighted, 1)

            def add_projection(first, j0):
                for j in range(4):
                    dve.wait_ge(S.chunk_done, first + j + 1)
                    part = xT[:, 512 * j:512 * j + 512]
                    V.tensor_tensor(part, part, bank[(j0 + j) % 2], ALU.add).then_inc(S.proj_saved, 1)

            def ffn(first, layer):
                for i in range(FFN_STEPS):
                    w3_at = first + (3 * i if i else 1)
                    dve.wait_ge(S.chunk_done, w3_at + 1)
                    dve.wait_ge(S.ffn_silu, layer * FFN_STEPS + i + 1)
                    V.tensor_tensor(ffn_h[i % 2], ffn_s[i % 2].rearrange("p (k t) -> p k t", k=2),
                                    bank[5 + 2 * (i % 2)].rearrange("p (k t) -> p k t", k=2), ALU.mult) \
                     .then_inc(S.ffn_hidden, 1)
                dve.wait_ge(S.chunk_done, first + 3 * FFN_STEPS)
                V.tensor_tensor(xT[:, :], xT[:, :], psum[:, 0:2048], ALU.add).then_inc(S.x_ready, 1)

            add_projection(C_EOUT, 30)
            norm(5, xT)
            gained(104)
            ffn(C_FFN0, 0)
            norm(6, xT)
            gained(96)

            dve.wait_ge(S.proj_saved, 50)
            for hh in range(2):
                V.memset(hg_near[:, 8 * hh:8 * hh + 8, :], 0.0).then_inc(S.hg_level, 1)
            link(V.memset(hg_pk, 1.0))

            def place(step):
                dve.wait_ge(S.hg_scores, step + 1)
                if step >= 2:
                    dve.wait_ge(S.hg_placed, step - 1)
                lv, hh = step // 2 - 1, step % 2
                mask = late_const("levels")[:, (lv % (LEVELS + 1)) * P:(lv % (LEVELS + 1) + 1) * P]
                at = 1024 * (step % 4)
                V.copy_predicated(hg_near[:, 8 * hh:8 * hh + 8, :], bcast(mask.bitcast(U32), 8),
                                  psum[:, at:at + 1024].rearrange("p (n c) -> p n c", c=P)).then_inc(S.hg_placed, 1)

            for lv in range(LEVELS):
                half = 2 ** lv
                for hh in range(2):
                    def cut(t):
                        flat = t[:, 4 * hh:4 * hh + 4, :].rearrange("p k t -> p (k t)")
                        return flat.rearrange("p (b g s) -> p b g s", g=2, s=half)

                    q, k, f, pk, qd, kd = (cut(t) for t in (hg_q, hg_k, hg_f, hg_pk, hg_qd, hg_kd))
                    n = 512 // half
                    if lv == 0:
                        V.tensor_copy(hg_kd[:, 4 * hh:4 * hh + 4, :], hg_k[:, 4 * hh:4 * hh + 4, :])
                        V.tensor_tensor(hg_qd[:, 4 * hh:4 * hh + 4, :], hg_q[:, 4 * hh:4 * hh + 4, :],
                                        hg_f[:, 4 * hh:4 * hh + 4, :], ALU.mult).then_inc(S.hg_level, 1)
                    else:
                        dve.wait_ge(S.hg_scores, 2 * lv + hh + 1)
                        V.tensor_tensor(kd[:, :, 0, :], k[:, :, 0, :], pk[:, :, 0, :], ALU.mult)
                        V.tensor_tensor(qd[:, :, 1, :], q[:, :, 1, :], f[:, :, 1, :], ALU.mult).then_inc(S.hg_level, 1)
                    dve.wait_ge(S.hg_level, 2 * lv + hh + 3)
                    link(V.tensor_tensor(pk[:, :, 0, :], pk[:, :, 0, :], f[:, :, 1, half - 1:half].broadcast_to([P, n, half]),
                                         ALU.mult))
                    link(V.tensor_tensor(f[:, :, 1, :], f[:, :, 1, :], f[:, :, 0, half - 1:half].broadcast_to([P, n, half]),
                                         ALU.mult))
                    place(2 * lv + hh)
            for hh in range(2):
                place(2 * LEVELS + hh)
            V.tensor_tensor(hg_kd[:, :, 0:P], hg_k[:, :, 0:P], hg_pk[:, :, 0:P], ALU.mult)
            V.tensor_tensor(hg_qd[:, :, P:T], hg_q[:, :, P:T], hg_f[:, :, P:T], ALU.mult).then_inc(S.hg_level, 1)
            dve.wait_ge(S.hg_scores, 2 * (LEVELS + 1) + 1)
            V.tensor_copy(hg_cross, psum[:, 0:1024].rearrange("p (n c) -> p n c", c=P)).then_inc(S.hg_placed, 1)
            dve.wait_ge(S.hg_root, 1)
            link(V.reciprocal(hT[:, :], hT[:, :]))
            link(V.tensor_tensor(hg_o, hg_o, tiles(hT[:, :]), ALU.mult))
            V.scalar_tensor_tensor(out=tiles(mixT[:, :]), in0=hg_o, scalar=cols_b[:, 1:2], in1=hg_g, op0=ALU.mult,
                                   op1=ALU.mult).then_inc(S.mix_ready, 1)
            add_projection(C_OOUT, 50)
            norm(7, xT)
            gained(112)
            ffn(C_FFN1, 1)
            norm(8, xT)
            gained(120)


_NAMES = """x c w_ada b_ada g_pre_mix g_post_mix w_in w_out lam_q1 lam_k1 lam_q2 lam_k2 g_subln nat_rpb
g_pre_ffn g_post_ffn w_router b_router w1 b1 w2 b2 norm_mix_g_2 norm_ffn_g_2 final_norm_g_2 even_w_in_2
even_w_out_2 cmp_pos_k_2 cmp_w1_k_2 cmp_w2_k_2 cmp_pos_v_2 cmp_w1_v_2 cmp_w2_v_2 odd_w_in_2 odd_w_out_2
hgrn_norm_g_2 hgrn_lb_logits_2 ffn_w1_2 ffn_w3_2 ffn_w2_2""".split()


def kernel(**inputs):
    import concourse.bacc as _bacc
    from concourse.bass_utils import run_bass_kernel_spmd as _run

    nc = _bacc.Bacc("TRN2", target_bir_lowering=False, num_devices=1)
    arrays, args = {}, []
    early, late = shape_constants()
    given = [(n, np.ascontiguousarray(inputs[n])) for n in _NAMES] + [("early", early), ("late", late)]
    for name, a in given:
        arrays[f"in_{name}_dram"] = a
        args.append(nc.dram_tensor(f"in_{name}_dram", a.shape, mybir.dt.from_np(a.dtype), kind="ExternalInput").ap())
    args.append(nc.dram_tensor("out_0_dram", (1, T, D), F32, kind="ExternalOutput").ap())
    two_layer_program(nc, *args)
    r = _run(nc, [arrays], core_ids=[0])
    return r.results[0]["out_0_dram"]
```
